# Optimizing a Trainium2 kernel written in Bass

```python
import jax, jax.numpy as jnp
from jax import lax
import numpy as np

D_MODEL = 1024
BATCH = 1
SEQ = 256
DEPTH = 2
DEC_BATCH = 8
DEC_SEQ = 8
PAST_LEN = 2048
PAGE_SIZE = 128

HEAD_DIM = 64
ROT_DIM = HEAD_DIM // 4
ROPE_THETA = 500000.0
DIL_PAIRS = ((128, 1), (512, 4), (2048, 16))
N_GROUPS_A = 3
HEADS_PER_GROUP_A = 4
A_OUT = HEADS_PER_GROUP_A * HEAD_DIM
N_HEADS_B = 8
N_KV_B = 2
GQA_B = N_HEADS_B // N_KV_B
WINDOW_B = 128
B_Q = N_HEADS_B * HEAD_DIM
B_KV = N_KV_B * HEAD_DIM
IN_COLS = N_GROUPS_A * 3 * A_OUT + B_Q + 2 * B_KV + 2 * D_MODEL
D_FF = ((8 * D_MODEL // 3 + 127) // 128) * 128
BLK = 128
NORM_EPS = 1e-6
NEG = -1e30
SCALE = HEAD_DIM ** -0.5

kernel_name = "hybrid_dilated_sinkgqa_macaron_decode_step"

def _rms(x, g):
    xf = x.astype(jnp.float32)
    y = xf * lax.rsqrt(jnp.mean(xf * xf, axis=-1, keepdims=True) + NORM_EPS)
    return (y * g.astype(jnp.float32)).astype(x.dtype)

def _swiglu(h, wg, wu, wd):
    return (jax.nn.silu(h @ wg) * (h @ wu)) @ wd

def _rope(x, pos):
    half = ROT_DIM // 2
    inv = ROPE_THETA ** (-(jnp.arange(half, dtype=jnp.float32) * 2.0 / ROT_DIM))
    ang = pos.astype(jnp.float32)[:, None] * inv[None, :]
    cos = jnp.cos(ang)[:, None, :]
    sin = jnp.sin(ang)[:, None, :]
    xr = x[..., :ROT_DIM].astype(jnp.float32)
    x1, x2 = xr[..., :half], xr[..., half:]
    rot = jnp.concatenate([x1 * cos - x2 * sin, x2 * cos + x1 * sin], axis=-1).astype(x.dtype)
    return jnp.concatenate([rot, x[..., ROT_DIM:]], axis=-1)

def _softmax_stats(s, valid):
    s = jnp.where(valid, s, NEG)
    m = jnp.max(s, axis=-1, keepdims=True)
    e = jnp.exp(s - m)
    den = jnp.sum(e, axis=-1, keepdims=True)
    return e / den, (m + jnp.log(den))[..., 0]

def _band_attn(q, k, v, n_back):
    N, L, Hk, G, Dh = q.shape
    nb = -(-L // BLK)
    Lp = nb * BLK
    pad = Lp - L
    qb = jnp.pad(q, ((0, 0), (0, pad), (0, 0), (0, 0), (0, 0))).reshape(N, nb, BLK, Hk, G, Dh)
    kp = jnp.pad(k, ((0, 0), (BLK, pad), (0, 0), (0, 0))).reshape(N, nb + 1, BLK, Hk, Dh)
    vp = jnp.pad(v, ((0, 0), (BLK, pad), (0, 0), (0, 0))).reshape(N, nb + 1, BLK, Hk, Dh)
    kw = jnp.concatenate([kp[:, :-1], kp[:, 1:]], axis=2)
    vw = jnp.concatenate([vp[:, :-1], vp[:, 1:]], axis=2)
    s = jnp.einsum('nbqhgd,nbkhd->nbhgqk', qb, kw, preferred_element_type=jnp.float32)
    b = jnp.arange(nb)[:, None, None]
    r = jnp.arange(BLK)[None, :, None]
    c = jnp.arange(2 * BLK)[None, None, :]
    dist = BLK + r - c
    valid = (dist >= 0) & (dist <= n_back) & ((b - 1) * BLK + c >= 0)
    p, lse = _softmax_stats(s, valid[None, :, None, None])
    o = jnp.einsum('nbhgqk,nbkhd->nbqhgd', p.astype(v.dtype), vw,
                   preferred_element_type=jnp.float32).astype(v.dtype)
    o = o.reshape(N, Lp, Hk, G, Dh)[:, :L]
    lse = lse.transpose(0, 1, 4, 2, 3).reshape(N, Lp, Hk, G)[:, :L]
    return o, lse

def _dilated_prompt(q, k, v, window, dil):
    N, L, H, Dh = q.shape
    Ls = L // dil

    def strided(x):
        return x.reshape(N, Ls, dil, H, Dh).transpose(0, 2, 1, 3, 4).reshape(N * dil, Ls, H, Dh)

    o, lse = _band_attn(strided(q)[:, :, :, None], strided(k), strided(v), window // dil)
    o = o[:, :, :, 0].reshape(N, dil, Ls, H, Dh).transpose(0, 2, 1, 3, 4).reshape(N, L, H, Dh)
    lse = lse[..., 0].reshape(N, dil, Ls, H).transpose(0, 2, 1, 3).reshape(N, L, H)
    return o, lse

def _dilated_sample(q, k_new, v_new, buf, window, dil):
    N, T, H, Dh = q.shape
    Lb = buf.shape[1]
    kc = jnp.concatenate([buf[:, :, 0], k_new], axis=1)
    vc = jnp.concatenate([buf[:, :, 1], v_new], axis=1)
    idx = Lb + jnp.arange(T)[:, None] - dil * jnp.arange(window // dil + 1)[None, :]
    valid = idx >= 0
    idxc = jnp.maximum(idx, 0)
    kg = kc[:, idxc]
    vg = vc[:, idxc]
    s = jnp.einsum('nthd,ntjhd->nhtj', q, kg, preferred_element_type=jnp.float32)
    p, lse = _softmax_stats(s, valid[None, None])
    o = jnp.einsum('nhtj,ntjhd->nthd', p.astype(vg.dtype), vg,
                   preferred_element_type=jnp.float32).astype(vg.dtype)
    keep = min(window, Lb + T)
    new_buf = jnp.concatenate([buf, jnp.stack([k_new, v_new], axis=2)], axis=1)[:, Lb + T - keep:]
    return o, lse.transpose(0, 2, 1), new_buf

def _window_sample(q, k_new, v_new, buf):
    T = q.shape[1]
    Lb = buf.shape[1]
    kc = jnp.concatenate([buf[:, :, 0], k_new], axis=1)
    vc = jnp.concatenate([buf[:, :, 1], v_new], axis=1)
    s = jnp.einsum('nthgd,nkhd->nhgtk', q, kc, preferred_element_type=jnp.float32)
    dist = Lb + jnp.arange(T)[:, None] - jnp.arange(Lb + T)[None, :]
    valid = (dist >= 0) & (dist < WINDOW_B)
    p, lse = _softmax_stats(s, valid[None, None, None])
    o = jnp.einsum('nhgtk,nkhd->nthgd', p.astype(vc.dtype), vc,
                   preferred_element_type=jnp.float32).astype(vc.dtype)
    keep = min(WINDOW_B, Lb + T)
    new_buf = jnp.concatenate([buf, jnp.stack([k_new, v_new], axis=2)], axis=1)[:, Lb + T - keep:]
    return o, lse.transpose(0, 3, 1, 2), new_buf

def _mixer_inputs(h, w_in, pos):
    N, L, _ = h.shape
    sizes = [A_OUT] * (3 * N_GROUPS_A) + [B_Q, B_KV, B_KV, D_MODEL, D_MODEL]
    cuts = [int(c) for c in np.cumsum(sizes)[:-1]]
    parts = jnp.split(h @ w_in, cuts, axis=-1)
    groups = []
    for g in range(N_GROUPS_A):
        q, k, v = (p.reshape(N, L, HEADS_PER_GROUP_A, HEAD_DIM) for p in parts[3 * g:3 * g + 3])
        groups.append((_rope(q, pos) * SCALE, _rope(k, pos), v))
    bq, bk, bv, ga, gb = parts[3 * N_GROUPS_A:]
    bq = (_rope(bq.reshape(N, L, N_HEADS_B, HEAD_DIM), pos) * SCALE).reshape(N, L, N_KV_B, GQA_B, HEAD_DIM)
    bk = _rope(bk.reshape(N, L, N_KV_B, HEAD_DIM), pos)
    bv = bv.reshape(N, L, N_KV_B, HEAD_DIM)
    return groups, bq, bk, bv, ga, gb

def _mixer_output(oa_list, la_list, ob, lb, ga, gb, sinks, w_ba, w_bb, w_out):
    N, L = ga.shape[:2]
    wts = jax.nn.softmax(jnp.stack(la_list, axis=0), axis=0)
    oa = jnp.sum(wts[..., None] * jnp.stack(oa_list, axis=0).astype(jnp.float32), axis=0)
    oa = oa.astype(ga.dtype).reshape(N, L, A_OUT)
    sink_scale = jax.nn.sigmoid(lb - sinks.reshape(N_KV_B, GQA_B).astype(jnp.float32))
    ob = (ob.astype(jnp.float32) * sink_scale[..., None]).astype(ga.dtype).reshape(N, L, B_Q)
    merged = jax.nn.sigmoid(ga) * (oa @ w_ba) + jax.nn.sigmoid(gb) * (ob @ w_bb)
    return merged @ w_out

def _mixer_prompt(h, w_in, sinks, w_ba, w_bb, w_out):
    L = h.shape[1]
    pos = jnp.arange(L)
    groups, bq, bk, bv, ga, gb = _mixer_inputs(h, w_in, pos)
    oa, la, bufs = [], [], []
    for (q, k, v), (window, dil) in zip(groups, DIL_PAIRS):
        o, lse = _dilated_prompt(q, k, v, window, dil)
        oa.append(o)
        la.append(lse)
        keep = min(window, L)
        bufs.append(jnp.stack([k[:, L - keep:], v[:, L - keep:]], axis=2))
    ob, lb = _band_attn(bq, bk, bv, WINDOW_B - 1)
    keep = min(WINDOW_B, L)
    bufs.append(jnp.stack([bk[:, L - keep:], bv[:, L - keep:]], axis=2))
    return _mixer_output(oa, la, ob, lb, ga, gb, sinks, w_ba, w_bb, w_out), bufs

def _mixer_sample(h, bufs_a, buf_b, w_in, sinks, w_ba, w_bb, w_out):
    T = h.shape[1]
    pos = PAST_LEN + jnp.arange(T)
    groups, bq, bk, bv, ga, gb = _mixer_inputs(h, w_in, pos)
    oa, la, new_bufs = [], [], []
    for (q, k, v), buf, (window, dil) in zip(groups, bufs_a, DIL_PAIRS):
        o, lse, nb = _dilated_sample(q, k, v, buf, window, dil)
        oa.append(o)
        la.append(lse)
        new_bufs.append(nb)
    ob, lb, nbb = _window_sample(bq, bk, bv, buf_b)
    new_bufs.append(nbb)
    return _mixer_output(oa, la, ob, lb, ga, gb, sinks, w_ba, w_bb, w_out), new_bufs

def setup_inputs(seed: int = 0) -> dict:
    key = jax.random.key(seed)
    ks = iter(jax.random.split(key, 24))
    f32 = jnp.float32

    def nrm(shape, scale):
        return jax.random.normal(next(ks), shape, f32) * scale

    def gain(shape):
        return 1.0 + 0.05 * jax.random.normal(next(ks), shape, f32)

    inp = {}
    inp["x_prompt"] = nrm((BATCH, SEQ, D_MODEL), 1.0)
    inp["x_sample"] = nrm((DEC_BATCH, DEC_SEQ, D_MODEL), 1.0)
    inp["cache_a1"] = nrm((DEPTH, DEC_BATCH, min(DIL_PAIRS[0][0], PAST_LEN), 2, HEADS_PER_GROUP_A, HEAD_DIM), 1.0)
    inp["cache_a2"] = nrm((DEPTH, DEC_BATCH, min(DIL_PAIRS[1][0], PAST_LEN), 2, HEADS_PER_GROUP_A, HEAD_DIM), 1.0)
    inp["cache_a3"] = nrm((DEPTH, DEC_BATCH, min(DIL_PAIRS[2][0], PAST_LEN), 2, HEADS_PER_GROUP_A, HEAD_DIM), 1.0)
    inp["cache_b"] = nrm((DEPTH, DEC_BATCH, min(WINDOW_B, PAST_LEN), 2, N_KV_B, HEAD_DIM), 1.0)
    inp["norm_ffn1"] = gain((DEPTH, D_MODEL))
    inp["ffn1_gate"] = nrm((DEPTH, D_MODEL, D_FF), D_MODEL ** -0.5)
    inp["ffn1_up"] = nrm((DEPTH, D_MODEL, D_FF), D_MODEL ** -0.5)
    inp["ffn1_down"] = nrm((DEPTH, D_FF, D_MODEL), D_FF ** -0.5)
    inp["norm_mix"] = gain((DEPTH, D_MODEL))
    inp["w_in"] = nrm((DEPTH, D_MODEL, IN_COLS), D_MODEL ** -0.5)
    inp["sinks"] = nrm((DEPTH, N_HEADS_B), 0.5)
    inp["w_branch_a"] = nrm((DEPTH, A_OUT, D_MODEL), A_OUT ** -0.5)
    inp["w_branch_b"] = nrm((DEPTH, B_Q, D_MODEL), B_Q ** -0.5)
    inp["w_out"] = nrm((DEPTH, D_MODEL, D_MODEL), D_MODEL ** -0.5)
    inp["norm_ffn2"] = gain((DEPTH, D_MODEL))
    inp["ffn2_gate"] = nrm((DEPTH, D_MODEL, D_FF), D_MODEL ** -0.5)
    inp["ffn2_up"] = nrm((DEPTH, D_MODEL, D_FF), D_MODEL ** -0.5)
    inp["ffn2_down"] = nrm((DEPTH, D_FF, D_MODEL), D_FF ** -0.5)
    inp["norm_final"] = gain((D_MODEL,))
    return inp

def reference(x_prompt, x_sample, cache_a1, cache_a2, cache_a3, cache_b,
              norm_ffn1, ffn1_gate, ffn1_up, ffn1_down,
              norm_mix, w_in, sinks, w_branch_a, w_branch_b, w_out,
              norm_ffn2, ffn2_gate, ffn2_up, ffn2_down, norm_final):
    xp, xs = x_prompt, x_sample
    pa1, pa2, pa3, pb = [], [], [], []
    sa1, sa2, sa3, sb = [], [], [], []
    for l in range(DEPTH):
        f1 = (ffn1_gate[l], ffn1_up[l], ffn1_down[l])
        f2 = (ffn2_gate[l], ffn2_up[l], ffn2_down[l])
        mw = (w_in[l], sinks[l], w_branch_a[l], w_branch_b[l], w_out[l])
        xp = xp + 0.5 * _swiglu(_rms(xp, norm_ffn1[l]), *f1)
        xs = xs + 0.5 * _swiglu(_rms(xs, norm_ffn1[l]), *f1)
        yp, bp = _mixer_prompt(_rms(xp, norm_mix[l]), *mw)
        ys, bs = _mixer_sample(_rms(xs, norm_mix[l]), (cache_a1[l], cache_a2[l], cache_a3[l]), cache_b[l], *mw)
        xp = xp + yp
        xs = xs + ys
        xp = xp + 0.5 * _swiglu(_rms(xp, norm_ffn2[l]), *f2)
        xs = xs + 0.5 * _swiglu(_rms(xs, norm_ffn2[l]), *f2)
        pa1.append(bp[0]); pa2.append(bp[1]); pa3.append(bp[2]); pb.append(bp[3])
        sa1.append(bs[0]); sa2.append(bs[1]); sa3.append(bs[2]); sb.append(bs[3])
    y_prompt = _rms(xp, norm_final)
    y_sample = _rms(xs, norm_final)
    return (y_prompt, y_sample,
            jnp.stack(pa1), jnp.stack(pa2), jnp.stack(pa3), jnp.stack(pb),
            jnp.stack(sa1), jnp.stack(sa2), jnp.stack(sa3), jnp.stack(sb))


_drawn_inputs = setup_inputs


def setup_inputs(seed=0):
    import zlib

    import numpy as np

    out = dict(_drawn_inputs(seed))
    spreads = {}
    factors = {'sinks': 8.0}
    for name, (base, spread) in spreads.items():
        noise = np.random.default_rng([zlib.crc32(name.encode()), seed]).standard_normal(out[name].shape)
        drawn = base * np.exp(spread * noise) if base else spread * noise
        out[name] = __import__('jax').numpy.asarray(drawn.astype(out[name].dtype))
    for name, factor in factors.items():
        out[name] = (out[name] * factor).astype(out[name].dtype)
    return out
```

```python
from contextlib import ExitStack

import numpy as np

import concourse.bass as bass
from concourse import mybir

F32 = mybir.dt.float32
F32R = mybir.dt.float32r
ALU = mybir.AluOpType
ACT = mybir.ActivationFunctionType

P = 128
DEPTH = 2
D = 1024
SEQ = 256
NB, NT = 8, 8
TOK = SEQ + NB * NT
HD = 64
KD = D // P
F = ((8 * D // 3 + 127) // 128) * 128
KF = F // P
DILS = ((128, 1), (512, 4), (2048, 16))
NG = len(DILS)
SCALE = HD ** -0.5
EPS = 1e-6
NEG = -1e30
HALF = 32
CT = 13
WIN = 128

UT = 8
RAW = 2
RING = 4
DN_TILES = (6, 5, 6, 5)
DN_K0 = (0, 6, 11, 17)
BR_TILES = 6
N_IN = 40
U_GU = (0, 132)
U_DN = (44, 176)
U_IN, U_BR, U_WO = 76, 116, 124
NU = 208
R_GU, R_DN = (0, 68), (44, 112)
R_BR, R_WO = 52, 60
NR = 120

COLS = [("k", 3, 0), ("v", 3, 0)] + [("q", 3, c) for c in range(4)]
for _g in range(NG):
    COLS += [(_k, _g, _c) for _k in "qkv" for _c in range(2)]
COLS += [(_k, 0, _m) for _m in range(KD) for _k in ("ga", "gb")]
assert len(COLS) == N_IN
KV_UNITS = [u for u, c in enumerate(COLS) if c[0] in "kv"]
K_UNITS = [u for u in KV_UNITS if COLS[u][0] == "k"]
QK_UNITS = [u for u, c in enumerate(COLS) if c[0] in "qk"]
AQ_UNITS = [u for u in QK_UNITS if COLS[u][0] == "q" and COLS[u][1] < NG]
G_UNITS = [u for u, c in enumerate(COLS) if c[0] in ("ga", "gb")]


def qk_slot(kind, g, c):
    if g == 3:
        return 0 if kind == "k" else 1 + c
    return (5 if kind == "q" else 11) + 2 * g + c


def v_slot(g, c):
    return 6 if g == 3 else 2 * g + c


ITEMS = [("B", c, t) for c in range(4) for t in range(2)] + [("SB", h, 0) for h in range(2)]
ITEMS += [("A", h, t) for h in range(4) for t in range(2)] + [("SA", h, 0) for h in range(2)]
NI = len(ITEMS)
NPV = NI - 2
N_KV = 32


def mixer_steps():
    steps, nxt = [], [0]

    def unit():
        u = nxt[0]
        nxt[0] += 1
        steps.append(("U", u))
        if u >= 1:
            if u - 1 in KV_UNITS:
                steps.append(("R", u - 1))
            if u - 1 in G_UNITS:
                steps.append(("G", u - 1))

    for _ in range(7):
        unit()
    for p in range(NI + 2):
        if p == 10:
            while nxt[0] < 25:
                unit()
        if p < NI:
            steps.append(("S", p))
        if 1 <= p <= NI:
            steps.append(("N", p - 1))
        if p < 10:
            unit()
            if p < 7:
                unit()
        elif p < NI + 1 and nxt[0] < N_IN:
            unit()
        if 10 <= p < 18:
            steps += [("K", 2 * (p - 10)), ("K", 2 * (p - 10) + 1)]
            if p == 13:
                steps.append(("E", 1))
            if p == 17:
                steps.append(("E", 2))
        if 1 <= p <= NI:
            steps.append(("T", p - 1))
        if p == 6:
            steps += [("KB", 0), ("E", 0)]
        if 2 <= p:
            i = p - 2
            steps.append(("O", i))
            if ITEMS[i][0] == "SA":
                h = ITEMS[i][1]
                for n in range(8):
                    steps.append(("V", 16 + 8 * h + n))
                    if n % 3 == 2 and nxt[0] < N_IN:
                        unit()
            steps.append(("W", i))
    while nxt[0] < N_IN:
        unit()
    steps.append(("G", N_IN - 1))
    return steps


STEPS = mixer_steps()


def cache_load_places():
    at, last = {}, 0
    for kind, n in STEPS:
        if kind == "U":
            last = n
        if kind in "KV" and kind != "KB":
            at[n] = last
    return [14, 15] + [min(at[n - 2] + 6, 55) for n in range(2, N_KV)]


KV_PLACE = cache_load_places()

C_COS, C_SIN = 0, TOK
C_MA = 2 * TOK
C_MB = C_MA + NG * SEQ
C_SA = C_MB + SEQ
N_SA = NG * (P + HALF)
C_SB = C_SA + N_SA
N_SB = P + HALF
C_ID = C_SB + N_SB
N_C = C_ID + P


def constants():
    c = np.zeros((P, N_C), np.float32)
    rot = HD // 4
    half = rot // 2
    inv = np.float32(500000.0) ** (-(np.arange(half, dtype=np.float32) * np.float32(2.0) / np.float32(rot)))
    pos = np.concatenate([np.arange(SEQ), np.tile(2048 + np.arange(NT), NB)]).astype(np.float32)
    ang = (inv[:, None] * pos[None, :]).astype(np.float32)
    c[:, C_COS:C_COS + TOK] = 1.0
    for base in (0, HD):
        for part, sign in ((0, -1.0), (half, 1.0)):
            c[base + part:base + part + half, C_COS:C_COS + TOK] = np.cos(ang)
            c[base + part:base + part + half, C_SIN:C_SIN + TOK] = sign * np.sin(ang)
    dist = (P + np.arange(P))[:, None] - np.arange(SEQ)[None, :]
    for g, (win, dil) in enumerate(DILS):
        ok = (dist >= 0) & (dist <= win) & (dist % dil == 0)
        c[:, C_MA + g * SEQ:C_MA + (g + 1) * SEQ] = np.where(ok, 0, NEG)
    c[:, C_MB:C_MB + SEQ] = np.where((dist >= 0) & (dist < WIN), 0, NEG)
    b, t = (np.arange(P) // NT % 4)[:, None], (np.arange(P) % NT)[:, None]
    r = np.arange(P)[None, :]
    nb, s = (np.arange(HALF) // NT)[None, :], (np.arange(HALF) % NT)[None, :]
    for g, (win, dil) in enumerate(DILS):
        row = r if g == 0 else t % dil + dil * r
        ok = (row >= t) & (row <= win + t)
        c[:, C_SA + g * P:C_SA + (g + 1) * P] = np.where(ok, 0, NEG)
        ok = (nb == b) & (s <= t) & ((t - s) % dil == 0)
        o = C_SA + NG * P + g * HALF
        c[:, o:o + HALF] = np.where(ok, 0, NEG)
    c[:, C_SB:C_SB + P] = np.where(r > t, 0, NEG)
    c[:, C_SB + P:C_SB + N_SB] = np.where((nb == b) & (s <= t), 0, NEG)
    c[:, C_ID:C_ID + P] = np.eye(P, dtype=np.float32)
    return c


BK_KV = 2
BK_S = 3
BK_T = 5
BK_O = 7
BK_DN = 4
BK_WO = 5
BK_BR = ((0, 1), (3, 4))


def build(nc, a):
    ctx = ExitStack()
    with ctx:
        def sb(name, shape, dt=F32, where=ctx):
            return where.enter_context(nc.sbuf_tensor(name, shape, dt))

        def sem(name):
            return ctx.enter_context(nc.semaphore(name))

        const = sb("const", [P, N_C])
        ones = sb("ones", [P, P])
        eps = sb("eps", [P, 1])
        gains = sb("gains", [P, 3 * DEPTH + 1, KD])
        sinks = sb("sinks", [P, DEPTH, 10])
        x = sb("x", [P, KD, TOK])
        xg = sb("xg", [P, 2, TOK])
        xhi = sb("xhi", [P, KD, TOK], F32R)
        xlo = sb("xlo", [P, KD, TOK], F32R)
        sq = sb("sq", [P, TOK])
        ssq = sb("ssq", [P, TOK])
        rms = sb("rms", [P, TOK])
        rinv = sb("rinv", [P, TOK])
        raw = sb("raw", [P, RAW, UT * P])
        whi = sb("whi", [P, RING, UT * P], F32R)
        wlo = sb("wlo", [P, RING, UT * P], F32R)

        with ExitStack() as ffn:
            act_hi = sb("act_hi", [P, KF, TOK], F32R, ffn)
            act_lo = sb("act_lo", [P, KF, TOK], F32R, ffn)
            gate_s = sb("gate_s", [P, 2, TOK], F32, ffn)
            up_s = sb("up_s", [P, 2, TOK], F32, ffn)
        gate = sb("gate", [P, 2 * KD, TOK])
        ohi = sb("ohi", [P, BR_TILES, TOK], F32R)
        olo = sb("olo", [P, BR_TILES, TOK], F32R)
        with ExitStack() as att:
            kvc = sb("kvc", [P, 2, CT * P], F32, att)
            kb = sb("kb", [P, NB, P], F32, att)
            vb = sb("vb", [P, NB, P], F32, att)
            qk = sb("qk", [P, 17, TOK], F32, att)
            vtok = sb("vtok", [P, 2, 7 * P], F32, att)
            vnew = sb("vnew", [HALF, 2, 7 * P], F32, att)
            kst = sb("kst", [P, 2, 4 * P], F32, att)
            qbd = sb("qbd", [P, NG, 2, 2, NB * NT], F32, att)
            e = sb("e", [P, 2, NG * SEQ], F32, att)
            pts = sb("pts", [P, 2, NG * SEQ], F32, att)
            ptn = sb("ptn", [HALF, 2, NG * P], F32, att)
            sts = sb("sts", [P, 2, 4 * P], F32, att)
            zs = sb("zs", [P, 2, TOK], F32, att)
            t1 = sb("t1", [P, 2, TOK], F32, att)
            sh = sb("sh", [P, TOK], F32, att)
            cosr = sb("cosr", [P, TOK], F32, att)
            sinr = sb("sinr", [P, TOK], F32, att)
            mx = sb("mx", [P, 2, 2], F32, att)
            nmx = sb("nmx", [P, 2, 2], F32, att)
            den = sb("den", [P, 2, 2], F32, att)
            esk = sb("esk", [P, 2, 2], F32, att)
            rden = sb("rden", [P, 2, 2], F32, att)
        with ExitStack() as out_mem:
            mhi = sb("mhi", [P, KD, TOK], F32R, out_mem)
            mlo = sb("mlo", [P, KD, TOK], F32R, out_mem)
            ma = sb("ma", [P, 2, TOK], F32, out_mem)
            mb = sb("mb", [P, 2, TOK], F32, out_mem)
        ps = ctx.enter_context(nc.psum_tensor("ps", [P, 8, 512], F32))

        passed = sem("passed")
        start_in = sem("start_in")
        set_up = sem("set_up")
        raw_in = [sem(f"raw_in{s}") for s in range(RAW)]
        whi_done = sem("whi_done")
        wlo_done = sem("wlo_done")
        unit_used = sem("unit_used")
        taken = sem("taken")
        silu_done = sem("silu_done")
        prod_done = sem("prod_done")
        acthi_done = sem("acthi_done")
        actlo_done = sem("actlo_done")
        xg_ready = sem("xg_ready")
        xhi_done = sem("xhi_done")
        xs_ready = sem("xs_ready")
        sq_done = sem("sq_done")
        ssq_done = sem("ssq_done")
        ms_ready = sem("ms_ready")
        rms_done = sem("rms_done")
        rinv_ready = sem("rinv_ready")
        tabs_ready = sem("tabs_ready")
        zs_done = sem("zs_done")
        t1_done = sem("t1_done")
        shuf_done = sem("shuf_done")
        shs_done = sem("shs_done")
        rope_done = sem("rope_done")
        qbd_zero = sem("qbd_zero")
        qbd_done = sem("qbd_done")
        kvt_done = sem("kvt_done")
        kvtok_done = sem("kvtok_done")
        kst_out = [sem(f"kst_out{s}") for s in range(2)]
        v_out = sem("v_out")
        gexp_done = sem("gexp_done")
        gadd_done = sem("gadd_done")
        gate_ready = sem("gate_ready")
        kb_in = sem("kb_in")
        kvc_in = [sem(f"kvc_in{s}") for s in range(2)]
        kvc_used = sem("kvc_used")
        st_ready = sem("st_ready")
        sts_done = sem("sts_done")
        s_scores = sem("s_scores")
        s_max = sem("s_max")
        s_masked = sem("s_masked")
        s_exp = sem("s_exp")
        s_den = sem("s_den")
        s_rden = sem("s_rden")
        s_norm = sem("s_norm")
        s_pt = sem("s_pt")
        s_pts = sem("s_pts")
        s_pv = sem("s_pv")
        s_ohi = sem("s_ohi")
        s_olo = sem("s_olo")
        mab_done = sem("mab_done")
        mhi_done = sem("mhi_done")
        mlo_done = sem("mlo_done")
        y_sum = sem("y_sum")
        y_done = sem("y_done")
        copy_out = sem("copy_out")
        y_out = sem("y_out")

        block = ctx.enter_context(nc.Block())
        ident = const[:, C_ID:C_ID + P]

        def at(v):
            return bass.ds(v, 1)

        def plain(eng):
            eng.sem_inc(passed, 1)

        def segments(i):
            kind, _, t = ITEMS[i]
            return {"B": (P * (t + 1), 2), "A": (NG * P * (t + 1), 1), "SB": (N_SB, 2), "SA": (N_SA, 1)}[kind]

        def out_place(i, o):
            kind, h, t = ITEMS[i]
            if kind == "B":
                return o[:, 2 + h, t * P:(t + 1) * P], ps[:, BK_O, 0:P]
            if kind == "A":
                r = slice(HD * (h % 2), HD * (h % 2 + 1))
                return o[r, h // 2, t * P:(t + 1) * P], ps[r, BK_O, 0:P]
            s0 = SEQ + HALF * h
            return o[:, 2:6, s0:s0 + HALF], ps[:, BK_O, 0:P].rearrange("p (c n) -> p c n", c=4)

        def out_halves(half, hh, o):
            r = slice(HD * hh, HD * (hh + 1))
            s0 = SEQ + HALF * half
            src = ps[r, BK_KV, 0:P].rearrange("p (c h n) -> p c h n", c=2, h=2)[:, :, hh, :]
            return o[r, 0:2, s0:s0 + HALF], src

        @block.sync
        def _(sp):
            sp.dma_start(x[:, :, :], a["x"]).then_inc(start_in, 16)
            sp.dma_start(gains[:, :, :], a["gains"]).then_inc(start_in, 16)
            sp.dma_start(sinks[:, :, :], a["sinks"]).then_inc(start_in, 16)
            sp.dma_start(const[:, :], a["const"]).then_inc(start_in, 16)

            kpre, vpre = a["kcache"], a["vcache"]
            big = a["cache_a3"][:, :, NT:, :, :, :].rearrange(
                "l b w v h d -> l b (w v h d)").rearrange("l b (f k n) -> l b f k n", f=2, k=P)
            big_o = a["new_a3_sample"][:, :, :DILS[2][0] - NT, :, :, :].rearrange(
                "l b w v h d -> l b (w v h d)").rearrange("l b (f k n) -> l b f k n", f=2, k=P)
            mid = a["cache_a2"][:, :, NT:, :, :, :].rearrange(
                "l b w v h d -> l b (w v h d)").rearrange("l b (k n) -> l b k n", k=P)
            mid_o = a["new_a2_sample"][:, :, :DILS[1][0] - NT, :, :, :].rearrange(
                "l b w v h d -> l b (w v h d)").rearrange("l b (k n) -> l b k n", k=P)

            def load_at(L, base, i, step, s, src, tiles):
                sp.wait_ge(wlo_done, L * NU + i * step + base + s + 1)
                sp.dma_start(raw[:, (base + s) % RAW, 0:tiles * P], src).then_inc(raw_in[(base + s) % RAW], 16)

            def one(ap):
                return ap.rearrange("o p n -> (o p) n")

            def ffn_loads(L, f):
                wg, wu, wd = (a[f"ffn{f + 1}_{k}"] for k in ("gate", "up", "down"))

                def group(i):
                    for s in range(4):
                        w = (wg, wu)[s % 2]
                        load_at(L, U_GU[f], i, 4, s, one(w[at(L * KF + 2 * i + s // 2), :, :]), UT)

                with sp.Fori(0, NB) as i:
                    group(i)
                    sp.dma_start(one(big_o[at(L), at(i), f, :, :].rearrange("l b k n -> (l b) k n")),
                                 one(big[at(L), at(i), f, :, :].rearrange("l b k n -> (l b) k n")))\
                        .then_inc(copy_out, 16)
                with sp.Fori(NB, KF // 2) as i:
                    group(i)
                with sp.Fori(0, KD // 2) as i:
                    for o in range(2):
                        for s in range(4):
                            k0, n = DN_K0[s] * P, DN_TILES[s]
                            load_at(L, U_DN[f], i, 8, 4 * o + s,
                                    one(wd[at(L * KD + 2 * i + o), :, k0:k0 + n * P]), n)
                    sp.dma_start(one(mid_o[at(L), at(i + 4 * f), :, :].rearrange("l b k n -> (l b) k n")),
                                 one(mid[at(L), at(i + 4 * f), :, :].rearrange("l b k n -> (l b) k n")))\
                        .then_inc(copy_out, 16)

            def store_kv(L, n):
                kind, g, c = COLS[KV_UNITS[n]]
                name = ("a1", "a2", "a3", "b")[g]
                kv = 0 if kind == "k" else 1
                heads = P * c
                sp.wait_ge(kvtok_done, L * 14 + n + 1)
                if kind == "k":
                    nk = K_UNITS.index(KV_UNITS[n])
                    src, new, done = kst[:, nk % 2, 0:2 * P], kst[0:HALF, nk % 2, 2 * P:4 * P], kst_out[nk % 2]
                    src = src.rearrange("p (t f) -> p t f", t=2)
                    new = new.rearrange("p (t f) -> p t f", t=2)
                else:
                    src, new, done = (v[:, :, v_slot(g, c) * P:(v_slot(g, c) + 1) * P] for v in (vtok, vnew)), None, v_out
                    src, new = tuple(src)
                t0 = 0 if g in (1, 2) else 1
                dst = a[f"new_{name}_prompt"].rearrange("l n (t p) v h d -> l p (n t) v (h d)", p=P)
                dst = dst[at(L), :, :, kv, heads:heads + P].rearrange("l p t f -> (l p) t f")
                sp.dma_start(dst, src[:, t0:2, :]).then_inc(done, 16)
                dst = a[f"new_{name}_sample"]
                w = dst.shape[2]
                dst = dst[:, :, w - NT:w, :, :, :].rearrange("l b t v h d -> l b t v (h d)")
                for half in range(2):
                    to = dst[at(L), 4 * half:4 * half + 4, :, kv, heads:heads + P].rearrange("l b t f -> (l b) t f")
                    sp.dma_start(to, new[:, half, :]).then_inc(done, 16)

            def mixer_loads(L):
                w_in, w_br, w_out = a["w_in"], a["w_branch"], a["w_out"]
                for v in range(N_IN + 2 * KD):
                    if v < N_IN:
                        load_at(L, U_IN, 0, 0, v, one(w_in[at(L * N_IN + v), :, :]), UT)
                    elif v < N_IN + KD:
                        load_at(L, U_IN, 0, 0, v, one(w_br[at(L * KD + v - N_IN), :, :]), BR_TILES)
                    else:
                        load_at(L, U_IN, 0, 0, v, one(w_out[at(L * KD + v - N_IN - KD), :, :]), UT)
                    if v == 12:
                        sp.wait_ge(unit_used, L * NU + RING + U_IN)
                        sp.dma_start(kb[:, :, :], kpre_b(L)).then_inc(kb_in, 16)
                        sp.dma_start(vb[:, :, :], vpre_b(L)).then_inc(kb_in, 16)
                    for n in range(N_KV):
                        if KV_PLACE[n] == v:
                            half, b, c = n // 8 % 2, n // 2 % 4, n % 2
                            src = (kpre if n < N_KV // 2 else vpre)[at((L * NB + 4 * half + b) * 2 + c), :, :]
                            if n >= 2:
                                sp.wait_ge(kvc_used, L * N_KV + n - 1)
                            sp.dma_start(kvc[:, n % 2, :], one(src)).then_inc(kvc_in[n % 2], 16)
                    for n, u in enumerate(KV_UNITS):
                        if u + 8 == v:
                            store_kv(L, n)
                    if v == N_IN + KD:
                        for name, g in (("a1", 0), ("b", 3)):
                            src = a[f"cache_{name}"][:, :, NT:, :, :, :].rearrange(
                                "l b w v h d -> l b (w v h d)").rearrange("l b (k n) -> l k b n", k=P)
                            to = a[f"new_{name}_sample"][:, :, :P - NT, :, :, :].rearrange(
                                "l b w v h d -> l b (w v h d)").rearrange("l b (k n) -> l k b n", k=P)
                            sp.dma_start(to[at(L), :, :, :].rearrange("l k b n -> (l k) b n"),
                                         src[at(L), :, :, :].rearrange("l k b n -> (l k) b n"))\
                                .then_inc(copy_out, 16)
                sp.wait_ge(v_out, (L + 1) * (7 * 48))
                plain(sp)
                sp.wait_ge(kst_out[0], (L + 1) * (4 * 48))
                plain(sp)
                sp.wait_ge(kst_out[1], (L + 1) * (3 * 48))
                plain(sp)

            def kpre_b(L):
                return a["kcache_b"][at(L), :, :, :].rearrange("l p b f -> (l p) b f")

            def vpre_b(L):
                return a["vcache_b"][at(L), :, :, :].rearrange("l p b f -> (l p) b f")

            with sp.Fori(0, DEPTH) as L:
                ffn_loads(L, 0)
                mixer_loads(L)
                ffn_loads(L, 1)
            sp.wait_ge(y_done, KD)
            sp.dma_start(a["y"], x[:, :, :]).then_inc(y_out, 16)
            sp.wait_ge(y_out, 16)
            sp.wait_ge(copy_out, 16 * DEPTH * (2 * NB + KD + 2))
            sp.wait_ge(v_out, DEPTH * 7 * 48)
            sp.wait_ge(kst_out[0], DEPTH * 4 * 48)
            sp.wait_ge(kst_out[1], DEPTH * 3 * 48)

        @block.tensor
        def _(pe):
            def product(out, slot, tile, hi, lo, first, last):
                w0, w1 = (w[:, slot, tile * P:(tile + 1) * P] for w in (whi, wlo))
                pe.matmul(out, w0, hi, start=first, stop=False)
                pe.matmul(out, w0, lo, start=False, stop=False)
                return pe.matmul(out, w1, hi, start=False, stop=last)

            def sum_squares(n):
                pe.wait_ge(ssq_done, (n + 1) * (KD + 1))
                pe.matmul(ps[:, BK_O, 0:TOK], ones[:, :], ssq[:, :], start=True, stop=True).then_inc(ms_ready, 1)

            def ffn_products(L, f):
                def gate_up(i, first):
                    for s in range(4):
                        pe.wait_ge(wlo_done, L * NU + i * 4 + U_GU[f] + s + RAW + 1)
                        pe.wait_ge(taken, L * NR + i * 4 + R_GU[f] + s + 1)
                        for k in range(KD):
                            if first and s == 0:
                                pe.wait_ge(xs_ready, (L * 3 + 2 * f) * KD + k + 1)
                            mm = product(ps[:, s, 0:TOK], s, k, xhi[:, k, :], xlo[:, k, :], k == 0, k == KD - 1)
                        mm.then_inc(unit_used, 1)
                        if first and s == 0:
                            sum_squares(L * 3 + 2 * f)

                def down(i, first):
                    for o in range(2):
                        pe.wait_ge(taken, L * NR + i * 2 + R_DN[f] + o + RING - 1)
                        for s in range(4):
                            pe.wait_ge(wlo_done, L * NU + i * 8 + U_DN[f] + 4 * o + s + RAW + 1)
                            for n in range(DN_TILES[s]):
                                k = DN_K0[s] + n
                                if first and o == 0:
                                    pe.wait_ge(actlo_done, L * 2 * KF + f * KF + 2 + k + 1)
                                mm = product(ps[:, BK_DN + o, 0:TOK], s, n, act_hi[:, k, :], act_lo[:, k, :],
                                             k == 0, k == KF - 1)
                            mm.then_inc(unit_used, 1)

                gate_up(0, True)
                with pe.Fori(1, KF // 2) as i:
                    gate_up(i, False)
                down(0, True)
                with pe.Fori(1, KD // 2) as i:
                    down(i, False)

            def columns(i):
                if i == 0:
                    return 0, slice(0, NT)
                if i < 5:
                    return 1, slice(i - 1, NT, 4)
                return 2, slice(i - 5, i - 4)

            def mixer_products(L):
                def scores(i):
                    kind, h, t = ITEMS[i]
                    if i >= 1:
                        pe.wait_ge(s_masked, L * NI + i)
                    if kind == "B":
                        if i == 0:
                            pe.wait_ge(rope_done, L * 17 + 5)
                        n = P * (t + 1)
                        for j in range(2):
                            r = slice(HD * j, HD * (j + 1))
                            mm = pe.matmul(ps[:, BK_S + j, 0:n], qk[r, 1 + h, t * P:(t + 1) * P], qk[r, 0, 0:n],
                                           start=True, stop=True)
                    elif kind == "A":
                        pe.wait_ge(rope_done, L * 17 + 17)
                        n = P * (t + 1)
                        r = slice(HD * (h % 2), HD * (h % 2 + 1))
                        for g in range(NG):
                            bank, col = divmod(g * n, 512)
                            mm = pe.matmul(ps[:, BK_S + bank, col:col + n],
                                           qk[r, qk_slot("q", g, h // 2), t * P:(t + 1) * P],
                                           qk[r, qk_slot("k", g, h // 2), 0:n], start=True, stop=True)
                    elif kind == "SB":
                        pe.wait_ge(sts_done, L * 3 + 1)
                        new = slice(SEQ + HALF * h, SEQ + HALF * (h + 1))
                        for j in range(2):
                            pe.transpose(ps[:, BK_S + j, 0:P], sts[:, j, h * P:(h + 1) * P], ident)
                            r = slice(HD * j, HD * (j + 1))
                            for c in range(4):
                                mm = pe.matmul(ps[HALF * c:HALF * (c + 1), BK_S + j, P:P + HALF],
                                               qk[r, 1 + c, new], qk[r, 0, new], start=True, stop=True)
                    else:
                        pe.wait_ge(sts_done, L * 3 + 2 + h)
                        new = slice(SEQ + HALF * h, SEQ + HALF * (h + 1))
                        for g in range(NG):
                            pe.transpose(ps[:, BK_S, g * P:(g + 1) * P], sts[:, h, g * P:(g + 1) * P], ident)
                            for hh in range(4):
                                mm = pe.matmul(ps[HALF * hh:HALF * (hh + 1), BK_S,
                                                  NG * P + g * HALF:NG * P + (g + 1) * HALF],
                                               qbd[:, g, hh // 2, hh % 2, HALF * h:HALF * (h + 1)],
                                               qk[:, qk_slot("k", g, hh // 2), new], start=True, stop=True)
                    mm.then_inc(s_scores, 1)

                def transposes(i):
                    kind, h, t = ITEMS[i]
                    pe.wait_ge(s_norm, L * NI + i + 1)
                    if i >= 1:
                        pe.wait_ge(s_pts, L * NI + i)
                    if i == 6:
                        pe.wait_ge(sts_done, L * 3 + 1)
                    eb = e[:, i % 2, :]
                    if kind in ("A", "B"):
                        for n in range((NG if kind == "A" else 2) * (t + 1)):
                            mm = pe.transpose(ps[:, BK_T + n // 4, n % 4 * P:(n % 4 + 1) * P],
                                              eb[:, n * P:(n + 1) * P], ident)
                    else:
                        for n in range(2 if kind == "SB" else NG):
                            o = n * N_SB if kind == "SB" else n * P
                            on = n * N_SB + P if kind == "SB" else NG * P + n * HALF
                            pe.transpose(ps[:, BK_T, n * P:(n + 1) * P], eb[:, o:o + P], ident)
                            mm = pe.transpose(ps[0:HALF, BK_T + 1, n * P:(n + 1) * P], eb[:, on:on + HALF], ident)
                    mm.then_inc(s_pt, 1)

                def values(i):
                    kind, h, t = ITEMS[i]
                    pe.wait_ge(s_pts, L * NI + i + 1)
                    if i >= 1:
                        pe.wait_ge(s_olo, L * NI + i)
                    pb, nb = pts[:, i % 2, :], ptn[:, i % 2, :]
                    if kind == "B":
                        pe.wait_ge(kvtok_done, L * 14 + 2)
                        for j in range(2):
                            for kt in range(t + 1):
                                n = j * (t + 1) + kt
                                mm = pe.matmul(ps[HD * j:HD * (j + 1), BK_O, 0:P],
                                               vtok[:, kt, 6 * P + HD * j:6 * P + HD * (j + 1)],
                                               pb[:, n * P:(n + 1) * P], start=kt == 0, stop=kt == t)
                        mm.then_inc(s_pv, 1)
                    elif kind == "A":
                        pe.wait_ge(kvtok_done, L * 14 + 14)
                        for g in range(NG):
                            for kt in range(t + 1):
                                n = g * (t + 1) + kt
                                f0 = v_slot(g, h // 2) * P + HD * (h % 2)
                                mm = pe.matmul(ps[HD * (h % 2):HD * (h % 2 + 1), BK_O, 0:P],
                                               vtok[:, kt, f0:f0 + HD], pb[:, n * P:(n + 1) * P],
                                               start=n == 0, stop=n == NG * (t + 1) - 1)
                        mm.then_inc(s_pv, 1)
                    elif kind == "SB":
                        pe.wait_ge(kb_in, L * 32 + 32)
                        for j in range(2):
                            r = slice(HD * j, HD * (j + 1))
                            pe.matmul(ps[r, BK_O, 0:P], vnew[:, h, 6 * P + HD * j:6 * P + HD * (j + 1)],
                                      nb[:, j * P:(j + 1) * P], start=True, stop=False)
                            for b in range(4):
                                cols = pb[:, j * P:(j + 1) * P].rearrange("p (c n) -> p c n", c=4)[:, :, NT * b:NT * (b + 1)]
                                to = ps[r, BK_O, 0:P].rearrange("p (c n) -> p c n", c=4)[:, :, NT * b:NT * (b + 1)]
                                mm = pe.matmul(to, vb[:, 4 * h + b, r], cols, start=False, stop=b == 3)
                        mm.then_inc(s_pv, 1)
                    else:
                        if h == 0:
                            pe.wait_ge(sts_done, L * 3 + 3)
                        for c in range(2):
                            for g in range(NG):
                                pe.matmul(ps[:, BK_KV, HD * c:HD * (c + 1)],
                                          vnew[:, h, v_slot(g, c) * P:(v_slot(g, c) + 1) * P],
                                          nb[:, g * P + HD * c:g * P + HD * (c + 1)],
                                          start=c == 0 and g == 0, stop=False, skip_group_check=True)

                def cached(n):
                    half, b, c = n // 8 % 2, n // 2 % 4, n % 2
                    pe.wait_ge(kvc_in[n % 2], (L * (N_KV // 2) + n // 2 + 1) * 16)
                    if n == 0:
                        pe.wait_ge(kvtok_done, L * 14 + 14)
                        pe.wait_ge(qbd_done, L * 6 + 6)
                    if n == 8:
                        pe.wait_ge(sts_done, L * 3 + 2)
                    for i in range(CT):
                        g, t = columns(i)
                        w = kvc[:, n % 2, i * P:(i + 1) * P]
                        toks = slice(NT * b + t.start, NT * b + t.stop, t.step or 1)
                        if n < N_KV // 2:
                            s0 = HALF * half
                            mv = qbd[:, g, c, :, s0 + toks.start:s0 + toks.stop:toks.step]
                            to = ps[:, BK_KV, g * P:(g + 1) * P]
                            flags = dict(start=True, stop=True)
                        else:
                            mv = pts[:, half, g * P:(g + 1) * P].rearrange("p (h n) -> p h n", h=4)[:, 2 * c:2 * c + 2, toks]
                            to = ps[:, BK_KV, 0:P]
                            flags = dict(start=False, stop=(n % 8 == 7 and i == CT - 1), skip_group_check=True)
                        to = to.rearrange("p (h n) -> p h n", h=4)[:, 2 * c:2 * c + 2, toks]
                        mm = pe.matmul(to, w, mv, **flags)
                    mm.then_inc(kvc_used, 1)

                def cached_b():
                    pe.wait_ge(kb_in, L * 32 + 32)
                    pe.wait_ge(s_pts, L * NI + 6)
                    for j in range(2):
                        r = slice(HD * j, HD * (j + 1))
                        for b in range(NB):
                            to = ps[:, BK_T + j, b // 4 * P:(b // 4 + 1) * P].rearrange("p (c n) -> p c n", c=4)
                            mm = pe.matmul(to[:, :, NT * (b % 4):NT * (b % 4 + 1)], kb[r, b, :],
                                           qk[r, 1:5, SEQ + NT * b:SEQ + NT * (b + 1)], start=True, stop=True)
                    mm.then_inc(st_ready, 1)

                def token_rows(u):
                    n = KV_UNITS.index(u)
                    if COLS[u][0] == "k":
                        src = qk[:, qk_slot(*COLS[u]), :]
                        pe.wait_ge(rope_done, L * 17 + QK_UNITS.index(u) + 1)
                    else:
                        src = t1[:, u % 2, :]
                        pe.wait_ge(t1_done, L * N_IN + u + 1)
                    if n >= 1:
                        pe.wait_ge(kvtok_done, L * 14 + n)
                    pe.transpose(ps[:, BK_KV, 0:P], src[:, 0:P], ident)
                    pe.transpose(ps[:, BK_KV, P:2 * P], src[:, P:2 * P], ident)
                    pe.transpose(ps[0:HALF, BK_KV, 2 * P:3 * P], src[:, SEQ:SEQ + HALF], ident)
                    pe.transpose(ps[0:HALF, BK_KV, 3 * P:4 * P], src[:, SEQ + HALF:TOK], ident).then_inc(kvt_done, 1)

                for kind, n in STEPS:
                    if kind == "U":
                        pe.wait_ge(wlo_done, L * NU + U_IN + n + RAW + 1)
                        if n >= 2:
                            pe.wait_ge(zs_done, L * N_IN + n - 1)
                        for k in range(KD):
                            if n == 0:
                                pe.wait_ge(xs_ready, (L * 3 + 1) * KD + k + 1)
                            mm = product(ps[:, n % 2, 0:TOK], n % RING, k, xhi[:, k, :], xlo[:, k, :], k == 0, k == KD - 1)
                        mm.then_inc(unit_used, 1)
                        if n == 0:
                            sum_squares(L * 3 + 1)
                    elif kind == "R":
                        token_rows(n)
                    elif kind == "S":
                        scores(n)
                    elif kind == "T":
                        transposes(n)
                    elif kind == "O":
                        values(n)
                    elif kind in ("K", "V"):
                        cached(n)
                    elif kind == "E" and n > 0:
                        pass
                    elif kind == "KB":
                        cached_b()
                for m in range(KD):
                    ba, bb = BK_BR[m % 2]
                    pe.wait_ge(wlo_done, L * NU + U_BR + m + RAW + 1)
                    if m == 0:
                        pe.wait_ge(s_olo, L * NI + NI)
                        pe.wait_ge(zs_done, L * N_IN + N_IN)
                    else:
                        pe.wait_ge(taken, L * NR + R_BR + m + RING - 1)
                    for k in range(BR_TILES):
                        out = ps[:, ba if k < 2 else bb, 0:TOK]
                        mm = product(out, m % RING, k, ohi[:, k, :], olo[:, k, :], k in (0, 2), k in (1, 5))
                    mm.then_inc(unit_used, 1)
                for m in range(KD):
                    pe.wait_ge(wlo_done, L * NU + U_WO + m + RAW + 1)
                    pe.wait_ge(taken, L * NR + R_WO + m + RING - 1)
                    for k in range(KD):
                        if m == 0:
                            pe.wait_ge(mlo_done, L * KD + k + 1)
                        mm = product(ps[:, BK_WO + m % 2, 0:TOK], m % RING, k, mhi[:, k, :], mlo[:, k, :],
                                     k == 0, k == KD - 1)
                    mm.then_inc(unit_used, 1)

            pe.wait_ge(set_up, 2)
            pe.wait_ge(start_in, 64)
            with pe.Fori(0, DEPTH) as L:
                ffn_products(L, 0)
                mixer_products(L)
                ffn_products(L, 1)
            sum_squares(3 * DEPTH)

        @block.scalar
        def _(act):
            def round_unit(L, base, i, step, s, tiles):
                act.wait_ge(unit_used, L * NU + i * step + base + s + 1)
                act.wait_ge(raw_in[(base + s) % RAW], (L * (NU // 2) + i * (step // 2) + (base + s) // 2 + 1) * 16)
                nc.scalar.activation(whi[:, (base + s) % RING, 0:tiles * P], raw[:, (base + s) % RAW, 0:tiles * P],
                                     ACT.Copy).then_inc(whi_done, 1)

            def root(n):
                act.wait_ge(ms_ready, n + 1)
                nc.scalar.activation(rms[:, :], ps[:, BK_O, 0:TOK], ACT.Sqrt, bias=eps[:, :], scale=1.0 / D)\
                    .then_inc(rms_done, 1)

            def round_x(norm, m, slot):
                act.wait_ge(xg_ready, norm * KD + m + 1)
                dst = xhi[:, m, :] if isinstance(m, int) else xhi[:, at(m), :].rearrange("p o n -> p (o n)")
                nc.scalar.activation(dst, xg[:, slot, :], ACT.Copy).then_inc(xhi_done, 1)

            def ffn_act(L, f):
                def gate_up(i, first, tiles):
                    if first:
                        root(L * 3 + 2 * f)
                    for s in range(4):
                        if s % 2 == 0:
                            act.wait_ge(taken, L * NR + i * 4 + R_GU[f] + s + RING + 1)
                            nc.scalar.activation(gate_s[:, s // 2, :], gate_s[:, s // 2, :], ACT.Silu)\
                                .then_inc(silu_done, 1)
                        round_unit(L, U_GU[f] + 4, i, 4, s, tiles[s])
                        if s % 2 == 1:
                            act.wait_ge(prod_done, L * 2 * KF + i * 2 + f * KF + s // 2 + 1)
                            j = i * 2 + s // 2
                            dst = act_hi[:, j, :] if isinstance(j, int) else \
                                act_hi[:, at(j), :].rearrange("p o n -> p (o n)")
                            nc.scalar.activation(dst, up_s[:, s // 2, :], ACT.Copy).then_inc(acthi_done, 1)

                def down(i, tail):
                    for o in range(2):
                        for s in range(4):
                            if o == 0 or tail != "none":
                                round_unit(L, U_DN[f] + 4, i, 8, 4 * o + s,
                                           UT if o == 1 and tail == "next" else DN_TILES[s])
                        round_x(L * 3 + 1 + 2 * f, i * 2 + o, o)

                gate_up(0, True, (UT,) * 4)
                with act.Fori(1, KF // 2 - 1) as i:
                    gate_up(i, False, (UT,) * 4)
                gate_up(KF // 2 - 1, False, DN_TILES)
                with act.Fori(0, KD // 2 - 1) as i:
                    down(i, "same")
                down(KD // 2 - 1, ("next", "none")[f])

            def mixer_act(L):
                for kind, n in STEPS:
                    if kind == "U":
                        if n == 0:
                            root(L * 3 + 1)
                        act.wait_ge(unit_used, L * NU + U_IN + n + RING + 1)
                        if n >= 2:
                            act.wait_ge(t1_done, L * N_IN + n - 1)
                            if n - 2 in QK_UNITS:
                                act.wait_ge(shuf_done, L * 17 + QK_UNITS.index(n - 2) + 1)
                        nc.scalar.activation(zs[:, n % 2, :], ps[:, n % 2, 0:TOK], ACT.Copy).then_inc(zs_done, 1)
                        round_unit(L, U_IN + 4, 0, 0, n, UT if n + 4 < N_IN else BR_TILES)
                    elif kind == "R":
                        g, c = COLS[n][1:]
                        act.wait_ge(kvt_done, L * 14 + KV_UNITS.index(n) + 1)
                        if COLS[n][0] == "k":
                            nk = K_UNITS.index(n)
                            if nk >= 2:
                                tot = (4 * 48, 3 * 48)[nk % 2]
                                act.wait_ge(kst_out[nk % 2], L * tot + 48 * (nk // 2))
                            to, new = kst[:, nk % 2, 0:2 * P], kst[0:HALF, nk % 2, 2 * P:4 * P]
                            nc.scalar.activation(to, ps[:, BK_KV, 0:2 * P], ACT.Copy)
                            nc.scalar.activation(new, ps[0:HALF, BK_KV, 2 * P:4 * P], ACT.Copy)\
                                .then_inc(kvtok_done, 1)
                        else:
                            v0 = v_slot(g, c) * P
                            nc.scalar.activation(vtok[:, :, v0:v0 + P],
                                                 ps[:, BK_KV, 0:2 * P].rearrange("p (t f) -> p t f", t=2), ACT.Copy)
                            nc.scalar.activation(vnew[:, :, v0:v0 + P],
                                                 ps[0:HALF, BK_KV, 2 * P:4 * P].rearrange("p (t f) -> p t f", t=2),
                                                 ACT.Copy).then_inc(kvtok_done, 1)
                    elif kind == "G":
                        k = G_UNITS.index(n)
                        act.wait_ge(t1_done, L * N_IN + n + 1)
                        nc.scalar.activation(gate[:, k, :], t1[:, n % 2, :], ACT.Exp, scale=-1.0).then_inc(gexp_done, 1)
                    elif kind == "S":
                        what, h, t = ITEMS[n]
                        w, segs = segments(n)
                        act.wait_ge(s_masked, L * NI + n + 1)
                        for j in range(segs):
                            mm = nc.scalar.activation(e[:, n % 2, j * w:(j + 1) * w], e[:, n % 2, j * w:(j + 1) * w],
                                                      ACT.Exp, bias=nmx[:, n % 2, j:j + 1], scale=SCALE,
                                                      accum_out=den[:, n % 2, j:j + 1])
                            if segs == 2:
                                col = h + 4 * j if what == "B" else 8 + j
                                sink = sinks[:, at(L), col:col + 1].rearrange("p o n -> p (o n)")
                                mm = nc.scalar.activation(esk[:, n % 2, j:j + 1], nmx[:, n % 2, j:j + 1], ACT.Exp,
                                                          bias=sink)
                        mm.then_inc(s_exp, 1)
                    elif kind == "T":
                        what, h, t = ITEMS[n]
                        act.wait_ge(s_pt, L * NI + n + 1)
                        if n >= 2:
                            act.wait_ge(s_pv, L * NPV + n - 1)
                        if what in ("A", "B"):
                            w = (NG if what == "A" else 2) * (t + 1) * P
                        else:
                            w = (NG if what == "SA" else 2) * P
                            nc.scalar.activation(ptn[:, n % 2, 0:w], ps[0:HALF, BK_T + 1, 0:w], ACT.Copy)
                        flat = ps[:, BK_T:BK_T + 2, :].rearrange("p b n -> p (b n)")
                        nc.scalar.activation(pts[:, n % 2, 0:w], flat[:, 0:w], ACT.Copy).then_inc(s_pts, 1)
                    elif kind == "E":
                        if n == 0:
                            act.wait_ge(st_ready, L + 1)
                            nc.scalar.activation(sts[:, :, 0:2 * P], ps[:, BK_T:BK_T + 2, 0:2 * P], ACT.Copy)\
                                .then_inc(sts_done, 1)
                        else:
                            act.wait_ge(kvc_used, L * N_KV + 8 * n)
                            act.wait_ge(s_scores, L * NI + 10)
                            nc.scalar.activation(sts[:, n - 1, 0:NG * P], ps[:, BK_KV, 0:NG * P], ACT.Copy)\
                                .then_inc(sts_done, 1)
                    elif kind == "W":
                        if ITEMS[n][0] == "SA":
                            act.wait_ge(kvc_used, L * N_KV + N_KV // 2 + 8 * (ITEMS[n][1] + 1))
                            for hh in range(2):
                                to, src = out_halves(ITEMS[n][1], hh, ohi)
                                mm = nc.scalar.activation(to, src, ACT.Copy)
                        else:
                            act.wait_ge(s_pv, L * NPV + n + 1)
                            to, src = out_place(n, ohi)
                            mm = nc.scalar.activation(to, src, ACT.Copy)
                        mm.then_inc(s_ohi, 1)
                for m in range(KD):
                    round_unit(L, U_BR + 4, 0, 0, m, BR_TILES if m < 4 else UT)
                    act.wait_ge(mab_done, L * KD + m + 1)
                    nc.scalar.activation(mhi[:, m, :], ma[:, m % 2, :], ACT.Copy).then_inc(mhi_done, 1)
                for m in range(KD):
                    round_unit(L, U_WO + 4, 0, 0, m, UT)
                    round_x(L * 3 + 2, m, m % 2)

            act.wait_ge(set_up, 2)
            act.wait_ge(start_in, 64)
            for m in range(KD):
                round_x(0, m, m % 2)
            with act.Fori(0, DEPTH) as L:
                for s in range(4):
                    round_unit(L, 0, 0, 0, s, UT)
                ffn_act(L, 0)
                mixer_act(L)
                ffn_act(L, 1)
            root(3 * DEPTH)

        @block.vector
        def _(dve):
            def rest_unit(L, base, i, step, s, tiles):
                dve.wait_ge(whi_done, L * NU + i * step + base + s + 1)
                nc.vector.tensor_tensor(wlo[:, (base + s) % RING, 0:tiles * P], raw[:, (base + s) % RAW, 0:tiles * P],
                                        whi[:, (base + s) % RING, 0:tiles * P].bitcast(F32), ALU.subtract)\
                    .then_inc(wlo_done, 1)

            def chunk(t, m):
                return t[:, m, :] if isinstance(m, int) else t[:, at(m), :].rearrange("p o n -> p (o n)")

            def gain(norm, m):
                if isinstance(norm, int) and isinstance(m, int):
                    return gains[:, norm, m:m + 1]
                g = gains[:, :, :].rearrange("p n k -> p (n k)")
                return g[:, at(norm * KD + m)]

            def scale_x(norm, m, slot):
                nc.vector.tensor_scalar(xg[:, slot, :], chunk(x, m), gain(norm, m), None, ALU.mult)\
                    .then_inc(xg_ready, 1)

            def rest_x(norm, m, slot):
                dve.wait_ge(xhi_done, norm * KD + m + 1)
                nc.vector.tensor_tensor(chunk(xlo, m), xg[:, slot, :], chunk(xhi, m).bitcast(F32), ALU.subtract)\
                    .then_inc(xs_ready, 1)

            def invert(n):
                dve.wait_ge(rms_done, n + 1)
                nc.vector.reciprocal(rinv[:, :], rms[:, :]).then_inc(rinv_ready, 1)
                dve.wait_ge(rinv_ready, n + 1)

            def add_to_x(L, bank, m, result, factor):
                nc.vector.scalar_tensor_tensor(chunk(x, m), ps[:, bank, 0:TOK], factor, chunk(x, m),
                                               ALU.mult, ALU.add).then_inc(taken, 1)
                dve.wait_ge(taken, L * NR + result + RING + 1)

            def ffn_vec(L, f):
                def gate_up(i, first, tiles):
                    if first:
                        invert(L * 3 + 2 * f)
                    for s in range(4):
                        dve.wait_ge(unit_used, L * NU + i * 4 + U_GU[f] + s + RING + 1)
                        if s % 2 == 0:
                            dve.wait_ge(actlo_done, L * 2 * KF + i * 2 + f * KF + s // 2 + 1)
                        nc.vector.tensor_tensor((gate_s, up_s)[s % 2][:, s // 2, :], ps[:, s, 0:TOK], rinv[:, :],
                                                ALU.mult).then_inc(taken, 1)
                        rest_unit(L, U_GU[f] + 4, i, 4, s, tiles[s])

                def down(i, tail):
                    norm = L * 3 + 1 + 2 * f
                    for o in range(2):
                        for s in range(4):
                            if s == 3:
                                dve.wait_ge(unit_used, L * NU + i * 8 + U_DN[f] + 4 * o + s + RING + 1)
                                add_to_x(L, BK_DN + o, i * 2 + o, i * 2 + R_DN[f] + o, 0.5)
                                scale_x(norm, i * 2 + o, o)
                            if o == 0 or tail != "none":
                                rest_unit(L, U_DN[f] + 4, i, 8, 4 * o + s,
                                          UT if o == 1 and tail == "next" else DN_TILES[s])
                        rest_x(norm, i * 2 + o, o)

                gate_up(0, True, (UT,) * 4)
                with dve.Fori(1, KF // 2 - 1) as i:
                    gate_up(i, False, (UT,) * 4)
                gate_up(KF // 2 - 1, False, DN_TILES)
                with dve.Fori(0, KD // 2 - 1) as i:
                    down(i, "same")
                down(KD // 2 - 1, ("next", "none")[f])

            def mixer_vec(L):
                shuffle = [p + 8 if p < 8 else p - 8 if p < 16 else p for p in range(32)]
                for kind, n in STEPS:
                    b = n % 2
                    if kind == "U":
                        if n == 0:
                            invert(L * 3 + 1)
                            nc.vector.tensor_tensor(cosr[:, :], const[:, C_COS:C_COS + TOK], rinv[:, :], ALU.mult)\
                                .then_inc(tabs_ready, 1)
                            nc.vector.tensor_tensor(sinr[:, :], const[:, C_SIN:C_SIN + TOK], rinv[:, :], ALU.mult)\
                                .then_inc(tabs_ready, 1)
                        if n in QK_UNITS:
                            k = QK_UNITS.index(n)
                            dve.wait_ge(zs_done, L * N_IN + n + 1)
                            if k >= 1:
                                dve.wait_ge(rope_done, L * 17 + k)
                            plain(dve)
                            nc.vector.stream_shuffle(sh[:, :], zs[:, b, :], shuffle).then_inc(shuf_done, 1)
                            dve.wait_ge(shuf_done, L * 17 + k + 1)
                            if k == 0:
                                dve.wait_ge(tabs_ready, L * 2 + 2)
                            nc.vector.tensor_tensor(sh[:, :], sh[:, :], sinr[:, :], ALU.mult).then_inc(shs_done, 1)
                            dve.wait_ge(shs_done, L * 17 + k + 1)
                            dve.wait_ge(t1_done, L * N_IN + n + 1)
                            nc.vector.tensor_tensor(qk[:, qk_slot(*COLS[n]), :], t1[:, b, :], sh[:, :], ALU.add)\
                                .then_inc(rope_done, 1)
                            if n in AQ_UNITS:
                                what, g, c = COLS[n]
                                dve.wait_ge(rope_done, L * 17 + k + 1)
                                if n == AQ_UNITS[0]:
                                    dve.wait_ge(qbd_zero, L + 1)
                                for hh in range(2):
                                    r = slice(HD * hh, HD * (hh + 1))
                                    mm = nc.vector.tensor_copy(qbd[r, g, c, hh, :], qk[r, qk_slot(what, g, c), SEQ:TOK])
                                mm.then_inc(qbd_done, 1)
                        rest_unit(L, U_IN + 4, 0, 0, n, UT if n + 4 < N_IN else BR_TILES)
                    elif kind == "G":
                        k = G_UNITS.index(n)
                        dve.wait_ge(gexp_done, L * 16 + k + 1)
                        nc.vector.tensor_scalar_add(gate[:, k, :], gate[:, k, :], 1.0).then_inc(gadd_done, 1)
                        dve.wait_ge(gadd_done, L * 16 + k + 1)
                        nc.vector.reciprocal(gate[:, k, :], gate[:, k, :]).then_inc(gate_ready, 1)
                    elif kind == "S":
                        what, h, t = ITEMS[n]
                        w, segs = segments(n)
                        dve.wait_ge(s_scores, L * NI + n + 1)
                        if n >= 2:
                            dve.wait_ge(s_pt, L * NI + n - 1)
                        plain(dve)
                        flat = ps[:, BK_S:BK_S + 2, :].rearrange("p b n -> p (b n)")
                        for j in range(segs):
                            to = e[:, b, j * w:(j + 1) * w]
                            src = ps[:, BK_S + j, 0:w] if segs == 2 else flat[:, 0:w]
                            if what == "B":
                                mask = const[:, C_MB + SEQ - w:C_MB + SEQ]
                            elif what == "A":
                                mask = const[:, C_MA:C_MA + NG * SEQ].rearrange("p (g k) -> p g k", g=NG)
                                mask = mask[:, :, SEQ - w // NG:SEQ]
                                to, src = (v.rearrange("p (g k) -> p g k", g=NG) for v in (to, src))
                            else:
                                c0 = C_SA if what == "SA" else C_SB
                                mask = const[:, c0:c0 + w]
                            mm = nc.vector.tensor_tensor_reduce(out=to, in0=src, in1=mask, scale=1.0, scalar=-3e38,
                                                                op0=ALU.add, op1=ALU.max,
                                                                accum_out=mx[:, b, j:j + 1])
                        mm.then_inc(s_max, 1)
                        dve.wait_ge(s_max, L * NI + n + 1)
                        nc.vector.tensor_scalar(nmx[:, b, 0:segs], mx[:, b, 0:segs], -SCALE, None, ALU.mult)\
                            .then_inc(s_masked, 1)
                    elif kind == "N":
                        w, segs = segments(n)
                        dve.wait_ge(s_exp, L * NI + n + 1)
                        if segs == 2:
                            nc.vector.tensor_tensor(den[:, b, :], den[:, b, :], esk[:, b, :], ALU.add)\
                                .then_inc(s_den, 1)
                            dve.wait_ge(s_den, L * 10 + n + 1)
                        nc.vector.reciprocal(rden[:, b, 0:segs], den[:, b, 0:segs]).then_inc(s_rden, 1)
                        dve.wait_ge(s_rden, L * NI + n + 1)
                        for j in range(segs):
                            part = e[:, b, j * w:(j + 1) * w]
                            mm = nc.vector.tensor_scalar(part, part, rden[:, b, j:j + 1], None, ALU.mult)
                        mm.then_inc(s_norm, 1)
                    elif kind == "W":
                        dve.wait_ge(s_ohi, L * NI + n + 1)
                        pairs = []
                        if ITEMS[n][0] == "SA":
                            pairs = [(out_halves(ITEMS[n][1], hh, olo), out_halves(ITEMS[n][1], hh, ohi)[0])
                                     for hh in range(2)]
                        else:
                            pairs = [(out_place(n, olo), out_place(n, ohi)[0])]
                        for (to, src), hi in pairs:
                            mm = nc.vector.tensor_tensor(to, src, hi.bitcast(F32), ALU.subtract)
                        mm.then_inc(s_olo, 1)
                for m in range(KD):
                    ba, bb = BK_BR[m % 2]
                    dve.wait_ge(unit_used, L * NU + U_BR + m + RING + 1)
                    dve.wait_ge(gate_ready, L * 16 + 2 * m + 2)
                    if m >= 2:
                        dve.wait_ge(mlo_done, L * KD + m - 1)
                    nc.vector.tensor_tensor(ma[:, m % 2, :], ps[:, ba, 0:TOK], gate[:, 2 * m, :], ALU.mult)
                    nc.vector.tensor_tensor(mb[:, m % 2, :], ps[:, bb, 0:TOK], gate[:, 2 * m + 1, :], ALU.mult)\
                        .then_inc(taken, 1)
                    rest_unit(L, U_BR + 4, 0, 0, m, BR_TILES if m < 4 else UT)
                for m in range(KD):
                    dve.wait_ge(unit_used, L * NU + U_WO + m + RING + 1)
                    add_to_x(L, BK_WO + m % 2, m, R_WO + m, 1.0)
                    scale_x(L * 3 + 2, m, m % 2)
                    rest_unit(L, U_WO + 4, 0, 0, m, UT)
                    rest_x(L * 3 + 2, m, m % 2)

            dve.sem_inc(wlo_done, RAW)
            dve.sem_inc(unit_used, RING)
            dve.sem_inc(taken, RING)
            dve.sem_inc(actlo_done, 2)
            nc.vector.memset(ones[:, :], 1.0).then_inc(set_up, 1)
            nc.vector.memset(eps[:, :], EPS).then_inc(set_up, 1)
            dve.wait_ge(start_in, 64)
            for m in range(KD):
                scale_x(0, m, m % 2)
                rest_x(0, m, m % 2)
            with dve.Fori(0, DEPTH) as L:
                for s in range(4):
                    rest_unit(L, 0, 0, 0, s, UT)
                ffn_vec(L, 0)
                mixer_vec(L)
                ffn_vec(L, 1)
            dve.wait_ge(xs_ready, (3 * DEPTH + 1) * KD)
            dve.wait_ge(ssq_done, (3 * DEPTH + 1) * (KD + 1))
            for m in range(KD):
                nc.vector.tensor_tensor(x[:, m, :], xhi[:, m, :].bitcast(F32), xlo[:, m, :].bitcast(F32), ALU.add)\
                    .then_inc(y_sum, 1)
            invert(3 * DEPTH)
            for m in range(KD):
                dve.wait_ge(y_sum, m + 1)
                nc.vector.tensor_tensor(x[:, m, :], x[:, m, :], rinv[:, :], ALU.mult).then_inc(y_done, 1)

        @block.gpsimd
        def _(pool):
            def chunk(t, m):
                return t[:, m, :] if isinstance(m, int) else t[:, at(m), :].rearrange("p o n -> p (o n)")

            def clear_squares(norm, first=False):
                if not first:
                    pool.wait_ge(rinv_ready, norm)
                    plain(pool)
                nc.gpsimd.memset(ssq[:, :], 0.0).then_inc(ssq_done, 1)

            def add_squares(norm, m):
                pool.wait_ge(ssq_done, norm * (KD + 1) + m + 1)
                nc.gpsimd.tensor_tensor(sq[:, :], chunk(x, m), chunk(x, m), ALU.mult).then_inc(sq_done, 1)
                pool.wait_ge(sq_done, norm * KD + m + 1)
                nc.gpsimd.tensor_tensor(ssq[:, :], ssq[:, :], sq[:, :], ALU.add).then_inc(ssq_done, 1)

            def ffn_pool(L, f):
                with pool.Fori(0, KF // 2) as i:
                    for q in range(2):
                        pool.wait_ge(silu_done, L * 2 * KF + i * 2 + f * KF + q + 1)
                        pool.wait_ge(taken, L * NR + i * 4 + R_GU[f] + 2 * q + 2 + RING)
                        nc.gpsimd.tensor_tensor(up_s[:, q, :], gate_s[:, q, :], up_s[:, q, :], ALU.mult)\
                            .then_inc(prod_done, 1)
                        pool.wait_ge(acthi_done, L * 2 * KF + i * 2 + f * KF + q + 1)
                        j = i * 2 + q
                        nc.gpsimd.tensor_tensor(chunk(act_lo, j), up_s[:, q, :], chunk(act_hi, j).bitcast(F32),
                                                ALU.subtract).then_inc(actlo_done, 1)
                norm = L * 3 + 1 + 2 * f
                clear_squares(norm)
                with pool.Fori(0, KD // 2) as i:
                    for o in range(2):
                        pool.wait_ge(taken, L * NR + i * 2 + R_DN[f] + o + RING + 1)
                        add_squares(norm, i * 2 + o)

            def mixer_pool(L):
                pool.wait_ge(unit_used, L * NU + RING + U_IN)
                plain(pool)
                nc.gpsimd.memset(qbd[:, :, :, :, :], 0.0).then_inc(qbd_zero, 1)
                pool.wait_ge(tabs_ready, L * 2 + 2)
                for kind, n in STEPS:
                    if kind != "U":
                        continue
                    what, g, c = COLS[n]
                    pool.wait_ge(zs_done, L * N_IN + n + 1)
                    if n >= 2:
                        before = COLS[n - 2][0]
                        if n - 2 in QK_UNITS:
                            pool.wait_ge(rope_done, L * 17 + QK_UNITS.index(n - 2) + 1)
                        elif before == "v":
                            pool.wait_ge(kvt_done, L * 14 + KV_UNITS.index(n - 2) + 1)
                        else:
                            pool.wait_ge(gexp_done, L * 16 + G_UNITS.index(n - 2) + 1)
                    by = cosr if what in "qk" else rinv
                    nc.gpsimd.tensor_tensor(t1[:, n % 2, :], zs[:, n % 2, :], by[:, :], ALU.mult).then_inc(t1_done, 1)
                norm = L * 3 + 2
                for m in range(KD):
                    pool.wait_ge(taken, L * NR + R_BR + m + RING + 1)
                    nc.gpsimd.tensor_tensor(ma[:, m % 2, :], ma[:, m % 2, :], mb[:, m % 2, :], ALU.add)\
                        .then_inc(mab_done, 1)
                    pool.wait_ge(mhi_done, L * KD + m + 1)
                    nc.gpsimd.tensor_tensor(mlo[:, m, :], ma[:, m % 2, :], mhi[:, m, :].bitcast(F32), ALU.subtract)\
                        .then_inc(mlo_done, 1)
                clear_squares(norm)
                for m in range(KD):
                    pool.wait_ge(taken, L * NR + R_WO + m + RING + 1)
                    add_squares(norm, m)

            pool.wait_ge(start_in, 64)
            clear_squares(0, True)
            for m in range(KD):
                add_squares(0, m)
            with pool.Fori(0, DEPTH) as L:
                ffn_pool(L, 0)
                mixer_pool(L)
                ffn_pool(L, 1)


def tiles_of(w, order=None):
    l, k, n = w.shape
    w = w.reshape(l, k // P, P, n // P, P).transpose(0, 3, 2, 1, 4).reshape(l, n // P, P, k)
    return np.ascontiguousarray(w if order is None else w[:, order]).reshape(-1, P, k)


def gqa_columns(w, axis):
    shape = list(w.shape)
    split = shape[:axis] + [2, 4, HD] + shape[axis + 1:]
    return w.reshape(split).swapaxes(axis, axis + 1).reshape(shape)


def lay_out(inputs):
    i = {k: np.asarray(v) for k, v in inputs.items()}
    tok = np.concatenate([i["x_prompt"].reshape(SEQ, D), i["x_sample"].reshape(NB * NT, D)])
    a = {"x": np.ascontiguousarray(tok.reshape(TOK, KD, P).transpose(2, 1, 0)), "const": constants()}
    norms = np.stack([i[k][l] for l in range(DEPTH) for k in ("norm_ffn1", "norm_mix", "norm_ffn2")] + [i["norm_final"]])
    a["gains"] = np.ascontiguousarray(norms.reshape(-1, KD, P).transpose(2, 0, 1))
    s = i["sinks"]
    rows = np.repeat(s.reshape(DEPTH, 2, 4), HALF, axis=2)
    a["sinks"] = np.ascontiguousarray(np.concatenate(
        [np.broadcast_to(s[None], (P, DEPTH, 8)), rows.transpose(2, 0, 1)], axis=2))
    for f in (1, 2):
        for k in ("gate", "up", "down"):
            a[f"ffn{f}_{k}"] = tiles_of(i[f"ffn{f}_{k}"])
    w = i["w_in"]
    ag = NG * 3 * 256
    bq = gqa_columns(w[:, :, ag:ag + 512], 2)
    parts = {("k", 3): w[:, :, ag + 512:ag + 640], ("v", 3): w[:, :, ag + 640:ag + 768], ("q", 3): bq,
             ("ga", 0): w[:, :, ag + 768:ag + 768 + D], ("gb", 0): w[:, :, ag + 768 + D:]}
    for g in range(NG):
        for n, k in enumerate("qkv"):
            c0 = (3 * g + n) * 256
            parts[(k, g)] = w[:, :, c0:c0 + 256]
    a["w_in"] = tiles_of(np.concatenate([parts[(k, g)][:, :, c * P:(c + 1) * P] for k, g, c in COLS], axis=2))
    a["w_branch"] = tiles_of(np.concatenate([i["w_branch_a"], gqa_columns(i["w_branch_b"], 1)], axis=1))
    a["w_out"] = tiles_of(i["w_out"])
    tiles = [i["cache_a1"]] + [i["cache_a2"][:, :, r::4] for r in range(4)] + [i["cache_a3"][:, :, r::16] for r in range(8)]
    kv = np.stack(tiles, axis=2).reshape(DEPTH, NB, CT, P, 2, 2, P)
    a["kcache"] = np.ascontiguousarray(kv[:, :, :, :, 0].transpose(0, 1, 4, 5, 2, 3)).reshape(-1, P, CT * P)
    a["vcache"] = np.ascontiguousarray(kv[:, :, :, :, 1].transpose(0, 1, 4, 3, 2, 5)).reshape(-1, P, CT * P)
    b = i["cache_b"].reshape(DEPTH, NB, P, 2, P)
    a["kcache_b"] = np.ascontiguousarray(b[:, :, :, 0].transpose(0, 3, 1, 2))
    a["vcache_b"] = np.ascontiguousarray(b[:, :, :, 1].transpose(0, 2, 1, 3))
    for k in ("a1", "a2", "a3", "b"):
        a[f"cache_{k}"] = i[f"cache_{k}"]
    return a


_OUTS = {"y": (P, KD, TOK)}
for _n, _w, _h in (("a1", 128, 4), ("a2", 512, 4), ("a3", 2048, 4), ("b", 128, 2)):
    _OUTS[f"new_{_n}_prompt"] = (DEPTH, 1, min(_w, SEQ), 2, _h, HD)
    _OUTS[f"new_{_n}_sample"] = (DEPTH, NB, _w, 2, _h, HD)


def kernel(**inputs):
    import concourse.bacc as _bacc
    from concourse.bass_utils import run_bass_kernel_spmd as _run

    arrays = lay_out(inputs)
    nc = _bacc.Bacc("TRN2", target_bir_lowering=False, num_devices=1, dynamic_dma_scratch_size=1024)
    aps = {n: nc.dram_tensor(f"in_{n}", v.shape, mybir.dt.from_np(v.dtype), kind="ExternalInput").ap() for n, v in arrays.items()}
    for n, shape in _OUTS.items():
        aps[n] = nc.dram_tensor(f"out_{n}", shape, F32, kind="ExternalOutput").ap()
    build(nc, aps)
    got = _run(nc, [{f"in_{n}": v for n, v in arrays.items()}], core_ids=[0]).results[0]
    y = got["out_y"].transpose(2, 1, 0).reshape(TOK, D)
    return (np.ascontiguousarray(y[:SEQ]).reshape(1, SEQ, D), np.ascontiguousarray(y[SEQ:]).reshape(NB, NT, D),
            *(got[f"out_new_{n}_{k}"] for k in ("prompt", "sample") for n in ("a1", "a2", "a3", "b")))
```

```python
from contextlib import ExitStack

import numpy as np

import concourse.bass as bass
from concourse import mybir

F32 = mybir.dt.float32
F32R = mybir.dt.float32r
ALU = mybir.AluOpType
ACT = mybir.ActivationFunctionType

P = 128
DEPTH = 2
D = 1024
SEQ = 256
NB, NT = 8, 8
TOK = SEQ + NB * NT
HD = 64
KD = D // P
F = ((8 * D // 3 + 127) // 128) * 128
KF = F // P
DILS = ((128, 1), (512, 4), (2048, 16))
NG = len(DILS)
SCALE = HD ** -0.5
EPS = 1e-6
NEG = -1e30
HALF = 32
CT = 13
WIN = 128

UT = 8
RAW = 2
RING = 4
DN_TILES = (6, 5, 6, 5)
DN_K0 = (0, 6, 11, 17)
BR_TILES = 6
N_IN = 40
U_GU = (0, 132)
U_DN = (44, 176)
U_IN, U_BR, U_WO = 76, 116, 124
NU = 208
R_GU, R_DN = (0, 68), (44, 112)
R_BR, R_WO = 52, 60
NR = 120

COLS = [("k", 3, 0), ("v", 3, 0)] + [("q", 3, c) for c in range(4)]
for _g in range(NG):
    COLS += [(_k, _g, _c) for _k in "qkv" for _c in range(2)]
COLS += [(_k, 0, _m) for _m in range(KD) for _k in ("ga", "gb")]
assert len(COLS) == N_IN
KV_UNITS = [u for u, c in enumerate(COLS) if c[0] in "kv"]
K_UNITS = [u for u in KV_UNITS if COLS[u][0] == "k"]
QK_UNITS = [u for u, c in enumerate(COLS) if c[0] in "qk"]
G_UNITS = [u for u, c in enumerate(COLS) if c[0] in ("ga", "gb")]


def qk_slot(kind, g, c):
    if g == 3:
        return 0 if kind == "k" else 1 + c
    return (5 if kind == "q" else 11) + 2 * g + c


def v_slot(g, c):
    return 6 if g == 3 else 2 * g + c


ITEMS = [("B", c, t) for c in range(4) for t in range(2)] + [("SB", h, 0) for h in range(2)]
ITEMS += [("A", h, t) for h in range(4) for t in range(2)] + [("SA", h, 0) for h in range(2)]
NI = len(ITEMS)
NSC = NI - 2
KV_RING = 3
N_KV = 1 + 4 * CT
K_FULL = (0, CT, CT + 1)
N_QM = CT + 2


K_BEATS = {10: (0, 4), 11: (4, 8), 12: (8, 13), 13: (13, 16), 14: (16, 19), 15: (19, 22), 16: (22, 26)}


def mixer_steps():
    steps, nxt = [], [0]

    def unit():
        u = nxt[0]
        nxt[0] += 1
        steps.append(("U", u))
        if u >= 1:
            if u - 1 in KV_UNITS:
                steps.append(("R", u - 1))
            if u - 1 in G_UNITS:
                steps.append(("G", u - 1))

    for _ in range(7):
        unit()
    for p in range(NI + 2):
        if p == 10:
            while nxt[0] < 25:
                unit()
            steps.append(("Q", 0))
        if p < NI:
            steps.append(("S", p))
        if 1 <= p <= NI:
            steps.append(("N", p - 1))
        if p < 10:
            unit()
            if p < 7:
                unit()
        elif p < NI + 1 and nxt[0] < N_IN:
            unit()
        if p in K_BEATS:
            steps += [("K", 1 + n) for n in range(*K_BEATS[p])]
            if p == 12:
                steps += [("E", 1), ("Q", 1)]
        if 1 <= p <= NI - 1:
            steps.append(("T", p - 1))
        if p == 6:
            steps += [("KB", 0), ("E", 0)]
        if 2 <= p:
            i = p - 2
            steps.append(("O", i))
            if ITEMS[i][0] == "SA":
                h = ITEMS[i][1]
                for n in range(CT):
                    steps.append(("V", 1 + (2 + h) * CT + n))
                    if n in (4, 9) and nxt[0] < N_IN:
                        unit()
                steps.append(("Y", i))
                if h == 0:
                    steps.append(("T", i + 1))
                if nxt[0] < N_IN:
                    unit()
                steps.append(("X", i))
            steps.append(("W", i))
    while nxt[0] < N_IN:
        unit()
    steps.append(("G", N_IN - 1))
    return steps


STEPS = mixer_steps()


def cache_load_places():
    at, last = {0: 19}, 0
    for kind, n in STEPS:
        if kind == "U":
            last = n
        if kind in ("K", "V"):
            at[n] = last
    return [12, 14, 15] + [min(at[n - KV_RING] + 6, 55) for n in range(KV_RING, N_KV)]


KV_PLACE = cache_load_places()

C_COS, C_SIN = 0, TOK
C_MA = 2 * TOK
C_MB = C_MA + NG * SEQ
C_SA = C_MB + SEQ
N_SA = NG * (P + HALF)
C_SB = C_SA + N_SA
N_SB = P + HALF
C_ID = C_SB + N_SB
N_C = C_ID + P


def constants():
    c = np.zeros((P, N_C), np.float32)
    rot = HD // 4
    half = rot // 2
    inv = np.float32(500000.0) ** (-(np.arange(half, dtype=np.float32) * np.float32(2.0) / np.float32(rot)))
    pos = np.concatenate([np.arange(SEQ), np.tile(2048 + np.arange(NT), NB)]).astype(np.float32)
    ang = (inv[:, None] * pos[None, :]).astype(np.float32)
    c[:, C_COS:C_COS + TOK] = 1.0
    for base in (0, HD):
        for part, sign in ((0, -1.0), (half, 1.0)):
            c[base + part:base + part + half, C_COS:C_COS + TOK] = np.cos(ang)
            c[base + part:base + part + half, C_SIN:C_SIN + TOK] = sign * np.sin(ang)
    dist = (P + np.arange(P))[:, None] - np.arange(SEQ)[None, :]
    for g, (win, dil) in enumerate(DILS):
        ok = (dist >= 0) & (dist <= win) & (dist % dil == 0)
        c[:, C_MA + g * SEQ:C_MA + (g + 1) * SEQ] = np.where(ok, 0, NEG)
    c[:, C_MB:C_MB + SEQ] = np.where((dist >= 0) & (dist < WIN), 0, NEG)
    b, t = (np.arange(P) // HALF)[:, None], (np.arange(P) % NT)[:, None]
    r = np.arange(P)[None, :]
    nb, s = (np.arange(HALF) // NT)[None, :], (np.arange(HALF) % NT)[None, :]
    for g, (win, dil) in enumerate(DILS):
        row = r if g == 0 else t % dil + dil * r
        ok = (row >= t) & (row <= win + t)
        c[:, C_SA + g * P:C_SA + (g + 1) * P] = np.where(ok, 0, NEG)
        ok = (nb == b) & (s <= t) & ((t - s) % dil == 0)
        o = C_SA + NG * P + g * HALF
        c[:, o:o + HALF] = np.where(ok, 0, NEG)
    b = (np.arange(P) // NT % 4)[:, None]
    c[:, C_SB:C_SB + P] = np.where(r > t, 0, NEG)
    c[:, C_SB + P:C_SB + N_SB] = np.where((nb == b) & (s <= t), 0, NEG)
    c[:, C_ID:C_ID + P] = np.eye(P, dtype=np.float32)
    return c


BK_KV = 2
BK_S = 3
BK_T = 5
BK_O = 7
BK_DN = 4
BK_WO = 5
BK_BR = ((0, 1), (3, 4))


def build(nc, a):
    ctx = ExitStack()
    with ctx:
        def sb(name, shape, dt=F32, where=ctx):
            return where.enter_context(nc.sbuf_tensor(name, shape, dt))

        def sem(name):
            return ctx.enter_context(nc.semaphore(name))

        const = sb("const", [P, N_C])
        ones = sb("ones", [P, P])
        eps = sb("eps", [P, 1])
        gains = sb("gains", [P, 3 * DEPTH + 1, KD])
        sinks = sb("sinks", [P, DEPTH, 10])
        x = sb("x", [P, KD, TOK])
        xg = sb("xg", [P, 2, TOK])
        xhi = sb("xhi", [P, KD, TOK], F32R)
        xlo = sb("xlo", [P, KD, TOK], F32R)
        sq = sb("sq", [P, TOK])
        ssq = sb("ssq", [P, TOK])
        rms = sb("rms", [P, TOK])
        rinv = sb("rinv", [P, TOK])
        raw = sb("raw", [P, RAW, UT * P])
        whi = sb("whi", [P, RING, UT * P], F32R)
        wlo = sb("wlo", [P, RING, UT * P], F32R)

        with ExitStack() as ffn:
            act_hi = sb("act_hi", [P, KF, TOK], F32R, ffn)
            act_lo = sb("act_lo", [P, KF, TOK], F32R, ffn)
            gate_s = sb("gate_s", [P, 2, TOK], F32, ffn)
            up_s = sb("up_s", [P, 2, TOK], F32, ffn)
        gate = sb("gate", [P, 2 * KD, TOK])
        ohi = sb("ohi", [P, BR_TILES, TOK], F32R)
        olo = sb("olo", [P, BR_TILES, TOK], F32R)
        with ExitStack() as att:
            kvc = sb("kvc", [P, KV_RING, NB * P], F32, att)
            vb = sb("vb", [P, NB, P], F32, att)
            qk = sb("qk", [P, 17, TOK], F32, att)
            vtok = sb("vtok", [P, 2, 7 * P], F32, att)
            vnew = sb("vnew", [HALF, 2, 7 * P], F32, att)
            kst = sb("kst", [P, 2, 4 * P], F32, att)
            qm = sb("qm", [P, 4, N_QM, 3 * 2 * NT], F32, att)
            e = sb("e", [P, 2, NG * SEQ], F32, att)
            pt_mem = sb("pt_mem", [P, 4 * CT * HALF], F32, att)
            ptn = sb("ptn", [HALF, 2, NG * P], F32, att)
            sts = sb("sts", [P, 4 * P], F32, att)
            osb = sb("osb", [P, 2 * P], F32, att)
            zs = sb("zs", [P, 2, TOK], F32, att)
            t1 = sb("t1", [P, 2, TOK], F32, att)
            sh = sb("sh", [P, TOK], F32, att)
            cosr = sb("cosr", [P, TOK], F32, att)
            sinr = sb("sinr", [P, TOK], F32, att)
            mx = sb("mx", [P, 2, 2], F32, att)
            nmx = sb("nmx", [P, 2, 2], F32, att)
            den = sb("den", [P, 2, 2], F32, att)
            esk = sb("esk", [P, 2, 2], F32, att)
            rden = sb("rden", [P, 2, 2], F32, att)
        with ExitStack() as out_mem:
            mhi = sb("mhi", [P, KD, TOK], F32R, out_mem)
            mlo = sb("mlo", [P, KD, TOK], F32R, out_mem)
            ma = sb("ma", [P, 2, TOK], F32, out_mem)
            mb = sb("mb", [P, 2, TOK], F32, out_mem)
        pts = pt_mem[:, 0:2 * NG * SEQ].rearrange("p (s n) -> p s n", s=2)
        pm = pt_mem[:, :].rearrange("p (b i n) -> p b i n", b=4, i=CT)
        stb = sts[:, :].rearrange("p (j n) -> p j n", j=2)
        ps = ctx.enter_context(nc.psum_tensor("ps", [P, 8, 512], F32))

        passed = sem("passed")
        start_in = sem("start_in")
        set_up = sem("set_up")
        raw_in = [sem(f"raw_in{s}") for s in range(RAW)]
        whi_done = sem("whi_done")
        wlo_done = sem("wlo_done")
        unit_used = sem("unit_used")
        taken = sem("taken")
        silu_done = sem("silu_done")
        prod_done = sem("prod_done")
        acthi_done = sem("acthi_done")
        actlo_done = sem("actlo_done")
        xg_ready = sem("xg_ready")
        xhi_done = sem("xhi_done")
        xs_ready = sem("xs_ready")
        sq_done = sem("sq_done")
        ssq_done = sem("ssq_done")
        ms_ready = sem("ms_ready")
        rms_done = sem("rms_done")
        rinv_ready = sem("rinv_ready")
        tabs_ready = sem("tabs_ready")
        zs_done = sem("zs_done")
        t1_done = sem("t1_done")
        shuf_done = sem("shuf_done")
        shs_done = sem("shs_done")
        rope_done = sem("rope_done")
        qm_zero = sem("qm_zero")
        qm_done = sem("qm_done")
        pm_zero = sem("pm_zero")
        kvt_done = sem("kvt_done")
        kvtok_done = sem("kvtok_done")
        kst_out = [sem(f"kst_out{s}") for s in range(2)]
        v_out = sem("v_out")
        gexp_done = sem("gexp_done")
        gadd_done = sem("gadd_done")
        gate_ready = sem("gate_ready")
        vb_in = sem("vb_in")
        kvc_in = [sem(f"kvc_in{s}") for s in range(KV_RING)]
        kvc_used = sem("kvc_used")
        sts_done = sem("sts_done")
        osb_done = sem("osb_done")
        s_scores = sem("s_scores")
        s_max = sem("s_max")
        s_masked = sem("s_masked")
        s_exp = sem("s_exp")
        s_den = sem("s_den")
        s_rden = sem("s_rden")
        s_norm = sem("s_norm")
        s_pt = sem("s_pt")
        s_pts = sem("s_pts")
        s_pv = sem("s_pv")
        s_ohi = sem("s_ohi")
        s_olo = sem("s_olo")
        mab_done = sem("mab_done")
        mhi_done = sem("mhi_done")
        mlo_done = sem("mlo_done")
        y_sum = sem("y_sum")
        y_done = sem("y_done")
        copy_out = sem("copy_out")
        y_out = sem("y_out")

        block = ctx.enter_context(nc.Block())
        ident = const[:, C_ID:C_ID + P]

        def at(v):
            return bass.ds(v, 1)

        def plain(eng):
            eng.sem_inc(passed, 1)

        def segments(i):
            kind, _, t = ITEMS[i]
            return {"B": (P * (t + 1), 2), "A": (NG * P * (t + 1), 1), "SB": (N_SB, 2), "SA": (N_SA, 1)}[kind]

        def out_place(i, o):
            kind, h, t = ITEMS[i]
            if kind == "B":
                return o[:, 2 + h, t * P:(t + 1) * P], ps[:, BK_O, 0:P]
            if kind == "A":
                r = slice(HD * (h % 2), HD * (h % 2 + 1))
                return o[r, h // 2, t * P:(t + 1) * P], ps[r, BK_O, 0:P]
            s0 = SEQ + HALF * h
            return o[:, 2:6, s0:s0 + HALF], ps[:, BK_O, 0:P].rearrange("p (c n) -> p c n", c=4)

        def out_halves(half, hh, o):
            r = slice(HD * hh, HD * (hh + 1))
            s0 = SEQ + HALF * half
            src = ps[r, BK_KV, 0:2 * (P + 2 * NT)].rearrange("p (c n) -> p c n", c=2)[:, :, 0:P]
            src = src.rearrange("p c (b x) -> p c b x", b=4)[:, :, :, NT * hh:NT * (hh + 1)]
            return o[r, 0:2, s0:s0 + HALF].rearrange("p c (b n) -> p c b n", b=4), src

        def kvc_wait(eng, L, n):
            s = n % KV_RING
            per_layer = (N_KV - s + KV_RING - 1) // KV_RING
            eng.wait_ge(kvc_in[s], (L * per_layer + n // KV_RING + 1) * 16)

        def strided(ap, offset, dims):
            return bass.AP(tensor=ap.tensor, offset=ap.offset + offset, ap=[list(ap.ap[0])] + [list(d) for d in dims])

        @block.sync
        def _(sp):
            sp.dma_start(x[:, :, :], a["x"]).then_inc(start_in, 16)
            sp.dma_start(gains[:, :, :], a["gains"]).then_inc(start_in, 16)
            sp.dma_start(sinks[:, :, :], a["sinks"]).then_inc(start_in, 16)
            sp.dma_start(const[:, :], a["const"]).then_inc(start_in, 16)

            kpre, vpre = a["kcache"], a["vcache"]
            big = a["cache_a3"][:, :, NT:, :, :, :].rearrange(
                "l b w v h d -> l b (w v h d)").rearrange("l b (f k n) -> l b f k n", f=2, k=P)
            big_o = a["new_a3_sample"][:, :, :DILS[2][0] - NT, :, :, :].rearrange(
                "l b w v h d -> l b (w v h d)").rearrange("l b (f k n) -> l b f k n", f=2, k=P)
            mid = a["cache_a2"][:, :, NT:, :, :, :].rearrange(
                "l b w v h d -> l b (w v h d)").rearrange("l b (k n) -> l b k n", k=P)
            mid_o = a["new_a2_sample"][:, :, :DILS[1][0] - NT, :, :, :].rearrange(
                "l b w v h d -> l b (w v h d)").rearrange("l b (k n) -> l b k n", k=P)

            def load_at(L, base, i, step, s, src, tiles):
                sp.wait_ge(wlo_done, L * NU + i * step + base + s + 1)
                sp.dma_start(raw[:, (base + s) % RAW, 0:tiles * P], src).then_inc(raw_in[(base + s) % RAW], 16)

            def one(ap):
                return ap.rearrange("o p n -> (o p) n")

            def ffn_loads(L, f):
                wg, wu, wd = (a[f"ffn{f + 1}_{k}"] for k in ("gate", "up", "down"))

                def group(i):
                    for s in range(4):
                        w = (wg, wu)[s % 2]
                        load_at(L, U_GU[f], i, 4, s, one(w[at(L * KF + 2 * i + s // 2), :, :]), UT)

                with sp.Fori(0, NB) as i:
                    group(i)
                    sp.dma_start(one(big_o[at(L), at(i), f, :, :].rearrange("l b k n -> (l b) k n")),
                                 one(big[at(L), at(i), f, :, :].rearrange("l b k n -> (l b) k n")))\
                        .then_inc(copy_out, 16)
                with sp.Fori(NB, KF // 2) as i:
                    group(i)
                with sp.Fori(0, KD // 2) as i:
                    for o in range(2):
                        for s in range(4):
                            k0, n = DN_K0[s] * P, DN_TILES[s]
                            load_at(L, U_DN[f], i, 8, 4 * o + s,
                                    one(wd[at(L * KD + 2 * i + o), :, k0:k0 + n * P]), n)
                    sp.dma_start(one(mid_o[at(L), at(i + 4 * f), :, :].rearrange("l b k n -> (l b) k n")),
                                 one(mid[at(L), at(i + 4 * f), :, :].rearrange("l b k n -> (l b) k n")))\
                        .then_inc(copy_out, 16)

            def store_kv(L, n):
                kind, g, c = COLS[KV_UNITS[n]]
                name = ("a1", "a2", "a3", "b")[g]
                kv = 0 if kind == "k" else 1
                heads = P * c
                sp.wait_ge(kvtok_done, L * 14 + n + 1)
                if kind == "k":
                    nk = K_UNITS.index(KV_UNITS[n])
                    src, new, done = kst[:, nk % 2, 0:2 * P], kst[0:HALF, nk % 2, 2 * P:4 * P], kst_out[nk % 2]
                    src = src.rearrange("p (t f) -> p t f", t=2)
                    new = new.rearrange("p (t f) -> p t f", t=2)
                else:
                    src, new, done = (v[:, :, v_slot(g, c) * P:(v_slot(g, c) + 1) * P] for v in (vtok, vnew)), None, v_out
                    src, new = tuple(src)
                t0 = 0 if g in (1, 2) else 1
                dst = a[f"new_{name}_prompt"].rearrange("l n (t p) v h d -> l p (n t) v (h d)", p=P)
                dst = dst[at(L), :, :, kv, heads:heads + P].rearrange("l p t f -> (l p) t f")
                sp.dma_start(dst, src[:, t0:2, :]).then_inc(done, 16)
                dst = a[f"new_{name}_sample"]
                w = dst.shape[2]
                dst = dst[:, :, w - NT:w, :, :, :].rearrange("l b t v h d -> l b t v (h d)")
                for half in range(2):
                    to = dst[at(L), 4 * half:4 * half + 4, :, kv, heads:heads + P].rearrange("l b t f -> (l b) t f")
                    sp.dma_start(to, new[:, half, :]).then_inc(done, 16)

            def mixer_loads(L):
                w_in, w_br, w_out = a["w_in"], a["w_branch"], a["w_out"]
                for v in range(N_IN + 2 * KD):
                    if v < N_IN:
                        load_at(L, U_IN, 0, 0, v, one(w_in[at(L * N_IN + v), :, :]), UT)
                    elif v < N_IN + KD:
                        load_at(L, U_IN, 0, 0, v, one(w_br[at(L * KD + v - N_IN), :, :]), BR_TILES)
                    else:
                        load_at(L, U_IN, 0, 0, v, one(w_out[at(L * KD + v - N_IN - KD), :, :]), UT)
                    if v == 12:
                        sp.wait_ge(unit_used, L * NU + RING + U_IN)
                        sp.dma_start(vb[:, :, :], vpre_b(L)).then_inc(vb_in, 16)
                    for n in range(N_KV):
                        if KV_PLACE[n] == v:
                            if n == 0:
                                src = a["kcache_b"][at(L), :, :]
                            elif n <= 2 * CT:
                                src = kpre[at(L * 2 * CT + n - 1), :, :]
                            else:
                                src = vpre[at(L * 2 * CT + n - 1 - 2 * CT), :, :]
                            if n >= KV_RING:
                                sp.wait_ge(kvc_used, L * N_KV + n - KV_RING + 1)
                            sp.dma_start(kvc[:, n % KV_RING, :], one(src)).then_inc(kvc_in[n % KV_RING], 16)
                    for n, u in enumerate(KV_UNITS):
                        if u + 8 == v:
                            store_kv(L, n)
                    if v == N_IN + KD:
                        for name, g in (("a1", 0), ("b", 3)):
                            src = a[f"cache_{name}"][:, :, NT:, :, :, :].rearrange(
                                "l b w v h d -> l b (w v h d)").rearrange("l b (k n) -> l k b n", k=P)
                            to = a[f"new_{name}_sample"][:, :, :P - NT, :, :, :].rearrange(
                                "l b w v h d -> l b (w v h d)").rearrange("l b (k n) -> l k b n", k=P)
                            sp.dma_start(to[at(L), :, :, :].rearrange("l k b n -> (l k) b n"),
                                         src[at(L), :, :, :].rearrange("l k b n -> (l k) b n"))\
                                .then_inc(copy_out, 16)
                sp.wait_ge(v_out, (L + 1) * (7 * 48))
                plain(sp)
                sp.wait_ge(kst_out[0], (L + 1) * (4 * 48))
                plain(sp)
                sp.wait_ge(kst_out[1], (L + 1) * (3 * 48))
                plain(sp)

            def vpre_b(L):
                return a["vcache_b"][at(L), :, :, :].rearrange("l p b f -> (l p) b f")

            with sp.Fori(0, DEPTH) as L:
                ffn_loads(L, 0)
                mixer_loads(L)
                ffn_loads(L, 1)
            sp.wait_ge(y_done, KD)
            sp.dma_start(a["y"], x[:, :, :]).then_inc(y_out, 16)
            sp.wait_ge(y_out, 16)
            sp.wait_ge(copy_out, 16 * DEPTH * (2 * NB + KD + 2))
            sp.wait_ge(v_out, DEPTH * 7 * 48)
            sp.wait_ge(kst_out[0], DEPTH * 4 * 48)
            sp.wait_ge(kst_out[1], DEPTH * 3 * 48)

        @block.tensor
        def _(pe):
            def product(out, slot, tile, hi, lo, first, last):
                w0, w1 = (w[:, slot, tile * P:(tile + 1) * P] for w in (whi, wlo))
                pe.matmul(out, w0, hi, start=first, stop=False)
                pe.matmul(out, w0, lo, start=False, stop=False)
                return pe.matmul(out, w1, hi, start=False, stop=last)

            def sum_squares(n):
                pe.wait_ge(ssq_done, (n + 1) * (KD + 1))
                pe.matmul(ps[:, BK_O, 0:TOK], ones[:, :], ssq[:, :], start=True, stop=True).then_inc(ms_ready, 1)

            def ffn_products(L, f):
                def gate_up(i, first):
                    for s in range(4):
                        pe.wait_ge(wlo_done, L * NU + i * 4 + U_GU[f] + s + RAW + 1)
                        pe.wait_ge(taken, L * NR + i * 4 + R_GU[f] + s + 1)
                        for k in range(KD):
                            if first and s == 0:
                                pe.wait_ge(xs_ready, (L * 3 + 2 * f) * KD + k + 1)
                            mm = product(ps[:, s, 0:TOK], s, k, xhi[:, k, :], xlo[:, k, :], k == 0, k == KD - 1)
                        mm.then_inc(unit_used, 1)
                        if first and s == 0:
                            sum_squares(L * 3 + 2 * f)

                def down(i, first):
                    for o in range(2):
                        pe.wait_ge(taken, L * NR + i * 2 + R_DN[f] + o + RING - 1)
                        for s in range(4):
                            pe.wait_ge(wlo_done, L * NU + i * 8 + U_DN[f] + 4 * o + s + RAW + 1)
                            for n in range(DN_TILES[s]):
                                k = DN_K0[s] + n
                                if first and o == 0:
                                    pe.wait_ge(actlo_done, L * 2 * KF + f * KF + 2 + k + 1)
                                mm = product(ps[:, BK_DN + o, 0:TOK], s, n, act_hi[:, k, :], act_lo[:, k, :],
                                             k == 0, k == KF - 1)
                            mm.then_inc(unit_used, 1)

                gate_up(0, True)
                with pe.Fori(1, KF // 2) as i:
                    gate_up(i, False)
                down(0, True)
                with pe.Fori(1, KD // 2) as i:
                    down(i, False)

            def mixer_products(L):
                def scores(i):
                    kind, h, t = ITEMS[i]
                    if i >= 1:
                        pe.wait_ge(s_masked, L * NI + i)
                    if kind == "B":
                        if i == 0:
                            pe.wait_ge(rope_done, L * 17 + 5)
                        n = P * (t + 1)
                        for j in range(2):
                            r = slice(HD * j, HD * (j + 1))
                            mm = pe.matmul(ps[:, BK_S + j, 0:n], qk[r, 1 + h, t * P:(t + 1) * P], qk[r, 0, 0:n],
                                           start=True, stop=True)
                    elif kind == "A":
                        pe.wait_ge(rope_done, L * 17 + 17)
                        n = P * (t + 1)
                        r = slice(HD * (h % 2), HD * (h % 2 + 1))
                        for g in range(NG):
                            bank, col = divmod(g * n, 512)
                            mm = pe.matmul(ps[:, BK_S + bank, col:col + n],
                                           qk[r, qk_slot("q", g, h // 2), t * P:(t + 1) * P],
                                           qk[r, qk_slot("k", g, h // 2), 0:n], start=True, stop=True)
                    else:
                        pe.wait_ge(sts_done, L * 2 + 1)
                        new = slice(SEQ + HALF * h, SEQ + HALF * (h + 1))
                        for j in range(2):
                            pe.transpose(ps[:, BK_S + j, 0:P], stb[:, j, h * P:(h + 1) * P], ident)
                            r = slice(HD * j, HD * (j + 1))
                            for c in range(4):
                                mm = pe.matmul(ps[HALF * c:HALF * (c + 1), BK_S + j, P:P + HALF],
                                               qk[r, 1 + c, new], qk[r, 0, new], start=True, stop=True)
                    mm.then_inc(s_scores, 1)

                def transposes(i):
                    kind, h, t = ITEMS[i]
                    pe.wait_ge(s_norm, L * NI + i + 1)
                    if i >= 1:
                        pe.wait_ge(s_pts, L * NI + i)
                    if i == 6:
                        pe.wait_ge(sts_done, L * 2 + 1)
                    eb = e[:, i % 2, :]
                    if kind in ("A", "B"):
                        for n in range((NG if kind == "A" else 2) * (t + 1)):
                            mm = pe.transpose(ps[:, BK_T + n // 4, n % 4 * P:(n % 4 + 1) * P],
                                              eb[:, n * P:(n + 1) * P], ident)
                    else:
                        for n in range(2 if kind == "SB" else NG):
                            o = n * N_SB if kind == "SB" else n * P
                            on = n * N_SB + P if kind == "SB" else NG * P + n * HALF
                            pe.transpose(ps[:, BK_T, n * P:(n + 1) * P], eb[:, o:o + P], ident)
                            mm = pe.transpose(ps[0:HALF, BK_T + 1, n * P:(n + 1) * P], eb[:, on:on + HALF], ident)
                    mm.then_inc(s_pt, 1)

                def values(i):
                    kind, h, t = ITEMS[i]
                    pe.wait_ge(s_pts, L * NI + i + 1)
                    if i >= 1:
                        pe.wait_ge(s_olo, L * NI + i)
                    pb, nb = pts[:, i % 2, :], ptn[:, i % 2, :]
                    if kind == "B":
                        pe.wait_ge(kvtok_done, L * 14 + 2)
                        for j in range(2):
                            for kt in range(t + 1):
                                n = j * (t + 1) + kt
                                mm = pe.matmul(ps[HD * j:HD * (j + 1), BK_O, 0:P],
                                               vtok[:, kt, 6 * P + HD * j:6 * P + HD * (j + 1)],
                                               pb[:, n * P:(n + 1) * P], start=kt == 0, stop=kt == t)
                        mm.then_inc(s_pv, 1)
                    elif kind == "A":
                        pe.wait_ge(kvtok_done, L * 14 + 14)
                        for g in range(NG):
                            for kt in range(t + 1):
                                n = g * (t + 1) + kt
                                f0 = v_slot(g, h // 2) * P + HD * (h % 2)
                                mm = pe.matmul(ps[HD * (h % 2):HD * (h % 2 + 1), BK_O, 0:P],
                                               vtok[:, kt, f0:f0 + HD], pb[:, n * P:(n + 1) * P],
                                               start=n == 0, stop=n == NG * (t + 1) - 1)
                        mm.then_inc(s_pv, 1)
                    elif kind == "SB":
                        pe.wait_ge(vb_in, L * 16 + 16)
                        for j in range(2):
                            r = slice(HD * j, HD * (j + 1))
                            pe.matmul(ps[r, BK_O, 0:P], vnew[:, h, 6 * P + HD * j:6 * P + HD * (j + 1)],
                                      nb[:, j * P:(j + 1) * P], start=True, stop=False)
                            for b in range(4):
                                cols = pb[:, j * P:(j + 1) * P].rearrange("p (c n) -> p c n", c=4)[:, :, NT * b:NT * (b + 1)]
                                to = ps[r, BK_O, 0:P].rearrange("p (c n) -> p c n", c=4)[:, :, NT * b:NT * (b + 1)]
                                mm = pe.matmul(to, vb[:, 4 * h + b, r], cols, start=False, stop=b == 3)
                        mm.then_inc(s_pv, 1)
                    else:
                        if h == 1:
                            pe.wait_ge(osb_done, L * 2 + 1)
                        plain(pe)
                        for g in range(NG):
                            for b in range(4):
                                pe.matmul(ps[HALF * b:HALF * (b + 1), BK_O, 0:2 * P],
                                          nb[:, g * P + HALF * b:g * P + HALF * (b + 1)],
                                          vnew[:, h, v_slot(g, 0) * P:(v_slot(g, 0) + 2) * P],
                                          start=g == 0, stop=False, skip_group_check=True)

                def cached_keys(n):
                    half, i = divmod(n - 1, CT)
                    g = 0 if i == 0 else 1 if i < 5 else 2

                    def q(b, j, c):
                        return qm[:, b, j, 2 * NT * c:2 * NT * c + HALF]

                    kvc_wait(pe, L, n)
                    if i == 0:
                        pe.wait_ge(qm_done, L * 2 + half + 1)
                        if half == 0:
                            pe.wait_ge(kvtok_done, L * 14 + 14)
                        else:
                            pe.wait_ge(sts_done, L * 2 + 2)
                    new = slice(SEQ + HALF * half, SEQ + HALF * (half + 1))
                    if i == CT - 1:
                        for gn in range(NG):
                            for c in range(2):
                                for b in range(4):
                                    pe.matmul(ps[HALF * b:HALF * (b + 1), BK_KV,
                                                 NG * P + gn * HALF:NG * P + (gn + 1) * HALF],
                                              q(b, K_FULL[gn], c), qk[:, qk_slot("k", gn, c), new],
                                              start=False, stop=False, skip_group_check=True)
                    for c in range(2):
                        for b in range(4):
                            mm = pe.matmul(ps[HALF * b:HALF * (b + 1), BK_KV, g * P:(g + 1) * P], q(b, i, c),
                                           kvc[:, n % KV_RING, (4 * c + b) * P:(4 * c + b + 1) * P],
                                           start=i == 0 and c == 0, stop=i == CT - 1 and c == 1,
                                           skip_group_check=True)
                    mm.then_inc(kvc_used, 1)

                def cached_values(n):
                    half, i = divmod(n - 1 - 2 * CT, CT)
                    kvc_wait(pe, L, n)
                    for b in range(4):
                        mm = pe.matmul(ps[HALF * b:HALF * (b + 1), BK_O, 0:2 * P], pm[:, b, i, :],
                                       kvc[:, n % KV_RING, 2 * P * b:2 * P * (b + 1)],
                                       start=False, stop=i == CT - 1, skip_group_check=True)
                    mm.then_inc(kvc_used, 1)

                def output_rows(i):
                    half = ITEMS[i][1]
                    pe.wait_ge(osb_done, L * 2 + half + 1)
                    if half == 0:
                        pe.wait_ge(s_masked, L * NI + NI)
                    else:
                        pe.wait_ge(s_olo, L * NI + NI - 1)
                    for c in range(2):
                        mm = pe.transpose(ps[:, BK_KV, c * P:(c + 1) * P], osb[:, c * P:(c + 1) * P], ident)
                    mm.then_inc(s_pv, 1)

                def cached_b():
                    kvc_wait(pe, L, 0)
                    pe.wait_ge(s_pts, L * NI + 6)
                    for j in range(2):
                        r = slice(HD * j, HD * (j + 1))
                        for b in range(NB):
                            to = ps[:, BK_T + j, b // 4 * P:(b // 4 + 1) * P].rearrange("p (c n) -> p c n", c=4)
                            mm = pe.matmul(to[:, :, NT * (b % 4):NT * (b % 4 + 1)], kvc[r, 0, b * P:(b + 1) * P],
                                           qk[r, 1:5, SEQ + NT * b:SEQ + NT * (b + 1)], start=True, stop=True)
                    mm.then_inc(kvc_used, 1)

                def token_rows(u):
                    n = KV_UNITS.index(u)
                    if COLS[u][0] == "k":
                        src = qk[:, qk_slot(*COLS[u]), :]
                        pe.wait_ge(rope_done, L * 17 + QK_UNITS.index(u) + 1)
                    else:
                        src = t1[:, u % 2, :]
                        pe.wait_ge(t1_done, L * N_IN + u + 1)
                    if n >= 1:
                        pe.wait_ge(kvtok_done, L * 14 + n)
                    pe.transpose(ps[:, BK_KV, 0:P], src[:, 0:P], ident)
                    pe.transpose(ps[:, BK_KV, P:2 * P], src[:, P:2 * P], ident)
                    pe.transpose(ps[0:HALF, BK_KV, 2 * P:3 * P], src[:, SEQ:SEQ + HALF], ident)
                    pe.transpose(ps[0:HALF, BK_KV, 3 * P:4 * P], src[:, SEQ + HALF:TOK], ident).then_inc(kvt_done, 1)

                for kind, n in STEPS:
                    if kind == "U":
                        pe.wait_ge(wlo_done, L * NU + U_IN + n + RAW + 1)
                        if n >= 2:
                            pe.wait_ge(zs_done, L * N_IN + n - 1)
                        for k in range(KD):
                            if n == 0:
                                pe.wait_ge(xs_ready, (L * 3 + 1) * KD + k + 1)
                            mm = product(ps[:, n % 2, 0:TOK], n % RING, k, xhi[:, k, :], xlo[:, k, :], k == 0, k == KD - 1)
                        mm.then_inc(unit_used, 1)
                        if n == 0:
                            sum_squares(L * 3 + 1)
                    elif kind == "R":
                        token_rows(n)
                    elif kind == "S" and n < NSC:
                        scores(n)
                    elif kind == "T":
                        transposes(n)
                    elif kind == "O":
                        values(n)
                    elif kind == "K":
                        cached_keys(n)
                    elif kind == "V":
                        cached_values(n)
                    elif kind == "X":
                        output_rows(n)
                    elif kind == "KB":
                        cached_b()
                for m in range(KD):
                    ba, bb = BK_BR[m % 2]
                    pe.wait_ge(wlo_done, L * NU + U_BR + m + RAW + 1)
                    if m == 0:
                        pe.wait_ge(s_olo, L * NI + NI)
                        pe.wait_ge(zs_done, L * N_IN + N_IN)
                    else:
                        pe.wait_ge(taken, L * NR + R_BR + m + RING - 1)
                    for k in range(BR_TILES):
                        out = ps[:, ba if k < 2 else bb, 0:TOK]
                        mm = product(out, m % RING, k, ohi[:, k, :], olo[:, k, :], k in (0, 2), k in (1, 5))
                    mm.then_inc(unit_used, 1)
                for m in range(KD):
                    pe.wait_ge(wlo_done, L * NU + U_WO + m + RAW + 1)
                    pe.wait_ge(taken, L * NR + R_WO + m + RING - 1)
                    for k in range(KD):
                        if m == 0:
                            pe.wait_ge(mlo_done, L * KD + k + 1)
                        mm = product(ps[:, BK_WO + m % 2, 0:TOK], m % RING, k, mhi[:, k, :], mlo[:, k, :],
                                     k == 0, k == KD - 1)
                    mm.then_inc(unit_used, 1)

            pe.wait_ge(set_up, 2)
            pe.wait_ge(start_in, 64)
            with pe.Fori(0, DEPTH) as L:
                ffn_products(L, 0)
                mixer_products(L)
                ffn_products(L, 1)
            sum_squares(3 * DEPTH)

        @block.scalar
        def _(act):
            def round_unit(L, base, i, step, s, tiles):
                act.wait_ge(unit_used, L * NU + i * step + base + s + 1)
                act.wait_ge(raw_in[(base + s) % RAW], (L * (NU // 2) + i * (step // 2) + (base + s) // 2 + 1) * 16)
                nc.scalar.activation(whi[:, (base + s) % RING, 0:tiles * P], raw[:, (base + s) % RAW, 0:tiles * P],
                                     ACT.Copy).then_inc(whi_done, 1)

            def root(n):
                act.wait_ge(ms_ready, n + 1)
                nc.scalar.activation(rms[:, :], ps[:, BK_O, 0:TOK], ACT.Sqrt, bias=eps[:, :], scale=1.0 / D)\
                    .then_inc(rms_done, 1)

            def round_x(norm, m, slot):
                act.wait_ge(xg_ready, norm * KD + m + 1)
                dst = xhi[:, m, :] if isinstance(m, int) else xhi[:, at(m), :].rearrange("p o n -> p (o n)")
                nc.scalar.activation(dst, xg[:, slot, :], ACT.Copy).then_inc(xhi_done, 1)

            def ffn_act(L, f):
                def gate_up(i, first, tiles):
                    if first:
                        root(L * 3 + 2 * f)
                    for s in range(4):
                        if s % 2 == 0:
                            act.wait_ge(taken, L * NR + i * 4 + R_GU[f] + s + RING + 1)
                            nc.scalar.activation(gate_s[:, s // 2, :], gate_s[:, s // 2, :], ACT.Silu)\
                                .then_inc(silu_done, 1)
                        round_unit(L, U_GU[f] + 4, i, 4, s, tiles[s])
                        if s % 2 == 1:
                            act.wait_ge(prod_done, L * 2 * KF + i * 2 + f * KF + s // 2 + 1)
                            j = i * 2 + s // 2
                            dst = act_hi[:, j, :] if isinstance(j, int) else \
                                act_hi[:, at(j), :].rearrange("p o n -> p (o n)")
                            nc.scalar.activation(dst, up_s[:, s // 2, :], ACT.Copy).then_inc(acthi_done, 1)

                def down(i, tail):
                    for o in range(2):
                        for s in range(4):
                            if o == 0 or tail != "none":
                                round_unit(L, U_DN[f] + 4, i, 8, 4 * o + s,
                                           UT if o == 1 and tail == "next" else DN_TILES[s])
                        round_x(L * 3 + 1 + 2 * f, i * 2 + o, o)

                gate_up(0, True, (UT,) * 4)
                with act.Fori(1, KF // 2 - 1) as i:
                    gate_up(i, False, (UT,) * 4)
                gate_up(KF // 2 - 1, False, DN_TILES)
                with act.Fori(0, KD // 2 - 1) as i:
                    down(i, "same")
                down(KD // 2 - 1, ("next", "none")[f])

            def mixer_act(L):
                for kind, n in STEPS:
                    if kind == "U":
                        if n == 0:
                            root(L * 3 + 1)
                        act.wait_ge(unit_used, L * NU + U_IN + n + RING + 1)
                        if n >= 2:
                            act.wait_ge(t1_done, L * N_IN + n - 1)
                            if n - 2 in QK_UNITS:
                                act.wait_ge(shuf_done, L * 17 + QK_UNITS.index(n - 2) + 1)
                        nc.scalar.activation(zs[:, n % 2, :], ps[:, n % 2, 0:TOK], ACT.Copy).then_inc(zs_done, 1)
                        round_unit(L, U_IN + 4, 0, 0, n, UT if n + 4 < N_IN else BR_TILES)
                    elif kind == "R":
                        g, c = COLS[n][1:]
                        act.wait_ge(kvt_done, L * 14 + KV_UNITS.index(n) + 1)
                        if COLS[n][0] == "k":
                            nk = K_UNITS.index(n)
                            if nk >= 2:
                                tot = (4 * 48, 3 * 48)[nk % 2]
                                act.wait_ge(kst_out[nk % 2], L * tot + 48 * (nk // 2))
                            to, new = kst[:, nk % 2, 0:2 * P], kst[0:HALF, nk % 2, 2 * P:4 * P]
                            nc.scalar.activation(to, ps[:, BK_KV, 0:2 * P], ACT.Copy)
                            nc.scalar.activation(new, ps[0:HALF, BK_KV, 2 * P:4 * P], ACT.Copy)\
                                .then_inc(kvtok_done, 1)
                        else:
                            v0 = v_slot(g, c) * P
                            nc.scalar.activation(vtok[:, :, v0:v0 + P],
                                                 ps[:, BK_KV, 0:2 * P].rearrange("p (t f) -> p t f", t=2), ACT.Copy)
                            nc.scalar.activation(vnew[:, :, v0:v0 + P],
                                                 ps[0:HALF, BK_KV, 2 * P:4 * P].rearrange("p (t f) -> p t f", t=2),
                                                 ACT.Copy).then_inc(kvtok_done, 1)
                    elif kind == "G":
                        k = G_UNITS.index(n)
                        act.wait_ge(t1_done, L * N_IN + n + 1)
                        nc.scalar.activation(gate[:, k, :], t1[:, n % 2, :], ACT.Exp, scale=-1.0).then_inc(gexp_done, 1)
                    elif kind == "S":
                        what, h, t = ITEMS[n]
                        w, segs = segments(n)
                        act.wait_ge(s_masked, L * NI + n + 1)
                        for j in range(segs):
                            mm = nc.scalar.activation(e[:, n % 2, j * w:(j + 1) * w], e[:, n % 2, j * w:(j + 1) * w],
                                                      ACT.Exp, bias=nmx[:, n % 2, j:j + 1], scale=SCALE,
                                                      accum_out=den[:, n % 2, j:j + 1])
                            if segs == 2:
                                col = h + 4 * j if what == "B" else 8 + j
                                sink = sinks[:, at(L), col:col + 1].rearrange("p o n -> p (o n)")
                                mm = nc.scalar.activation(esk[:, n % 2, j:j + 1], nmx[:, n % 2, j:j + 1], ACT.Exp,
                                                          bias=sink)
                        mm.then_inc(s_exp, 1)
                    elif kind == "T":
                        what, h, t = ITEMS[n]
                        act.wait_ge(s_pt, L * NI + n + 1)
                        if n >= 2 and what != "SA":
                            act.wait_ge(s_pv, L * NI + n - 1)
                        if what in ("A", "B"):
                            w = (NG if what == "A" else 2) * (t + 1) * P
                        else:
                            w = (NG if what == "SA" else 2) * P
                            if what == "SA" and h == 0:
                                act.wait_ge(pm_zero, L + 1)
                            if what == "SA" and h == 1:
                                act.wait_ge(kvc_used, L * N_KV + 1 + 3 * CT)
                            nc.scalar.activation(ptn[:, n % 2, 0:w], ps[0:HALF, BK_T + 1, 0:w], ACT.Copy)
                        if what == "SA":
                            src = ps[:, BK_T, :]
                            by_tile = ((0, ((CT * HALF, 4), (1, HALF))),
                                       (HALF, ((CT * HALF, 4), (4, 2 * 4), (HALF + 1, 4))),
                                       (5 * HALF, ((CT * HALF, 4), (NT, 4), (HALF + 1, NT))))
                            for g, (offset, dims) in enumerate(by_tile):
                                shape = dict(b=4) if g == 0 else dict(b=4, h=dims[1][1])
                                part = src[:, g * P:(g + 1) * P].rearrange(
                                    "p (b n) -> p b n" if g == 0 else "p (b h n) -> p b h n", **shape)
                                mm = nc.scalar.activation(strided(pt_mem[:, :], offset, dims), part, ACT.Copy)
                            mm.then_inc(s_pts, 1)
                        else:
                            flat = ps[:, BK_T:BK_T + 2, :].rearrange("p b n -> p (b n)")
                            nc.scalar.activation(pts[:, n % 2, 0:w], flat[:, 0:w], ACT.Copy).then_inc(s_pts, 1)
                    elif kind == "E":
                        if n == 0:
                            act.wait_ge(kvc_used, L * N_KV + 1)
                            nc.scalar.activation(stb[:, :, :], ps[:, BK_T:BK_T + 2, 0:2 * P], ACT.Copy)\
                                .then_inc(sts_done, 1)
                        else:
                            act.wait_ge(kvc_used, L * N_KV + 1 + CT)
                            act.wait_ge(s_scores, L * NSC + 10)
                            nc.scalar.activation(sts[:, 0:N_SA], ps[:, BK_KV, 0:N_SA], ACT.Copy)\
                                .then_inc(sts_done, 1)
                    elif kind == "Y":
                        act.wait_ge(kvc_used, L * N_KV + 1 + (3 + ITEMS[n][1]) * CT)
                        if ITEMS[n][1] == 1:
                            act.wait_ge(s_pv, L * NI + n)
                        nc.scalar.activation(osb[:, :], ps[:, BK_O, 0:2 * P], ACT.Copy).then_inc(osb_done, 1)
                    elif kind == "W":
                        act.wait_ge(s_pv, L * NI + n + 1)
                        if ITEMS[n][0] == "SA":
                            for hh in range(2):
                                to, src = out_halves(ITEMS[n][1], hh, ohi)
                                mm = nc.scalar.activation(to, src, ACT.Copy)
                        else:
                            to, src = out_place(n, ohi)
                            mm = nc.scalar.activation(to, src, ACT.Copy)
                        mm.then_inc(s_ohi, 1)
                for m in range(KD):
                    round_unit(L, U_BR + 4, 0, 0, m, BR_TILES if m < 4 else UT)
                    act.wait_ge(mab_done, L * KD + m + 1)
                    nc.scalar.activation(mhi[:, m, :], ma[:, m % 2, :], ACT.Copy).then_inc(mhi_done, 1)
                for m in range(KD):
                    round_unit(L, U_WO + 4, 0, 0, m, UT)
                    round_x(L * 3 + 2, m, m % 2)

            act.wait_ge(set_up, 2)
            act.wait_ge(start_in, 64)
            for m in range(KD):
                round_x(0, m, m % 2)
            with act.Fori(0, DEPTH) as L:
                for s in range(4):
                    round_unit(L, 0, 0, 0, s, UT)
                ffn_act(L, 0)
                mixer_act(L)
                ffn_act(L, 1)
            root(3 * DEPTH)

        @block.vector
        def _(dve):
            def rest_unit(L, base, i, step, s, tiles):
                dve.wait_ge(whi_done, L * NU + i * step + base + s + 1)
                nc.vector.tensor_tensor(wlo[:, (base + s) % RING, 0:tiles * P], raw[:, (base + s) % RAW, 0:tiles * P],
                                        whi[:, (base + s) % RING, 0:tiles * P].bitcast(F32), ALU.subtract)\
                    .then_inc(wlo_done, 1)

            def chunk(t, m):
                return t[:, m, :] if isinstance(m, int) else t[:, at(m), :].rearrange("p o n -> p (o n)")

            def gain(norm, m):
                if isinstance(norm, int) and isinstance(m, int):
                    return gains[:, norm, m:m + 1]
                g = gains[:, :, :].rearrange("p n k -> p (n k)")
                return g[:, at(norm * KD + m)]

            def scale_x(norm, m, slot):
                nc.vector.tensor_scalar(xg[:, slot, :], chunk(x, m), gain(norm, m), None, ALU.mult)\
                    .then_inc(xg_ready, 1)

            def rest_x(norm, m, slot):
                dve.wait_ge(xhi_done, norm * KD + m + 1)
                nc.vector.tensor_tensor(chunk(xlo, m), xg[:, slot, :], chunk(xhi, m).bitcast(F32), ALU.subtract)\
                    .then_inc(xs_ready, 1)

            def invert(n):
                dve.wait_ge(rms_done, n + 1)
                nc.vector.reciprocal(rinv[:, :], rms[:, :]).then_inc(rinv_ready, 1)
                dve.wait_ge(rinv_ready, n + 1)

            def add_to_x(L, bank, m, result, factor):
                nc.vector.scalar_tensor_tensor(chunk(x, m), ps[:, bank, 0:TOK], factor, chunk(x, m),
                                               ALU.mult, ALU.add).then_inc(taken, 1)
                dve.wait_ge(taken, L * NR + result + RING + 1)

            def ffn_vec(L, f):
                def gate_up(i, first, tiles):
                    if first:
                        invert(L * 3 + 2 * f)
                    for s in range(4):
                        dve.wait_ge(unit_used, L * NU + i * 4 + U_GU[f] + s + RING + 1)
                        if s % 2 == 0:
                            dve.wait_ge(actlo_done, L * 2 * KF + i * 2 + f * KF + s // 2 + 1)
                        nc.vector.tensor_tensor((gate_s, up_s)[s % 2][:, s // 2, :], ps[:, s, 0:TOK], rinv[:, :],
                                                ALU.mult).then_inc(taken, 1)
                        rest_unit(L, U_GU[f] + 4, i, 4, s, tiles[s])

                def down(i, tail):
                    norm = L * 3 + 1 + 2 * f
                    for o in range(2):
                        for s in range(4):
                            if s == 3:
                                dve.wait_ge(unit_used, L * NU + i * 8 + U_DN[f] + 4 * o + s + RING + 1)
                                add_to_x(L, BK_DN + o, i * 2 + o, i * 2 + R_DN[f] + o, 0.5)
                                scale_x(norm, i * 2 + o, o)
                            if o == 0 or tail != "none":
                                rest_unit(L, U_DN[f] + 4, i, 8, 4 * o + s,
                                          UT if o == 1 and tail == "next" else DN_TILES[s])
                        rest_x(norm, i * 2 + o, o)

                gate_up(0, True, (UT,) * 4)
                with dve.Fori(1, KF // 2 - 1) as i:
                    gate_up(i, False, (UT,) * 4)
                gate_up(KF // 2 - 1, False, DN_TILES)
                with dve.Fori(0, KD // 2 - 1) as i:
                    down(i, "same")
                down(KD // 2 - 1, ("next", "none")[f])

            def mixer_vec(L):
                shuffle = [p + 8 if p < 8 else p - 8 if p < 16 else p for p in range(32)]
                for kind, n in STEPS:
                    b = n % 2
                    if kind == "U":
                        if n == 0:
                            invert(L * 3 + 1)
                            nc.vector.tensor_tensor(cosr[:, :], const[:, C_COS:C_COS + TOK], rinv[:, :], ALU.mult)\
                                .then_inc(tabs_ready, 1)
                            nc.vector.tensor_tensor(sinr[:, :], const[:, C_SIN:C_SIN + TOK], rinv[:, :], ALU.mult)\
                                .then_inc(tabs_ready, 1)
                        if n in QK_UNITS:
                            k = QK_UNITS.index(n)
                            dve.wait_ge(zs_done, L * N_IN + n + 1)
                            if k >= 1:
                                dve.wait_ge(rope_done, L * 17 + k)
                            plain(dve)
                            nc.vector.stream_shuffle(sh[:, :], zs[:, b, :], shuffle).then_inc(shuf_done, 1)
                            dve.wait_ge(shuf_done, L * 17 + k + 1)
                            if k == 0:
                                dve.wait_ge(tabs_ready, L * 2 + 2)
                            nc.vector.tensor_tensor(sh[:, :], sh[:, :], sinr[:, :], ALU.mult).then_inc(shs_done, 1)
                            dve.wait_ge(shs_done, L * 17 + k + 1)
                            dve.wait_ge(t1_done, L * N_IN + n + 1)
                            nc.vector.tensor_tensor(qk[:, qk_slot(*COLS[n]), :], t1[:, b, :], sh[:, :], ALU.add)\
                                .then_inc(rope_done, 1)
                        rest_unit(L, U_IN + 4, 0, 0, n, UT if n + 4 < N_IN else BR_TILES)
                    elif kind == "Q":
                        dve.wait_ge(qm_zero, L + 1)
                        if n == 0:
                            dve.wait_ge(rope_done, L * 17 + 17)
                        else:
                            dve.wait_ge(kvc_used, L * N_KV + 1 + CT)
                        new = slice(SEQ + HALF * n, SEQ + HALF * (n + 1))
                        step_b, step_j = N_QM * 6 * NT, 6 * NT
                        for c in range(2):
                            for hh in range(2):
                                r = slice(HD * hh, HD * (hh + 1))
                                f0 = 4 * NT * c + NT * hh
                                to = qm[r, :, :, :].rearrange("p b j n -> p (b j n)")
                                for g in range(NG):
                                    src = qk[r, qk_slot("q", g, c), new]
                                    nc.vector.tensor_copy(qm[r, :, K_FULL[g], f0:f0 + NT],
                                                          src.rearrange("p (b n) -> p b n", b=4))
                                src = qk[r, qk_slot("q", 1, c), new].rearrange("p (b k n) -> p b k n", b=4, k=2)
                                nc.vector.tensor_copy(
                                    strided(to, step_j + f0, ((step_b, 4), (4, 2), (step_j + 1, 4))), src)
                                src = qk[r, qk_slot("q", 2, c), new].rearrange("p (b n) -> p b n", b=4)
                                mm = nc.vector.tensor_copy(
                                    strided(to, 5 * step_j + f0, ((step_b, 4), (step_j + 1, NT))), src)
                        mm.then_inc(qm_done, 1)
                    elif kind == "G":
                        k = G_UNITS.index(n)
                        dve.wait_ge(gexp_done, L * 16 + k + 1)
                        nc.vector.tensor_scalar_add(gate[:, k, :], gate[:, k, :], 1.0).then_inc(gadd_done, 1)
                        dve.wait_ge(gadd_done, L * 16 + k + 1)
                        nc.vector.reciprocal(gate[:, k, :], gate[:, k, :]).then_inc(gate_ready, 1)
                    elif kind == "S":
                        what, h, t = ITEMS[n]
                        w, segs = segments(n)
                        if n < NSC:
                            dve.wait_ge(s_scores, L * NSC + n + 1)
                        elif h == 0:
                            dve.wait_ge(sts_done, L * 2 + 2)
                        else:
                            dve.wait_ge(kvc_used, L * N_KV + 1 + 2 * CT)
                        if n >= 2:
                            dve.wait_ge(s_pt, L * NI + n - 1)
                        plain(dve)
                        flat = ps[:, BK_S:BK_S + 2, :].rearrange("p b n -> p (b n)")
                        for j in range(segs):
                            to = e[:, b, j * w:(j + 1) * w]
                            src = ps[:, BK_S + j, 0:w] if segs == 2 else flat[:, 0:w]
                            if what == "B":
                                mask = const[:, C_MB + SEQ - w:C_MB + SEQ]
                            elif what == "A":
                                mask = const[:, C_MA:C_MA + NG * SEQ].rearrange("p (g k) -> p g k", g=NG)
                                mask = mask[:, :, SEQ - w // NG:SEQ]
                                to, src = (v.rearrange("p (g k) -> p g k", g=NG) for v in (to, src))
                            else:
                                c0 = C_SA if what == "SA" else C_SB
                                mask = const[:, c0:c0 + w]
                            if what == "SA":
                                src = sts[:, 0:w] if h == 0 else ps[:, BK_KV, 0:w]
                            mm = nc.vector.tensor_tensor_reduce(out=to, in0=src, in1=mask, scale=1.0, scalar=-3e38,
                                                                op0=ALU.add, op1=ALU.max,
                                                                accum_out=mx[:, b, j:j + 1])
                        mm.then_inc(s_max, 1)
                        dve.wait_ge(s_max, L * NI + n + 1)
                        nc.vector.tensor_scalar(nmx[:, b, 0:segs], mx[:, b, 0:segs], -SCALE, None, ALU.mult)\
                            .then_inc(s_masked, 1)
                    elif kind == "N":
                        w, segs = segments(n)
                        dve.wait_ge(s_exp, L * NI + n + 1)
                        if segs == 2:
                            nc.vector.tensor_tensor(den[:, b, :], den[:, b, :], esk[:, b, :], ALU.add)\
                                .then_inc(s_den, 1)
                            dve.wait_ge(s_den, L * 10 + n + 1)
                        nc.vector.reciprocal(rden[:, b, 0:segs], den[:, b, 0:segs]).then_inc(s_rden, 1)
                        dve.wait_ge(s_rden, L * NI + n + 1)
                        for j in range(segs):
                            part = e[:, b, j * w:(j + 1) * w]
                            mm = nc.vector.tensor_scalar(part, part, rden[:, b, j:j + 1], None, ALU.mult)
                        mm.then_inc(s_norm, 1)
                    elif kind == "W":
                        dve.wait_ge(s_ohi, L * NI + n + 1)
                        pairs = []
                        if ITEMS[n][0] == "SA":
                            pairs = [(out_halves(ITEMS[n][1], hh, olo), out_halves(ITEMS[n][1], hh, ohi)[0])
                                     for hh in range(2)]
                        else:
                            pairs = [(out_place(n, olo), out_place(n, ohi)[0])]
                        for (to, src), hi in pairs:
                            mm = nc.vector.tensor_tensor(to, src, hi.bitcast(F32), ALU.subtract)
                        mm.then_inc(s_olo, 1)
                for m in range(KD):
                    ba, bb = BK_BR[m % 2]
                    dve.wait_ge(unit_used, L * NU + U_BR + m + RING + 1)
                    dve.wait_ge(gate_ready, L * 16 + 2 * m + 2)
                    if m >= 2:
                        dve.wait_ge(mlo_done, L * KD + m - 1)
                    nc.vector.tensor_tensor(ma[:, m % 2, :], ps[:, ba, 0:TOK], gate[:, 2 * m, :], ALU.mult)
                    nc.vector.tensor_tensor(mb[:, m % 2, :], ps[:, bb, 0:TOK], gate[:, 2 * m + 1, :], ALU.mult)\
                        .then_inc(taken, 1)
                    rest_unit(L, U_BR + 4, 0, 0, m, BR_TILES if m < 4 else UT)
                for m in range(KD):
                    dve.wait_ge(unit_used, L * NU + U_WO + m + RING + 1)
                    add_to_x(L, BK_WO + m % 2, m, R_WO + m, 1.0)
                    scale_x(L * 3 + 2, m, m % 2)
                    rest_unit(L, U_WO + 4, 0, 0, m, UT)
                    rest_x(L * 3 + 2, m, m % 2)

            dve.sem_inc(wlo_done, RAW)
            dve.sem_inc(unit_used, RING)
            dve.sem_inc(taken, RING)
            dve.sem_inc(actlo_done, 2)
            nc.vector.memset(ones[:, :], 1.0).then_inc(set_up, 1)
            nc.vector.memset(eps[:, :], EPS).then_inc(set_up, 1)
            dve.wait_ge(start_in, 64)
            for m in range(KD):
                scale_x(0, m, m % 2)
                rest_x(0, m, m % 2)
            with dve.Fori(0, DEPTH) as L:
                for s in range(4):
                    rest_unit(L, 0, 0, 0, s, UT)
                ffn_vec(L, 0)
                mixer_vec(L)
                ffn_vec(L, 1)
            dve.wait_ge(xs_ready, (3 * DEPTH + 1) * KD)
            dve.wait_ge(ssq_done, (3 * DEPTH + 1) * (KD + 1))
            for m in range(KD):
                nc.vector.tensor_tensor(x[:, m, :], xhi[:, m, :].bitcast(F32), xlo[:, m, :].bitcast(F32), ALU.add)\
                    .then_inc(y_sum, 1)
            invert(3 * DEPTH)
            for m in range(KD):
                dve.wait_ge(y_sum, m + 1)
                nc.vector.tensor_tensor(x[:, m, :], x[:, m, :], rinv[:, :], ALU.mult).then_inc(y_done, 1)

        @block.gpsimd
        def _(pool):
            def chunk(t, m):
                return t[:, m, :] if isinstance(m, int) else t[:, at(m), :].rearrange("p o n -> p (o n)")

            def clear_squares(norm, first=False):
                if not first:
                    pool.wait_ge(rinv_ready, norm)
                    plain(pool)
                nc.gpsimd.memset(ssq[:, :], 0.0).then_inc(ssq_done, 1)

            def add_squares(norm, m):
                pool.wait_ge(ssq_done, norm * (KD + 1) + m + 1)
                nc.gpsimd.tensor_tensor(sq[:, :], chunk(x, m), chunk(x, m), ALU.mult).then_inc(sq_done, 1)
                pool.wait_ge(sq_done, norm * KD + m + 1)
                nc.gpsimd.tensor_tensor(ssq[:, :], ssq[:, :], sq[:, :], ALU.add).then_inc(ssq_done, 1)

            def ffn_pool(L, f):
                with pool.Fori(0, KF // 2) as i:
                    for q in range(2):
                        pool.wait_ge(silu_done, L * 2 * KF + i * 2 + f * KF + q + 1)
                        pool.wait_ge(taken, L * NR + i * 4 + R_GU[f] + 2 * q + 2 + RING)
                        nc.gpsimd.tensor_tensor(up_s[:, q, :], gate_s[:, q, :], up_s[:, q, :], ALU.mult)\
                            .then_inc(prod_done, 1)
                        pool.wait_ge(acthi_done, L * 2 * KF + i * 2 + f * KF + q + 1)
                        j = i * 2 + q
                        nc.gpsimd.tensor_tensor(chunk(act_lo, j), up_s[:, q, :], chunk(act_hi, j).bitcast(F32),
                                                ALU.subtract).then_inc(actlo_done, 1)
                norm = L * 3 + 1 + 2 * f
                clear_squares(norm)
                with pool.Fori(0, KD // 2) as i:
                    for o in range(2):
                        pool.wait_ge(taken, L * NR + i * 2 + R_DN[f] + o + RING + 1)
                        add_squares(norm, i * 2 + o)

            def mixer_pool(L):
                pool.wait_ge(unit_used, L * NU + RING + U_IN)
                plain(pool)
                nc.gpsimd.memset(qm[:, :, :, :], 0.0).then_inc(qm_zero, 1)
                pool.wait_ge(tabs_ready, L * 2 + 2)
                for kind, n in STEPS:
                    if kind == "O" and n == NSC - 1:
                        pool.wait_ge(s_pv, L * NI + NSC)
                        plain(pool)
                        nc.gpsimd.memset(pt_mem[:, :], 0.0).then_inc(pm_zero, 1)
                    if kind != "U":
                        continue
                    what, g, c = COLS[n]
                    pool.wait_ge(zs_done, L * N_IN + n + 1)
                    if n >= 2:
                        before = COLS[n - 2][0]
                        if n - 2 in QK_UNITS:
                            pool.wait_ge(rope_done, L * 17 + QK_UNITS.index(n - 2) + 1)
                        elif before == "v":
                            pool.wait_ge(kvt_done, L * 14 + KV_UNITS.index(n - 2) + 1)
                        else:
                            pool.wait_ge(gexp_done, L * 16 + G_UNITS.index(n - 2) + 1)
                    by = cosr if what in "qk" else rinv
                    nc.gpsimd.tensor_tensor(t1[:, n % 2, :], zs[:, n % 2, :], by[:, :], ALU.mult).then_inc(t1_done, 1)
                norm = L * 3 + 2
                for m in range(KD):
                    pool.wait_ge(taken, L * NR + R_BR + m + RING + 1)
                    nc.gpsimd.tensor_tensor(ma[:, m % 2, :], ma[:, m % 2, :], mb[:, m % 2, :], ALU.add)\
                        .then_inc(mab_done, 1)
                    pool.wait_ge(mhi_done, L * KD + m + 1)
                    nc.gpsimd.tensor_tensor(mlo[:, m, :], ma[:, m % 2, :], mhi[:, m, :].bitcast(F32), ALU.subtract)\
                        .then_inc(mlo_done, 1)
                clear_squares(norm)
                for m in range(KD):
                    pool.wait_ge(taken, L * NR + R_WO + m + RING + 1)
                    add_squares(norm, m)

            pool.wait_ge(start_in, 64)
            clear_squares(0, True)
            for m in range(KD):
                add_squares(0, m)
            with pool.Fori(0, DEPTH) as L:
                ffn_pool(L, 0)
                mixer_pool(L)
                ffn_pool(L, 1)


def tiles_of(w, order=None):
    l, k, n = w.shape
    w = w.reshape(l, k // P, P, n // P, P).transpose(0, 3, 2, 1, 4).reshape(l, n // P, P, k)
    return np.ascontiguousarray(w if order is None else w[:, order]).reshape(-1, P, k)


def gqa_columns(w, axis):
    shape = list(w.shape)
    split = shape[:axis] + [2, 4, HD] + shape[axis + 1:]
    return w.reshape(split).swapaxes(axis, axis + 1).reshape(shape)


def lay_out(inputs):
    i = {k: np.asarray(v) for k, v in inputs.items()}
    tok = np.concatenate([i["x_prompt"].reshape(SEQ, D), i["x_sample"].reshape(NB * NT, D)])
    a = {"x": np.ascontiguousarray(tok.reshape(TOK, KD, P).transpose(2, 1, 0)), "const": constants()}
    norms = np.stack([i[k][l] for l in range(DEPTH) for k in ("norm_ffn1", "norm_mix", "norm_ffn2")] + [i["norm_final"]])
    a["gains"] = np.ascontiguousarray(norms.reshape(-1, KD, P).transpose(2, 0, 1))
    s = i["sinks"]
    rows = np.repeat(s.reshape(DEPTH, 2, 4), HALF, axis=2)
    a["sinks"] = np.ascontiguousarray(np.concatenate(
        [np.broadcast_to(s[None], (P, DEPTH, 8)), rows.transpose(2, 0, 1)], axis=2))
    for f in (1, 2):
        for k in ("gate", "up", "down"):
            a[f"ffn{f}_{k}"] = tiles_of(i[f"ffn{f}_{k}"])
    w = i["w_in"]
    ag = NG * 3 * 256
    bq = gqa_columns(w[:, :, ag:ag + 512], 2)
    parts = {("k", 3): w[:, :, ag + 512:ag + 640], ("v", 3): w[:, :, ag + 640:ag + 768], ("q", 3): bq,
             ("ga", 0): w[:, :, ag + 768:ag + 768 + D], ("gb", 0): w[:, :, ag + 768 + D:]}
    for g in range(NG):
        for n, k in enumerate("qkv"):
            c0 = (3 * g + n) * 256
            parts[(k, g)] = w[:, :, c0:c0 + 256]
    a["w_in"] = tiles_of(np.concatenate([parts[(k, g)][:, :, c * P:(c + 1) * P] for k, g, c in COLS], axis=2))
    a["w_branch"] = tiles_of(np.concatenate([i["w_branch_a"], gqa_columns(i["w_branch_b"], 1)], axis=1))
    a["w_out"] = tiles_of(i["w_out"])
    tiles = [i["cache_a1"]] + [i["cache_a2"][:, :, r::4] for r in range(4)] + [i["cache_a3"][:, :, r::16] for r in range(8)]
    kv = np.stack(tiles, axis=2).reshape(DEPTH, NB, CT, P, 2, 2, P)
    kv = kv.reshape(DEPTH, 2, 4, CT, P, 2, 2, P)
    a["kcache"] = np.ascontiguousarray(kv[..., 0, :, :].transpose(0, 1, 3, 6, 5, 2, 4)).reshape(-1, P, NB * P)
    a["vcache"] = np.ascontiguousarray(kv[..., 1, :, :].transpose(0, 1, 3, 4, 2, 5, 6)).reshape(-1, P, NB * P)
    b = i["cache_b"].reshape(DEPTH, NB, P, 2, P)
    a["kcache_b"] = np.ascontiguousarray(b[:, :, :, 0].transpose(0, 3, 1, 2)).reshape(DEPTH, P, NB * P)
    a["vcache_b"] = np.ascontiguousarray(b[:, :, :, 1].transpose(0, 2, 1, 3))
    for k in ("a1", "a2", "a3", "b"):
        a[f"cache_{k}"] = i[f"cache_{k}"]
    return a


_OUTS = {"y": (P, KD, TOK)}
for _n, _w, _h in (("a1", 128, 4), ("a2", 512, 4), ("a3", 2048, 4), ("b", 128, 2)):
    _OUTS[f"new_{_n}_prompt"] = (DEPTH, 1, min(_w, SEQ), 2, _h, HD)
    _OUTS[f"new_{_n}_sample"] = (DEPTH, NB, _w, 2, _h, HD)


def kernel(**inputs):
    import concourse.bacc as _bacc
    from concourse.bass_utils import run_bass_kernel_spmd as _run

    arrays = lay_out(inputs)
    nc = _bacc.Bacc("TRN2", target_bir_lowering=False, num_devices=1, dynamic_dma_scratch_size=1024)
    aps = {n: nc.dram_tensor(f"in_{n}", v.shape, mybir.dt.from_np(v.dtype), kind="ExternalInput").ap() for n, v in arrays.items()}
    for n, shape in _OUTS.items():
        aps[n] = nc.dram_tensor(f"out_{n}", shape, F32, kind="ExternalOutput").ap()
    build(nc, aps)
    got = _run(nc, [{f"in_{n}": v for n, v in arrays.items()}], core_ids=[0]).results[0]
    y = got["out_y"].transpose(2, 1, 0).reshape(TOK, D)
    return (np.ascontiguousarray(y[:SEQ]).reshape(1, SEQ, D), np.ascontiguousarray(y[SEQ:]).reshape(NB, NT, D),
            *(got[f"out_new_{n}_{k}"] for k in ("prompt", "sample") for n in ("a1", "a2", "a3", "b")))
```

```python
from contextlib import ExitStack

import numpy as np

import concourse.bass as bass
from concourse import mybir

F32 = mybir.dt.float32
F32R = mybir.dt.float32r
ALU = mybir.AluOpType
ACT = mybir.ActivationFunctionType

P = 128
DEPTH = 2
D = 1024
SEQ = 256
NB, NT = 8, 8
TOK = SEQ + NB * NT
HD = 64
KD = D // P
F = ((8 * D // 3 + 127) // 128) * 128
KF = F // P
DILS = ((128, 1), (512, 4), (2048, 16))
NG = len(DILS)
SCALE = HD ** -0.5
EPS = 1e-6
NEG = -1e30
HALF = 32
CT = 13
WIN = 128

UT = 8
RAW = 4
RING = 4
DN_TILES = (6, 5, 6, 5)
DN_K0 = (0, 6, 11, 17)
BR_TILES = 6
N_IN = 40
U_GU = (0, 132)
U_DN = (44, 176)
U_IN, U_BR, U_WO = 76, 116, 124
NU = 208
START_UNITS = (0, 3, 6, 7)
LOADS = (("x", 0), ("w", 0), ("x", 1), ("x", 2), ("w", 1), ("x", 3), ("w", 2), ("w", 3))
XPARTS = 4
R_GU, R_DN = (0, 68), (44, 112)
R_BR, R_WO = 52, 60
NR = 120

COLS = [("k", 3, 0), ("v", 3, 0)] + [("q", 3, c) for c in range(4)]
COLS += [("q", _g, _c) for _g in range(NG) for _c in range(2)]
COLS += [(_k, _g, _c) for _g in range(NG) for _k in "kv" for _c in range(2)]
COLS += [(_k, 0, _m) for _m in range(KD) for _k in ("ga", "gb")]
assert len(COLS) == N_IN
KV_UNITS = [u for u, c in enumerate(COLS) if c[0] in "kv"]
K_UNITS = [u for u in KV_UNITS if COLS[u][0] == "k"]
QK_UNITS = [u for u, c in enumerate(COLS) if c[0] in "qk"]
G_UNITS = [u for u, c in enumerate(COLS) if c[0] in ("ga", "gb")]


def qk_slot(kind, g, c):
    if g == 3:
        return 0 if kind == "k" else 1 + c
    return (5 if kind == "q" else 11) + 2 * g + c


def v_slot(g, c):
    return 6 if g == 3 else 2 * g + c


A_FIRST = 3
ITEMS = [("SB", h, 0) for h in range(2)] + [("B", c, t) for c in range(4) for t in range(2)]
_A = [("A", h, t) for h in range(4) for t in range(2)]
ITEMS += _A[:A_FIRST] + [("SA", h, 0) for h in range(2)] + _A[A_FIRST:]
NI = len(ITEMS)
SA0 = ITEMS.index(("SA", 0, 0))
NSC = NI - 2
KV_RING = 3
N_KV = 1 + 4 * CT
K_FULL = (0, CT, CT + 1)
N_QM = CT + 2


def mixer_steps():
    steps, unit_at, tile_at = [], [0], [1]

    def unit(with_tile=False):
        u = unit_at[0]
        if u == N_IN:
            return
        unit_at[0] += 1
        steps.append(("U", u))
        if with_tile and tile_at[0] < N_KV:
            INNER[u] = tile_at[0]
            tile()
        rows(u - 2)
        if u - 1 in G_UNITS:
            steps.append(("G", u - 1))

    def rows(u):
        if u in KV_UNITS and ("R", u) not in steps:
            steps.append(("R", u))

    def tile():
        n = tile_at[0]
        if n == N_KV or n == CT + 1 and ("Q", 1) in steps[-7:]:
            return
        tile_at[0] += 1
        steps.append(("K" if n <= 2 * CT else "V", n))
        if n == CT:
            steps.extend([("E", SA0), ("Q", 1)])
        if n == 3 * CT:
            steps.append(("Y", SA0))

    for _ in range(7):
        unit()
    for p in range(NI + 2):
        if p == 3:
            steps.append(("Q", 0))
        if p == SA0 + 1:
            while tile_at[0] <= 2 * CT:
                tile()
        places = TILE_PLACES[BEAT_TILES[p]]
        evacuated = ("Y", SA0) in steps
        if p < NI:
            steps.append(("S", p))
        if 1 <= p <= NI:
            steps.append(("N", p - 1))
        if "a" in places:
            tile()
        unit("b" in places)
        if "c" in places:
            tile()
        if p < 7:
            unit("d" in places)
        if p == 9:
            while unit_at[0] < 25:
                unit()
        if 1 <= p <= NI:
            steps.append(("T", p - 1))
        if "e" in places:
            tile()
        if 2 <= p:
            steps.append(("O", p - 2))
            if ITEMS[p - 2][0] != "SA":
                steps.append(("W", p - 2))
        if "f" in places:
            tile()
        if evacuated and ("X", SA0) not in steps:
            steps += [("X", SA0), ("W", SA0)]
    while tile_at[0] < N_KV:
        tile()
    steps.append(("Y", SA0 + 1))
    unit()
    steps += [("X", SA0 + 1), ("W", SA0 + 1)]
    while unit_at[0] < N_IN:
        unit()
    steps.append(("G", N_IN - 1))
    return steps


BEAT_TILES = [0] * 3 + [1, 2, 2, 2, 2, 2, 1] + [3, 4, 4, 5, 0] + [1, 4, 4, 4, 4, 4, 5]
TILE_PLACES = {0: "", 1: "f", 2: "bf", 3: "bef", 4: "bcef", 5: "abcef"}
INNER = {}
STEPS = mixer_steps()
OUT_ORDER = [n for _k, n in STEPS if _k == "W"]


def before(kind, step):
    return sum(k == kind for k, _ in STEPS[:STEPS.index(step)])


def cache_load_places():
    at, last = {}, 0
    for kind, n in STEPS:
        if kind == "U":
            last = n
        if kind in ("K", "V"):
            at[n] = last - (n in INNER.values())
        if (kind, n) == ("S", 1):
            at[0] = last
    return [8, 9, 10] + [min(at[n - KV_RING] + 7, 55) for n in range(KV_RING, N_KV)]


KV_PLACE = cache_load_places()

C_COS, C_SIN = 0, TOK
C_MA = 2 * TOK
C_MB = C_MA + NG * SEQ
C_SA = C_MB + SEQ
N_SA = NG * (P + HALF)
C_SB = C_SA + N_SA
N_SB = P + HALF
C_ID = C_SB + N_SB
N_C = C_ID + P


def constants():
    c = np.zeros((P, N_C), np.float32)
    rot = HD // 4
    half = rot // 2
    inv = np.float32(500000.0) ** (-(np.arange(half, dtype=np.float32) * np.float32(2.0) / np.float32(rot)))
    pos = np.concatenate([np.arange(SEQ), np.tile(2048 + np.arange(NT), NB)]).astype(np.float32)
    ang = (inv[:, None] * pos[None, :]).astype(np.float32)
    c[:, C_COS:C_COS + TOK] = 1.0
    for base in (0, HD):
        for part, sign in ((0, -1.0), (half, 1.0)):
            c[base + part:base + part + half, C_COS:C_COS + TOK] = np.cos(ang)
            c[base + part:base + part + half, C_SIN:C_SIN + TOK] = sign * np.sin(ang)
    dist = (P + np.arange(P))[:, None] - np.arange(SEQ)[None, :]
    for g, (win, dil) in enumerate(DILS):
        ok = (dist >= 0) & (dist <= win) & (dist % dil == 0)
        c[:, C_MA + g * SEQ:C_MA + (g + 1) * SEQ] = np.where(ok, 0, NEG)
    c[:, C_MB:C_MB + SEQ] = np.where((dist >= 0) & (dist < WIN), 0, NEG)
    b, t = (np.arange(P) // HALF)[:, None], (np.arange(P) % NT)[:, None]
    r = np.arange(P)[None, :]
    nb, s = (np.arange(HALF) // NT)[None, :], (np.arange(HALF) % NT)[None, :]
    for g, (win, dil) in enumerate(DILS):
        row = r if g == 0 else t % dil + dil * r
        ok = (row >= t) & (row <= win + t)
        c[:, C_SA + g * P:C_SA + (g + 1) * P] = np.where(ok, 0, NEG)
        ok = (nb == b) & (s <= t) & ((t - s) % dil == 0)
        o = C_SA + NG * P + g * HALF
        c[:, o:o + HALF] = np.where(ok, 0, NEG)
    c[:, C_SB:C_SB + P] = np.where(r > t, 0, NEG)
    c[:, C_SB + P:C_SB + N_SB] = np.where((nb == b) & (s <= t), 0, NEG)
    c[:, C_ID:C_ID + P] = np.eye(P, dtype=np.float32)
    return c


BK_KV = 2
BK_ROWS = 6
BK_S = 3
BK_T = 5
BK_O = 7
BK_DN = 4
BK_WO = 5
BK_BR = ((0, 1), (3, 4))


def build(nc, a):
    ctx = ExitStack()
    with ctx:
        def sb(name, shape, dt=F32, where=ctx):
            return where.enter_context(nc.sbuf_tensor(name, shape, dt))

        def sem(name):
            return ctx.enter_context(nc.semaphore(name))

        const = sb("const", [P, N_C])
        ones = sb("ones", [P, P])
        eps = sb("eps", [P, 1])
        gains = sb("gains", [P, 3 * DEPTH + 1, KD])
        sinks = sb("sinks", [P, DEPTH, 10])
        x = sb("x", [P, KD, TOK])
        xg = sb("xg", [P, 2, TOK])
        xhi = sb("xhi", [P, KD, TOK], F32R)
        xlo = sb("xlo", [P, KD, TOK], F32R)
        sq = sb("sq", [P, TOK])
        ssq = sb("ssq", [P, TOK])
        rms = sb("rms", [P, TOK])
        rinv = sb("rinv", [P, TOK])
        raw = sb("raw", [P, RAW, UT * P])
        whi = sb("whi", [P, RING, UT * P], F32R)
        wlo = sb("wlo", [P, RING, UT * P], F32R)

        with ExitStack() as ffn:
            act_hi = sb("act_hi", [P, KF, TOK], F32R, ffn)
            act_lo = sb("act_lo", [P, KF, TOK], F32R, ffn)
            gate_s = sb("gate_s", [P, 2, TOK], F32, ffn)
            up_s = sb("up_s", [P, 2, TOK], F32, ffn)
        gate = sb("gate", [P, 2 * KD, TOK])
        ohi = sb("ohi", [P, BR_TILES, TOK], F32R)
        olo = sb("olo", [P, BR_TILES, TOK], F32R)
        with ExitStack() as att:
            kvc = sb("kvc", [P, KV_RING, NB * P], F32, att)
            vb = sb("vb", [P, NB, P], F32, att)
            qk = sb("qk", [P, 17, TOK], F32, att)
            vtok = sb("vtok", [P, 2, 7 * P], F32, att)
            vnew = sb("vnew", [HALF, 2, 7 * P], F32, att)
            kst = sb("kst", [P, 2, 3 * P], F32, att)
            qm_mem = sb("qm_mem", [P, 2 * 4 * CT * HALF], F32, att)
            e = sb("e", [P, 2, NG * SEQ], F32, att)
            pts = sb("pts", [P, 2, NG * SEQ], F32, att)
            ptn = sb("ptn", [HALF, 2, NG * P], F32, att)
            sts = sb("sts", [P, N_SA], F32, att)
            osb = sb("osb", [P, 2 * P], F32, att)
            t1 = sb("t1", [P, 2, TOK], F32, att)
            cosr = sb("cosr", [P, TOK], F32, att)
            sinr = sb("sinr", [P, TOK], F32, att)
            mx = sb("mx", [P, 2, 2], F32, att)
            nmx = sb("nmx", [P, 2, 2], F32, att)
            den = sb("den", [P, 2, 2], F32, att)
            esk = sb("esk", [P, 2, 2], F32, att)
            rden = sb("rden", [P, 2, 2], F32, att)
        with ExitStack() as out_mem:
            mhi = sb("mhi", [P, KD, TOK], F32R, out_mem)
            mlo = sb("mlo", [P, KD, TOK], F32R, out_mem)
            ma = sb("ma", [P, 2, TOK], F32, out_mem)
            mb = sb("mb", [P, 2, TOK], F32, out_mem)
        qm = qm_mem[:, 0:4 * N_QM * 6 * NT].rearrange("p (b j n) -> p b j n", b=4, j=N_QM)
        zs, sh = xg, sq
        pm = qm_mem[:, :].rearrange("p (f b i n) -> p f b i n", f=2, b=4, i=CT)
        ps = ctx.enter_context(nc.psum_tensor("ps", [P, 8, 512], F32))

        passed = sem("passed")
        x_in = [sem(f"x_in{n}") for n in range(XPARTS)]
        gains_in = sem("gains_in")
        const_in = sem("const_in")
        set_up = sem("set_up")
        raw_in = [sem(f"raw_in{s}") for s in range(RAW)]
        whi_done = sem("whi_done")
        wlo_done = sem("wlo_done")
        unit_used = sem("unit_used")
        taken = sem("taken")
        silu_done = sem("silu_done")
        prod_done = sem("prod_done")
        acthi_done = sem("acthi_done")
        actlo_done = sem("actlo_done")
        xg_ready = sem("xg_ready")
        xhi_done = sem("xhi_done")
        xs_ready = sem("xs_ready")
        sq_done = sem("sq_done")
        ssq_done = sem("ssq_done")
        ms_ready = sem("ms_ready")
        rms_done = sem("rms_done")
        rinv_ready = sem("rinv_ready")
        tabs_ready = sem("tabs_ready")
        zs_done = sem("zs_done")
        t1_done = sem("t1_done")
        shuf_done = sem("shuf_done")
        shs_done = sem("shs_done")
        rope_done = sem("rope_done")
        qm_zero = sem("qm_zero")
        qm_done = sem("qm_done")
        pm_zero = sem("pm_zero")
        kvt_done = sem("kvt_done")
        kvtok_done = sem("kvtok_done")
        kst_out = [sem(f"kst_out{s}") for s in range(2)]
        v_out = sem("v_out")
        gtanh_done = sem("gtanh_done")
        gate_ready = sem("gate_ready")
        vb_in = sem("vb_in")
        kvc_in = [sem(f"kvc_in{s}") for s in range(KV_RING)]
        kvc_used = sem("kvc_used")
        qb_done = sem("qb_done")
        sts_done = sem("sts_done")
        osb_done = sem("osb_done")
        s_scores = sem("s_scores")
        s_max = sem("s_max")
        s_masked = sem("s_masked")
        s_exp = sem("s_exp")
        s_den = sem("s_den")
        s_rden = sem("s_rden")
        s_norm = sem("s_norm")
        s_pt = sem("s_pt")
        s_pts = sem("s_pts")
        s_new = sem("s_new")
        s_pv = sem("s_pv")
        s_ohi = sem("s_ohi")
        s_olo = sem("s_olo")
        mab_done = sem("mab_done")
        mhi_done = sem("mhi_done")
        mlo_done = sem("mlo_done")
        y_done = sem("y_done")
        copy_out = sem("copy_out")
        y_out = sem("y_out")

        block = ctx.enter_context(nc.Block())
        ident = const[:, C_ID:C_ID + P]

        def at(v):
            return bass.ds(v, 1)

        def plain(eng):
            eng.sem_inc(passed, 1)

        def segments(i):
            kind, _, t = ITEMS[i]
            return {"B": (P * (t + 1), 2), "A": (NG * P * (t + 1), 1), "SB": (N_SB, 2), "SA": (N_SA, 1)}[kind]

        def out_place(i, o):
            kind, h, t = ITEMS[i]
            if kind == "B":
                return o[:, 2 + h, t * P:(t + 1) * P], ps[:, BK_O, 0:P]
            if kind == "A":
                r = slice(HD * (h % 2), HD * (h % 2 + 1))
                return o[r, h // 2, t * P:(t + 1) * P], ps[r, BK_O, 0:P]
            s0 = SEQ + HALF * h
            return (o[:, 2:6, s0:s0 + HALF].rearrange("p c (b n) -> p b c n", b=4),
                    ps[:, BK_O, 0:P].rearrange("p (b c n) -> p b c n", b=4, c=4))

        def out_halves(half, hh, o):
            r = slice(HD * hh, HD * (hh + 1))
            s0 = SEQ + HALF * half
            src = ps[r, BK_O, 0:2 * (P + 2 * NT)].rearrange("p (c n) -> p c n", c=2)[:, :, 0:P]
            src = src.rearrange("p c (b x) -> p c b x", b=4)[:, :, :, NT * hh:NT * (hh + 1)]
            return o[r, 0:2, s0:s0 + HALF].rearrange("p c (b n) -> p c b n", b=4), src

        def skips_first_rows(u):
            kind, g, _ = COLS[u]
            return kind == "k" and g in (0, 3)

        def new_place(kind, n, count):
            first = 2 + n if kind == "SB" else n
            return BK_T + (kind == "SA"), slice(first * P, (first + count) * P)

        def wait_slot_used(eng, L, n):
            m = n - 2
            if m >= 0 and ITEMS[m][0] == "SA":
                eng.wait_ge(s_new, L * 2 + m - SA0 + 1)
            elif m >= 0:
                eng.wait_ge(s_pv, L * NI + OUT_ORDER.index(m) + 1)

        def score_number(n):
            return n if n < SA0 else n - 2

        def kvc_wait(eng, L, n):
            s = n % KV_RING
            per_layer = (N_KV - s + KV_RING - 1) // KV_RING
            eng.wait_ge(kvc_in[s], (L * per_layer + n // KV_RING + 1) * 16)

        def strided(ap, offset, dims):
            return bass.AP(tensor=ap.tensor, offset=ap.offset + offset, ap=[list(ap.ap[0])] + [list(d) for d in dims])

        @block.sync
        def _(sp):
            kpre, vpre = a["kcache"], a["vcache"]
            big = a["cache_a3"][:, :, NT:, :, :, :].rearrange(
                "l b w v h d -> l b (w v h d)").rearrange("l b (f k n) -> l b f k n", f=2, k=P)
            big_o = a["new_a3_sample"][:, :, :DILS[2][0] - NT, :, :, :].rearrange(
                "l b w v h d -> l b (w v h d)").rearrange("l b (f k n) -> l b f k n", f=2, k=P)
            mid = a["cache_a2"][:, :, NT:, :, :, :].rearrange(
                "l b w v h d -> l b (w v h d)").rearrange("l b (k n) -> l b k n", k=P)
            mid_o = a["new_a2_sample"][:, :, :DILS[1][0] - NT, :, :, :].rearrange(
                "l b w v h d -> l b (w v h d)").rearrange("l b (k n) -> l b k n", k=P)

            def load_at(L, base, i, step, s, src, tiles):
                sp.wait_ge(wlo_done, L * NU + i * step + base + s + 1)
                sp.dma_start(raw[:, (base + s) % RAW, 0:tiles * P], src).then_inc(raw_in[(base + s) % RAW], 16)

            def one(ap):
                return ap.rearrange("o p n -> (o p) n")

            def ffn_loads(L, f):
                wg, wu, wd = (a[f"ffn{f + 1}_{k}"] for k in ("gate", "up", "down"))

                def group(i, copy):
                    for s in range(4):
                        w = (wg, wu)[s % 2]
                        load_at(L, U_GU[f], i, 4, s, one(w[at(L * KF + 2 * i + s // 2), :, :]), UT)
                        if copy is not None:
                            rows = slice(s * P // 4, (s + 1) * P // 4)
                            sp.dma_start(one(big_o[at(L), at(copy), f, rows, :].rearrange("l b k n -> (l b) k n")),
                                         one(big[at(L), at(copy), f, rows, :].rearrange("l b k n -> (l b) k n")))\
                                .then_inc(copy_out, 16)

                first = 1 - f
                with sp.Fori(first, NB + first) as i:
                    group(i, i - first)
                with sp.Fori(NB + first, KF // 2) as i:
                    group(i, None)
                with sp.Fori(0, KD // 2) as i:
                    for o in range(2):
                        for s in range(4):
                            k0, n = DN_K0[s] * P, DN_TILES[s]
                            load_at(L, U_DN[f], i, 8, 4 * o + s,
                                    one(wd[at(L * KD + 2 * i + o), :, k0:k0 + n * P]), n)
                        rows = slice(o * P // 2, (o + 1) * P // 2)
                        sp.dma_start(one(mid_o[at(L), at(i + 4 * f), rows, :].rearrange("l b k n -> (l b) k n")),
                                     one(mid[at(L), at(i + 4 * f), rows, :].rearrange("l b k n -> (l b) k n")))\
                            .then_inc(copy_out, 16)
                if f == 1:
                    for s in range(4):
                        w = (a["ffn1_gate"], a["ffn1_up"])[s % 2]
                        load_at(L, NU, 0, 0, s, one(w[at(L * KF + KF + s // 2), :, :]), UT)

            def store_kv(L, n):
                kind, g, c = COLS[KV_UNITS[n]]
                name = ("a1", "a2", "a3", "b")[g]
                kv = 0 if kind == "k" else 1
                heads = P * c
                sp.wait_ge(kvtok_done, L * 14 + n + 1)
                if kind == "k":
                    nk = K_UNITS.index(KV_UNITS[n])
                    src, done = kst[:, nk % 2, 0:2 * P].rearrange("p (t f) -> p t f", t=2), kst_out[nk % 2]
                    parts = [(slice(0, NB), kst[0:NB * NT, nk % 2, 2 * P:3 * P])]
                else:
                    cols = slice(v_slot(g, c) * P, (v_slot(g, c) + 1) * P)
                    src, done = vtok[:, :, cols], v_out
                    parts = [(slice(4 * half, 4 * half + 4), vnew[:, half, cols]) for half in range(2)]
                t0 = 0 if g in (1, 2) else 1
                dst = a[f"new_{name}_prompt"].rearrange("l n (t p) v h d -> l p (n t) v (h d)", p=P)
                dst = dst[at(L), :, :, kv, heads:heads + P].rearrange("l p t f -> (l p) t f")
                sp.dma_start(dst, src[:, t0:2, :]).then_inc(done, 16)
                dst = a[f"new_{name}_sample"]
                w = dst.shape[2]
                dst = dst[:, :, w - NT:w, :, :, :].rearrange("l b t v h d -> l b t v (h d)")
                for batches, new in parts:
                    to = dst[at(L), batches, :, kv, heads:heads + P].rearrange("l b t f -> (l b) t f")
                    sp.dma_start(to, new).then_inc(done, 16)

            def mixer_loads(L):
                w_in, w_br, w_out = a["w_in"], a["w_branch"], a["w_out"]
                for v in range(N_IN + 2 * KD):
                    if v < N_IN:
                        load_at(L, U_IN, 0, 0, v, one(w_in[at(L * N_IN + v), :, :]), UT)
                    elif v < N_IN + KD:
                        load_at(L, U_IN, 0, 0, v, one(w_br[at(L * KD + v - N_IN), :, :]), BR_TILES)
                    else:
                        load_at(L, U_IN, 0, 0, v, one(w_out[at(L * KD + v - N_IN - KD), :, :]), UT)
                    if v == 8:
                        sp.wait_ge(unit_used, L * NU + RING + U_IN)
                        sp.dma_start(vb[:, :, :], vpre_b(L)).then_inc(vb_in, 16)
                    for n in range(N_KV):
                        if KV_PLACE[n] == v:
                            if n == 0:
                                src = a["kcache_b"][at(L), :, :]
                            elif n <= 2 * CT:
                                src = kpre[at(L * 2 * CT + n - 1), :, :]
                            else:
                                src = vpre[at(L * 2 * CT + n - 1 - 2 * CT), :, :]
                            if n >= KV_RING:
                                sp.wait_ge(kvc_used, L * N_KV + n - KV_RING + 1)
                            sp.dma_start(kvc[:, n % KV_RING, :], one(src)).then_inc(kvc_in[n % KV_RING], 16)
                    for n, u in enumerate(KV_UNITS):
                        if u + 8 == v:
                            store_kv(L, n)
                    if 14 <= v < 22:
                        name, rows = ("a1", "b")[v % 2], slice((v - 14) // 2 * P // 4, ((v - 14) // 2 + 1) * P // 4)
                        src = a[f"cache_{name}"][:, :, NT:, :, :, :].rearrange(
                            "l b w v h d -> l b (w v h d)").rearrange("l b (k n) -> l k b n", k=P)
                        to = a[f"new_{name}_sample"][:, :, :P - NT, :, :, :].rearrange(
                            "l b w v h d -> l b (w v h d)").rearrange("l b (k n) -> l k b n", k=P)
                        sp.dma_start(to[at(L), rows, :, :].rearrange("l k b n -> (l k) b n"),
                                     src[at(L), rows, :, :].rearrange("l k b n -> (l k) b n")).then_inc(copy_out, 16)
                sp.wait_ge(v_out, (L + 1) * (7 * 48))
                plain(sp)
                sp.wait_ge(kst_out[0], (L + 1) * (4 * 32))
                plain(sp)
                sp.wait_ge(kst_out[1], (L + 1) * (3 * 32))
                plain(sp)

            def vpre_b(L):
                return a["vcache_b"][at(L), :, :, :].rearrange("l p b f -> (l p) b f")

            sp.dma_start(gains[:, :, :], a["gains"]).then_inc(gains_in, 16)
            for part, n in LOADS:
                if part == "x":
                    m = slice(n * KD // XPARTS, (n + 1) * KD // XPARTS)
                    sp.dma_start(x[:, m, :], a["x"][:, m, :]).then_inc(x_in[n], 16)
                else:
                    w = (a["ffn1_gate"], a["ffn1_up"])[n % 2]
                    sp.dma_start(raw[:, n, :], w[n // 2, :, :]).then_inc(raw_in[n], 16)
            sp.dma_start(const[:, :], a["const"]).then_inc(const_in, 16)
            sp.dma_start(sinks[:, :, :], a["sinks"]).then_inc(const_in, 16)
            with sp.Fori(0, DEPTH) as L:
                ffn_loads(L, 0)
                mixer_loads(L)
                ffn_loads(L, 1)
            for n in range(XPARTS):
                m = slice(n * KD // XPARTS, (n + 1) * KD // XPARTS)
                sp.wait_ge(y_done, m.stop)
                sp.dma_start(a["y"][:, m, :], x[:, m, :]).then_inc(y_out, 16)
            sp.wait_ge(y_out, 16 * XPARTS)
            sp.wait_ge(copy_out, 16 * DEPTH * (4 * 2 * NB + 2 * KD + 4 * 2))
            sp.wait_ge(v_out, DEPTH * 7 * 48)
            sp.wait_ge(kst_out[0], DEPTH * 4 * 32)
            sp.wait_ge(kst_out[1], DEPTH * 3 * 32)

        @block.tensor
        def _(pe):
            def product(out, slot, tile, hi, lo, first, last):
                w0, w1 = (w[:, slot, tile * P:(tile + 1) * P] for w in (whi, wlo))
                pe.matmul(out, w0, hi, start=first, stop=False)
                pe.matmul(out, w0, lo, start=False, stop=False)
                return pe.matmul(out, w1, hi, start=False, stop=last)

            def sum_squares(n):
                pe.wait_ge(ssq_done, (n + 1) * (KD + 1))
                pe.matmul(ps[:, BK_O, 0:TOK], ones[:, :], ssq[:, :], start=True, stop=True).then_inc(ms_ready, 1)

            def first_units(L, base, norm, bank):
                outs = []
                for s in range(2):
                    pe.wait_ge(wlo_done, L * NU + base + s + RAW + 1)
                    outs.append(bank(s))
                    for k in range(KD - 1):
                        if s == 0:
                            pe.wait_ge(xs_ready, norm * KD + k + 1)
                        product(outs[s], s, k, xhi[:, k, :], xlo[:, k, :], k == 0, False)
                        if s == 1 and k == 2:
                            sum_squares(norm)
                pe.wait_ge(xs_ready, (norm + 1) * KD)
                for s in range(2):
                    product(outs[s], s, KD - 1, xhi[:, KD - 1, :], xlo[:, KD - 1, :], False, True)\
                        .then_inc(unit_used, 1)

            def ffn_products(L, f):
                def gate_up(i, units):
                    for s in units:
                        pe.wait_ge(wlo_done, L * NU + i * 4 + U_GU[f] + s + RAW + 1)
                        pe.wait_ge(taken, L * NR + i * 4 + R_GU[f] + s + 1)
                        for k in range(KD):
                            mm = product(ps[:, s, 0:TOK], s, k, xhi[:, k, :], xlo[:, k, :], k == 0, k == KD - 1)
                        mm.then_inc(unit_used, 1)

                def first_gate_up(s):
                    pe.wait_ge(taken, L * NR + R_GU[f] + s + 1)
                    return ps[:, s, 0:TOK]

                def down(i, first):
                    for o in range(2):
                        pe.wait_ge(taken, L * NR + i * 2 + R_DN[f] + o + RING - 1)
                        for s in range(4):
                            pe.wait_ge(wlo_done, L * NU + i * 8 + U_DN[f] + 4 * o + s + RAW + 1)
                            for n in range(DN_TILES[s]):
                                k = DN_K0[s] + n
                                if first and o == 0:
                                    pe.wait_ge(actlo_done, L * 2 * KF + f * KF + 2 + k + 1)
                                mm = product(ps[:, BK_DN + o, 0:TOK], s, n, act_hi[:, k, :], act_lo[:, k, :],
                                             k == 0, k == KF - 1)
                            mm.then_inc(unit_used, 1)

                first_units(L, U_GU[f], L * 3 + 2 * f, first_gate_up)
                gate_up(0, (2, 3))
                with pe.Fori(1, KF // 2) as i:
                    gate_up(i, range(4))
                down(0, True)
                with pe.Fori(1, KD // 2) as i:
                    down(i, False)

            def mixer_products(L):
                def scores(i):
                    kind, h, t = ITEMS[i]
                    if i >= 1:
                        pe.wait_ge(s_masked, L * NI + (SA0 if i == SA0 + 2 else i))
                    if i == 0:
                        pe.wait_ge(rope_done, L * 17 + 5)
                        pe.wait_ge(qb_done, L + 1)
                        kvc_wait(pe, L, 0)
                    if kind == "B":
                        n = P * (t + 1)
                        for j in range(2):
                            r = slice(HD * j, HD * (j + 1))
                            mm = pe.matmul(ps[:, BK_S + j, 0:n], qk[r, 1 + h, t * P:(t + 1) * P], qk[r, 0, 0:n],
                                           start=True, stop=True)
                    elif kind == "A":
                        pe.wait_ge(rope_done, L * 17 + 17)
                        n = P * (t + 1)
                        r = slice(HD * (h % 2), HD * (h % 2 + 1))
                        for g in range(NG):
                            bank, col = divmod(g * n, 512)
                            mm = pe.matmul(ps[:, BK_S + bank, col:col + n],
                                           qk[r, qk_slot("q", g, h // 2), t * P:(t + 1) * P],
                                           qk[r, qk_slot("k", g, h // 2), 0:n], start=True, stop=True)
                    else:
                        plain(pe)
                        new = slice(SEQ + HALF * h, SEQ + HALF * (h + 1))
                        for j in range(2):
                            r = slice(HD * j, HD * (j + 1))
                            for b in range(4):
                                t0 = P * h + HALF * b
                                mm = pe.matmul(ps[HALF * b:HALF * (b + 1), BK_S + j, 0:P], sts[r, t0:t0 + HALF],
                                               kvc[r, 0, (4 * h + b) * P:(4 * h + b + 1) * P], start=True, stop=True)
                        if h == 1:
                            mm.then_inc(kvc_used, 1)
                        for j in range(2):
                            r = slice(HD * j, HD * (j + 1))
                            for b in range(4):
                                t0 = P * h + HALF * b
                                mm = pe.matmul(ps[HALF * b:HALF * (b + 1), BK_S + j, P:P + HALF],
                                               sts[r, t0:t0 + HALF], qk[r, 0, new], start=True, stop=True)
                    mm.then_inc(s_scores, 1)

                def transposes(i):
                    kind, h, t = ITEMS[i]
                    pe.wait_ge(s_norm, L * NI + i + 1)
                    if i >= 1:
                        pe.wait_ge(s_pts, L * NI + i)
                    if kind in ("A", "SA"):
                        pe.wait_ge(kvtok_done, L * 14 + before("R", ("T", i)))
                    eb = e[:, i % 2, :]
                    if kind in ("A", "B"):
                        for n in range((NG if kind == "A" else 2) * (t + 1)):
                            mm = pe.transpose(ps[:, BK_T + n // 4, n % 4 * P:(n % 4 + 1) * P],
                                              eb[:, n * P:(n + 1) * P], ident)
                    else:
                        for n in range(2 if kind == "SB" else NG):
                            o = n * N_SB if kind == "SB" else n * P
                            on = n * N_SB + P if kind == "SB" else NG * P + n * HALF
                            pe.transpose(ps[:, BK_T, n * P:(n + 1) * P], eb[:, o:o + P], ident)
                            mm = pe.transpose(ps[0:HALF, *new_place(kind, n, 1)], eb[:, on:on + HALF], ident)
                    mm.then_inc(s_pt, 1)

                def values(i):
                    kind, h, t = ITEMS[i]
                    pe.wait_ge(s_pts, L * NI + i + 1)
                    if kind != "SA" and i >= 1:
                        pe.wait_ge(s_olo, L * NI + OUT_ORDER.index(i))
                    pb, nb = pts[:, i % 2, :], ptn[:, i % 2, :]
                    if kind == "B":
                        pe.wait_ge(kvtok_done, L * 14 + 2)
                        for kt in range(t + 1):
                            for j in range(2):
                                n = j * (t + 1) + kt
                                mm = pe.matmul(ps[HD * j:HD * (j + 1), BK_O, 0:P],
                                               vtok[:, kt, 6 * P + HD * j:6 * P + HD * (j + 1)],
                                               pb[:, n * P:(n + 1) * P], start=kt == 0, stop=kt == t)
                        mm.then_inc(s_pv, 1)
                    elif kind == "A":
                        pe.wait_ge(kvtok_done, L * 14 + 14)
                        for g in range(NG):
                            for kt in range(t + 1):
                                n = g * (t + 1) + kt
                                f0 = v_slot(g, h // 2) * P + HD * (h % 2)
                                mm = pe.matmul(ps[HD * (h % 2):HD * (h % 2 + 1), BK_O, 0:P],
                                               vtok[:, kt, f0:f0 + HD], pb[:, n * P:(n + 1) * P],
                                               start=n == 0, stop=n == NG * (t + 1) - 1)
                        mm.then_inc(s_pv, 1)
                    elif kind == "SB":
                        pe.wait_ge(vb_in, L * 16 + 16)
                        pe.wait_ge(kvtok_done, L * 14 + 2)
                        for j in range(2):
                            r = slice(HD * j, HD * (j + 1))
                            pe.matmul(ps[r, BK_O, 0:P], vnew[:, h, 6 * P + HD * j:6 * P + HD * (j + 1)],
                                      nb[:, j * P:(j + 1) * P], start=True, stop=False)
                            for b in range(4):
                                cols = slice(j * P + HALF * b, j * P + HALF * (b + 1))
                                mm = pe.matmul(ps[r, BK_O, HALF * b:HALF * (b + 1)], vb[:, 4 * h + b, r],
                                               pb[:, cols], start=False, stop=b == 3)
                        mm.then_inc(s_pv, 1)
                    else:
                        pe.wait_ge(s_masked, L * NI + SA0 + 2)
                        pe.wait_ge(kvtok_done, L * 14 + 14)
                        plain(pe)
                        for g in range(NG):
                            for b in range(4):
                                mm = pe.matmul(ps[HALF * b:HALF * (b + 1), BK_KV, 2 * P * h:2 * P * (h + 1)],
                                               nb[:, g * P + HALF * b:g * P + HALF * (b + 1)],
                                               vnew[:, h, v_slot(g, 0) * P:(v_slot(g, 0) + 2) * P],
                                               start=g == 0 and h == 0, stop=False, skip_group_check=True)
                        mm.then_inc(s_new, 1)

                def cached_keys(n):
                    half, i = divmod(n - 1, CT)
                    g = 0 if i == 0 else 1 if i < 5 else 2

                    def q(b, j, c):
                        return qm[:, b, j, 2 * NT * c:2 * NT * c + HALF]

                    kvc_wait(pe, L, n)
                    if i == 0:
                        pe.wait_ge(qm_done, L * 2 + half + 1)
                    if i == CT - 1 and half == 0:
                        pe.wait_ge(rope_done, L * 17 + 17)
                    if i == 0:
                        if half == 1:
                            pe.wait_ge(sts_done, L + 1)
                    new = slice(SEQ + HALF * half, SEQ + HALF * (half + 1))
                    if i == CT - 1:
                        for gn in range(NG):
                            for c in range(2):
                                for b in range(4):
                                    pe.matmul(ps[HALF * b:HALF * (b + 1), BK_KV,
                                                 NG * P + gn * HALF:NG * P + (gn + 1) * HALF],
                                              q(b, K_FULL[gn], c), qk[:, qk_slot("k", gn, c), new],
                                              start=False, stop=False, skip_group_check=True)
                    for c in range(2):
                        for b in range(4):
                            mm = pe.matmul(ps[HALF * b:HALF * (b + 1), BK_KV, g * P:(g + 1) * P], q(b, i, c),
                                           kvc[:, n % KV_RING, (4 * c + b) * P:(4 * c + b + 1) * P],
                                           start=i == 0 and c == 0, stop=i == CT - 1 and c == 1,
                                           skip_group_check=True)
                    mm.then_inc(kvc_used, 1)

                def cached_values(n):
                    half, i = divmod(n - 1 - 2 * CT, CT)
                    kvc_wait(pe, L, n)
                    if half == 1 and i == 0:
                        pe.wait_ge(osb_done, L * 2 + 1)
                    for b in range(4):
                        mm = pe.matmul(ps[HALF * b:HALF * (b + 1), BK_KV, 2 * P * half:2 * P * (half + 1)],
                                       pm[:, half, b, i, :],
                                       kvc[:, n % KV_RING, 2 * P * b:2 * P * (b + 1)],
                                       start=False, stop=i == CT - 1, skip_group_check=True)
                    mm.then_inc(kvc_used, 1)

                def output_rows(i):
                    pe.wait_ge(osb_done, L * 2 + ITEMS[i][1] + 1)
                    pe.wait_ge(s_olo, L * NI + OUT_ORDER.index(i))
                    for c in range(2):
                        mm = pe.transpose(ps[:, BK_O, c * P:(c + 1) * P], osb[:, c * P:(c + 1) * P], ident)
                    mm.then_inc(s_pv, 1)

                def token_rows(u):
                    n = KV_UNITS.index(u)
                    if COLS[u][0] == "k":
                        src = qk[:, qk_slot(*COLS[u]), :]
                        pe.wait_ge(rope_done, L * 17 + QK_UNITS.index(u) + 1)
                    else:
                        src = t1[:, u % 2, :]
                        pe.wait_ge(t1_done, L * N_IN + u + 1)
                    if n >= 1:
                        pe.wait_ge(kvtok_done, L * 14 + n)
                    if not skips_first_rows(u):
                        pe.transpose(ps[:, BK_ROWS, 0:P], src[:, 0:P], ident)
                    pe.transpose(ps[:, BK_ROWS, P:2 * P], src[:, P:2 * P], ident)
                    if COLS[u][0] == "k":
                        pe.transpose(ps[0:NB * NT, BK_ROWS, 2 * P:3 * P], src[:, SEQ:TOK], ident)\
                            .then_inc(kvt_done, 1)
                        return
                    pe.transpose(ps[0:HALF, BK_ROWS, 2 * P:3 * P], src[:, SEQ:SEQ + HALF], ident)
                    pe.transpose(ps[0:HALF, BK_ROWS, 3 * P:4 * P], src[:, SEQ + HALF:TOK], ident).then_inc(kvt_done, 1)

                pe.wait_ge(const_in, 32)
                for kind, n in STEPS:
                    if kind == "U" and n == 0:
                        first_units(L, U_IN, L * 3 + 1, lambda s: ps[:, s, 0:TOK])
                    elif kind == "U" and n > 1:
                        pe.wait_ge(wlo_done, L * NU + U_IN + n + RAW + 1)
                        pe.wait_ge(zs_done, L * N_IN + n - 1)
                        for k in range(KD):
                            mm = product(ps[:, n % 2, 0:TOK], n % RING, k, xhi[:, k, :], xlo[:, k, :], k == 0, k == KD - 1)
                            if k == KD // 2 - 1 and n in INNER:
                                (cached_keys if INNER[n] <= 2 * CT else cached_values)(INNER[n])
                        mm.then_inc(unit_used, 1)
                    elif kind == "R":
                        token_rows(n)
                    elif kind == "S" and ITEMS[n][0] != "SA":
                        scores(n)
                    elif kind == "T":
                        transposes(n)
                    elif kind == "O":
                        values(n)
                    elif kind == "K" and n not in INNER.values():
                        cached_keys(n)
                    elif kind == "V" and n not in INNER.values():
                        cached_values(n)
                    elif kind == "X":
                        output_rows(n)
                for m in range(KD):
                    ba, bb = BK_BR[m % 2]
                    pe.wait_ge(wlo_done, L * NU + U_BR + m + RAW + 1)
                    if m == 0:
                        pe.wait_ge(s_olo, L * NI + NI)
                        pe.wait_ge(zs_done, L * N_IN + N_IN)
                    else:
                        pe.wait_ge(taken, L * NR + R_BR + m + RING - 1)
                    for k in range(BR_TILES):
                        out = ps[:, ba if k < 2 else bb, 0:TOK]
                        mm = product(out, m % RING, k, ohi[:, k, :], olo[:, k, :], k in (0, 2), k in (1, 5))
                    mm.then_inc(unit_used, 1)
                def w_out(m, ks):
                    for k in ks:
                        mm = product(ps[:, BK_WO + m % 2, 0:TOK], m % RING, k, mhi[:, k, :], mlo[:, k, :],
                                     k == 0, k == KD - 1)
                    return mm

                for m in range(KD):
                    if m != 1:
                        pe.wait_ge(wlo_done, L * NU + U_WO + m + RAW + 1)
                    if m >= 2:
                        pe.wait_ge(taken, L * NR + R_WO + m + RING - 1)
                        w_out(m, range(KD)).then_inc(unit_used, 1)
                    if m == 0:
                        pe.wait_ge(mlo_done, L * KD + KD - 1)
                        w_out(0, range(KD - 1))
                        pe.wait_ge(wlo_done, L * NU + U_WO + 1 + RAW + 1)
                        w_out(1, range(KD - 1))
                        pe.wait_ge(mlo_done, L * KD + KD)
                        for o in range(2):
                            w_out(o, (KD - 1,)).then_inc(unit_used, 1)

            pe.wait_ge(set_up, 2)
            with pe.Fori(0, DEPTH) as L:
                ffn_products(L, 0)
                mixer_products(L)
                ffn_products(L, 1)
            sum_squares(3 * DEPTH)

        @block.scalar
        def _(act):
            def round_unit(L, base, i, step, s, tiles):
                act.wait_ge(unit_used, L * NU + i * step + base + s + 1)
                act.wait_ge(raw_in[(base + s) % RAW], (L * (NU // RAW) + i * (step // RAW) + (base + s) // RAW + 1) * 16)
                nc.scalar.activation(whi[:, (base + s) % RING, 0:tiles * P], raw[:, (base + s) % RAW, 0:tiles * P],
                                     ACT.Copy).then_inc(whi_done, 1)

            def root(n):
                act.wait_ge(ms_ready, n + 1)
                nc.scalar.activation(rms[:, :], ps[:, BK_O, 0:TOK], ACT.Sqrt, bias=eps[:, :], scale=1.0 / D)\
                    .then_inc(rms_done, 1)

            def round_x(norm, m, slot):
                act.wait_ge(xg_ready, norm * KD + m + 1)
                dst = xhi[:, m, :] if isinstance(m, int) else xhi[:, at(m), :].rearrange("p o n -> p (o n)")
                nc.scalar.activation(dst, xg[:, slot, :], ACT.Copy).then_inc(xhi_done, 1)

            def ffn_act(L, f):
                def gate_up(i, first, tiles):
                    if first:
                        root(L * 3 + 2 * f)
                    for s in range(4):
                        if s % 2 == 0:
                            act.wait_ge(taken, L * NR + i * 4 + R_GU[f] + s + RING + 1)
                            nc.scalar.activation(gate_s[:, s // 2, :], gate_s[:, s // 2, :], ACT.Silu)\
                                .then_inc(silu_done, 1)
                        round_unit(L, U_GU[f] + 4, i, 4, s, tiles[s])
                        if s % 2 == 1:
                            act.wait_ge(prod_done, L * 2 * KF + i * 2 + f * KF + s // 2 + 1)
                            j = i * 2 + s // 2
                            dst = act_hi[:, j, :] if isinstance(j, int) else \
                                act_hi[:, at(j), :].rearrange("p o n -> p (o n)")
                            nc.scalar.activation(dst, up_s[:, s // 2, :], ACT.Copy).then_inc(acthi_done, 1)

                def down(i, tail):
                    for o in range(2):
                        for s in range(4):
                            round_unit(L, U_DN[f] + 4, i, 8, 4 * o + s,
                                       UT if o == 1 and tail == "next" else DN_TILES[s])
                        round_x(L * 3 + 1 + 2 * f, i * 2 + o, o)

                gate_up(0, True, (UT,) * 4)
                with act.Fori(1, KF // 2 - 1) as i:
                    gate_up(i, False, (UT,) * 4)
                gate_up(KF // 2 - 1, False, DN_TILES)
                with act.Fori(0, KD // 2 - 1) as i:
                    down(i, "same")
                down(KD // 2 - 1, "next")

            def mixer_act(L):
                act.wait_ge(const_in, 32)
                for kind, n in STEPS:
                    if kind == "U":
                        if n == 0:
                            root(L * 3 + 1)
                        act.wait_ge(unit_used, L * NU + U_IN + n + RING + 1)
                        if n >= 2:
                            act.wait_ge(t1_done, L * N_IN + n - 1)
                            if n - 2 in QK_UNITS:
                                act.wait_ge(shuf_done, L * 17 + QK_UNITS.index(n - 2) + 1)
                        nc.scalar.activation(zs[:, n % 2, :], ps[:, n % 2, 0:TOK], ACT.Copy).then_inc(zs_done, 1)
                        round_unit(L, U_IN + 4, 0, 0, n, UT if n + 4 < N_IN else BR_TILES)
                    elif kind == "R":
                        g, c = COLS[n][1:]
                        act.wait_ge(kvt_done, L * 14 + KV_UNITS.index(n) + 1)
                        if COLS[n][0] == "k":
                            nk = K_UNITS.index(n)
                            if nk >= 2:
                                tot = (4 * 32, 3 * 32)[nk % 2]
                                act.wait_ge(kst_out[nk % 2], L * tot + 32 * (nk // 2))
                            to, new = kst[:, nk % 2, 0:2 * P], kst[0:NB * NT, nk % 2, 2 * P:3 * P]
                            t0 = P if skips_first_rows(n) else 0
                            nc.scalar.activation(to[:, t0:2 * P], ps[:, BK_ROWS, t0:2 * P], ACT.Copy)
                            nc.scalar.activation(new, ps[0:NB * NT, BK_ROWS, 2 * P:3 * P], ACT.Copy)\
                                .then_inc(kvtok_done, 1)
                        else:
                            v0 = v_slot(g, c) * P
                            nc.scalar.activation(vtok[:, :, v0:v0 + P],
                                                 ps[:, BK_ROWS, 0:2 * P].rearrange("p (t f) -> p t f", t=2), ACT.Copy)
                            nc.scalar.activation(vnew[:, :, v0:v0 + P],
                                                 ps[0:HALF, BK_ROWS, 2 * P:4 * P].rearrange("p (t f) -> p t f", t=2),
                                                 ACT.Copy).then_inc(kvtok_done, 1)
                    elif kind == "G":
                        k = G_UNITS.index(n)
                        act.wait_ge(t1_done, L * N_IN + n + 1)
                        nc.scalar.activation(gate[:, k, :], t1[:, n % 2, :], ACT.Tanh, scale=0.5).then_inc(gtanh_done, 1)
                    elif kind == "S":
                        what, h, t = ITEMS[n]
                        w, segs = segments(n)
                        act.wait_ge(s_masked, L * NI + n + 1)
                        for j in range(segs):
                            mm = nc.scalar.activation(e[:, n % 2, j * w:(j + 1) * w], e[:, n % 2, j * w:(j + 1) * w],
                                                      ACT.Exp, bias=nmx[:, n % 2, j:j + 1], scale=SCALE,
                                                      accum_out=den[:, n % 2, j:j + 1])
                            if segs == 2:
                                col = h + 4 * j if what == "B" else 8 + j
                                sink = sinks[:, at(L), col:col + 1].rearrange("p o n -> p (o n)")
                                mm = nc.scalar.activation(esk[:, n % 2, j:j + 1], nmx[:, n % 2, j:j + 1], ACT.Exp,
                                                          bias=sink)
                        mm.then_inc(s_exp, 1)
                    elif kind == "T":
                        what, h, t = ITEMS[n]
                        act.wait_ge(s_pt, L * NI + n + 1)
                        wait_slot_used(act, L, n)
                        if what in ("A", "B"):
                            w = (NG if what == "A" else 2) * (t + 1) * P
                        else:
                            w = (NG if what == "SA" else 2) * P
                            if what == "SA" and h == 0:
                                act.wait_ge(pm_zero, L + 1)
                            nc.scalar.activation(ptn[:, n % 2, 0:w], ps[0:HALF, *new_place(what, 0, w // P)],
                                                 ACT.Copy)
                        if what == "SA":
                            src = ps[:, BK_T, :]
                            by_tile = ((0, ((CT * HALF, 4), (1, HALF))),
                                       (HALF, ((CT * HALF, 4), (4, 2 * 4), (HALF + 1, 4))),
                                       (5 * HALF, ((CT * HALF, 4), (NT, 4), (HALF + 1, NT))))
                            for g, (offset, dims) in enumerate(by_tile):
                                shape = dict(b=4) if g == 0 else dict(b=4, h=dims[1][1])
                                part = src[:, g * P:(g + 1) * P].rearrange(
                                    "p (b n) -> p b n" if g == 0 else "p (b h n) -> p b h n", **shape)
                                mm = nc.scalar.activation(
                                    strided(qm_mem[:, :], h * 4 * CT * HALF + offset, dims), part, ACT.Copy)
                            mm.then_inc(s_pts, 1)
                        else:
                            flat = ps[:, BK_T:BK_T + 2, :].rearrange("p b n -> p (b n)")
                            nc.scalar.activation(pts[:, n % 2, 0:w], flat[:, 0:w], ACT.Copy).then_inc(s_pts, 1)
                    elif kind == "E":
                        act.wait_ge(kvc_used, L * N_KV + 1 + CT)
                        nc.scalar.activation(sts[:, :], ps[:, BK_KV, 0:N_SA], ACT.Copy).then_inc(sts_done, 1)
                    elif kind == "Y":
                        act.wait_ge(kvc_used, L * N_KV + 1 + (3 + ITEMS[n][1]) * CT)
                        if ITEMS[n][1] == 1:
                            act.wait_ge(s_pv, L * NI + OUT_ORDER.index(SA0) + 1)
                        f0 = 2 * P * ITEMS[n][1]
                        nc.scalar.activation(osb[:, :], ps[:, BK_KV, f0:f0 + 2 * P], ACT.Copy).then_inc(osb_done, 1)
                    elif kind == "W":
                        act.wait_ge(s_pv, L * NI + OUT_ORDER.index(n) + 1)
                        if ITEMS[n][0] == "SA":
                            for hh in range(2):
                                to, src = out_halves(ITEMS[n][1], hh, ohi)
                                mm = nc.scalar.activation(to, src, ACT.Copy)
                        else:
                            to, src = out_place(n, ohi)
                            mm = nc.scalar.activation(to, src, ACT.Copy)
                        mm.then_inc(s_ohi, 1)
                for m in range(KD):
                    round_unit(L, U_BR + 4, 0, 0, m, BR_TILES if m < 4 else UT)
                    act.wait_ge(mab_done, L * KD + m + 1)
                    nc.scalar.activation(mhi[:, m, :], ma[:, m % 2, :], ACT.Copy).then_inc(mhi_done, 1)
                for m in range(KD):
                    round_unit(L, U_WO + 4, 0, 0, m, UT)
                    round_x(L * 3 + 2, m, m % 2)

            for m in range(KD):
                round_x(0, m, m % 2)
                if m in START_UNITS:
                    round_unit(0, 0, 0, 0, START_UNITS.index(m), UT)
            act.wait_ge(set_up, 2)
            with act.Fori(0, DEPTH) as L:
                ffn_act(L, 0)
                mixer_act(L)
                ffn_act(L, 1)
            root(3 * DEPTH)

        @block.vector
        def _(dve):
            def rest_unit(L, base, i, step, s, tiles):
                dve.wait_ge(whi_done, L * NU + i * step + base + s + 1)
                nc.vector.tensor_tensor(wlo[:, (base + s) % RING, 0:tiles * P], raw[:, (base + s) % RAW, 0:tiles * P],
                                        whi[:, (base + s) % RING, 0:tiles * P].bitcast(F32), ALU.subtract)\
                    .then_inc(wlo_done, 1)

            def chunk(t, m):
                return t[:, m, :] if isinstance(m, int) else t[:, at(m), :].rearrange("p o n -> p (o n)")

            def gain(norm, m):
                if isinstance(norm, int) and isinstance(m, int):
                    return gains[:, norm, m:m + 1]
                g = gains[:, :, :].rearrange("p n k -> p (n k)")
                return g[:, at(norm * KD + m)]

            def scale_x(norm, m, slot):
                nc.vector.tensor_scalar(xg[:, slot, :], chunk(x, m), gain(norm, m), None, ALU.mult)\
                    .then_inc(xg_ready, 1)

            def rest_x(norm, m, slot):
                dve.wait_ge(xhi_done, norm * KD + m + 1)
                nc.vector.tensor_tensor(chunk(xlo, m), xg[:, slot, :], chunk(xhi, m).bitcast(F32), ALU.subtract)\
                    .then_inc(xs_ready, 1)

            def invert(n):
                dve.wait_ge(rms_done, n + 1)
                nc.vector.reciprocal(rinv[:, :], rms[:, :]).then_inc(rinv_ready, 1)
                dve.wait_ge(rinv_ready, n + 1)

            def add_to_x(L, bank, m, result, factor):
                nc.vector.scalar_tensor_tensor(chunk(x, m), ps[:, bank, 0:TOK], factor, chunk(x, m),
                                               ALU.mult, ALU.add).then_inc(taken, 1)
                dve.wait_ge(taken, L * NR + result + RING + 1)

            def ffn_vec(L, f):
                def gate_up(i, first, tiles):
                    if first:
                        invert(L * 3 + 2 * f)
                    for s in range(4):
                        dve.wait_ge(unit_used, L * NU + i * 4 + U_GU[f] + s + RING + 1)
                        if s % 2 == 0:
                            dve.wait_ge(actlo_done, L * 2 * KF + i * 2 + f * KF + s // 2 + 1)
                        nc.vector.tensor_tensor((gate_s, up_s)[s % 2][:, s // 2, :], ps[:, s, 0:TOK], rinv[:, :],
                                                ALU.mult).then_inc(taken, 1)
                        rest_unit(L, U_GU[f] + 4, i, 4, s, tiles[s])

                def down(i, tail):
                    norm = L * 3 + 1 + 2 * f
                    for o in range(2):
                        for s in range(4):
                            if s == 3:
                                dve.wait_ge(unit_used, L * NU + i * 8 + U_DN[f] + 4 * o + s + RING + 1)
                                add_to_x(L, BK_DN + o, i * 2 + o, i * 2 + R_DN[f] + o, 0.5)
                                scale_x(norm, i * 2 + o, o)
                            rest_unit(L, U_DN[f] + 4, i, 8, 4 * o + s,
                                      UT if o == 1 and tail == "next" else DN_TILES[s])
                        rest_x(norm, i * 2 + o, o)

                gate_up(0, True, (UT,) * 4)
                with dve.Fori(1, KF // 2 - 1) as i:
                    gate_up(i, False, (UT,) * 4)
                gate_up(KF // 2 - 1, False, DN_TILES)
                with dve.Fori(0, KD // 2 - 1) as i:
                    down(i, "same")
                down(KD // 2 - 1, "next")

            def mixer_vec(L):
                dve.wait_ge(const_in, 32)
                def finish_gate(k):
                    dve.wait_ge(gtanh_done, L * 16 + k + 1)
                    nc.vector.tensor_scalar(gate[:, k, :], gate[:, k, :], 0.5, 0.5, ALU.mult, ALU.add)\
                        .then_inc(gate_ready, 1)

                shuffle = [p + 8 if p < 8 else p - 8 if p < 16 else p for p in range(32)]
                for kind, n in STEPS:
                    b = n % 2
                    if kind == "U":
                        if n == 0:
                            invert(L * 3 + 1)
                            nc.vector.tensor_tensor(cosr[:, :], const[:, C_COS:C_COS + TOK], rinv[:, :], ALU.mult)\
                                .then_inc(tabs_ready, 1)
                            nc.vector.tensor_tensor(sinr[:, :], const[:, C_SIN:C_SIN + TOK], rinv[:, :], ALU.mult)\
                                .then_inc(tabs_ready, 1)
                        if n in QK_UNITS:
                            k = QK_UNITS.index(n)
                            dve.wait_ge(zs_done, L * N_IN + n + 1)
                            if k >= 1:
                                dve.wait_ge(rope_done, L * 17 + k)
                            plain(dve)
                            nc.vector.stream_shuffle(sh[:, :], zs[:, b, :], shuffle).then_inc(shuf_done, 1)
                            dve.wait_ge(shuf_done, L * 17 + k + 1)
                            if k == 0:
                                dve.wait_ge(tabs_ready, L * 2 + 2)
                            nc.vector.tensor_tensor(sh[:, :], sh[:, :], sinr[:, :], ALU.mult).then_inc(shs_done, 1)
                            dve.wait_ge(shs_done, L * 17 + k + 1)
                            dve.wait_ge(t1_done, L * N_IN + n + 1)
                            nc.vector.tensor_tensor(qk[:, qk_slot(*COLS[n]), :], t1[:, b, :], sh[:, :], ALU.add)\
                                .then_inc(rope_done, 1)
                            if COLS[n] == ("q", 3, 3):
                                dve.wait_ge(rope_done, L * 17 + k + 1)
                                nc.vector.tensor_copy(
                                    sts[:, 0:NB * HALF].rearrange("p (b c n) -> p b c n", b=NB, c=4),
                                    qk[:, 1:5, SEQ:TOK].rearrange("p c (b n) -> p b c n", b=NB)).then_inc(qb_done, 1)
                        rest_unit(L, U_IN + 4, 0, 0, n, UT if n + 4 < N_IN else BR_TILES)
                    elif kind == "Q":
                        dve.wait_ge(qm_zero, L + 1)
                        if n == 0:
                            dve.wait_ge(rope_done, L * 17 + 11)
                        else:
                            dve.wait_ge(kvc_used, L * N_KV + 1 + CT)
                        new = slice(SEQ + HALF * n, SEQ + HALF * (n + 1))
                        step_b, step_j = N_QM * 6 * NT, 6 * NT
                        for c in range(2):
                            for hh in range(2):
                                r = slice(HD * hh, HD * (hh + 1))
                                f0 = 4 * NT * c + NT * hh
                                to = qm[r, :, :, :].rearrange("p b j n -> p (b j n)")
                                for g in range(NG):
                                    src = qk[r, qk_slot("q", g, c), new]
                                    nc.vector.tensor_copy(qm[r, :, K_FULL[g], f0:f0 + NT],
                                                          src.rearrange("p (b n) -> p b n", b=4))
                                src = qk[r, qk_slot("q", 1, c), new].rearrange("p (b k n) -> p b k n", b=4, k=2)
                                nc.vector.tensor_copy(
                                    strided(to, step_j + f0, ((step_b, 4), (4, 2), (step_j + 1, 4))), src)
                                src = qk[r, qk_slot("q", 2, c), new].rearrange("p (b n) -> p b n", b=4)
                                mm = nc.vector.tensor_copy(
                                    strided(to, 5 * step_j + f0, ((step_b, 4), (step_j + 1, NT))), src)
                        mm.then_inc(qm_done, 1)
                    elif kind == "G":
                        if G_UNITS.index(n) < 14:
                            finish_gate(G_UNITS.index(n))
                    elif kind == "S":
                        what, h, t = ITEMS[n]
                        w, segs = segments(n)
                        if what != "SA":
                            dve.wait_ge(s_scores, L * NSC + score_number(n) + 1)
                        elif h == 0:
                            dve.wait_ge(sts_done, L + 1)
                        else:
                            dve.wait_ge(kvc_used, L * N_KV + 1 + 2 * CT)
                        if n >= 2:
                            dve.wait_ge(s_pt, L * NI + n - 1)
                        plain(dve)
                        flat = ps[:, BK_S:BK_S + 2, :].rearrange("p b n -> p (b n)")
                        for j in range(segs):
                            to = e[:, b, j * w:(j + 1) * w]
                            src = ps[:, BK_S + j, 0:w] if segs == 2 else flat[:, 0:w]
                            if what == "B":
                                mask = const[:, C_MB + SEQ - w:C_MB + SEQ]
                            elif what == "A":
                                mask = const[:, C_MA:C_MA + NG * SEQ].rearrange("p (g k) -> p g k", g=NG)
                                mask = mask[:, :, SEQ - w // NG:SEQ]
                                to, src = (v.rearrange("p (g k) -> p g k", g=NG) for v in (to, src))
                            else:
                                c0 = C_SA if what == "SA" else C_SB
                                mask = const[:, c0:c0 + w]
                            if what == "SA":
                                src = sts[:, 0:w] if h == 0 else ps[:, BK_KV, 0:w]
                            mm = nc.vector.tensor_tensor_reduce(out=to, in0=src, in1=mask, scale=1.0, scalar=-3e38,
                                                                op0=ALU.add, op1=ALU.max,
                                                                accum_out=mx[:, b, j:j + 1])
                        mm.then_inc(s_max, 1)
                        dve.wait_ge(s_max, L * NI + n + 1)
                        nc.vector.tensor_scalar(nmx[:, b, 0:segs], mx[:, b, 0:segs], -SCALE, None, ALU.mult)\
                            .then_inc(s_masked, 1)
                    elif kind == "N":
                        w, segs = segments(n)
                        dve.wait_ge(s_exp, L * NI + n + 1)
                        if segs == 2:
                            nc.vector.tensor_tensor(den[:, b, :], den[:, b, :], esk[:, b, :], ALU.add)\
                                .then_inc(s_den, 1)
                            dve.wait_ge(s_den, L * 10 + n + 1)
                        nc.vector.reciprocal(rden[:, b, 0:segs], den[:, b, 0:segs]).then_inc(s_rden, 1)
                        dve.wait_ge(s_rden, L * NI + n + 1)
                        for j in range(segs):
                            part = e[:, b, j * w:(j + 1) * w]
                            mm = nc.vector.tensor_scalar(part, part, rden[:, b, j:j + 1], None, ALU.mult)
                        mm.then_inc(s_norm, 1)
                    elif kind == "W":
                        dve.wait_ge(s_ohi, L * NI + OUT_ORDER.index(n) + 1)
                        pairs = []
                        if ITEMS[n][0] == "SA":
                            pairs = [(out_halves(ITEMS[n][1], hh, olo), out_halves(ITEMS[n][1], hh, ohi)[0])
                                     for hh in range(2)]
                        else:
                            pairs = [(out_place(n, olo), out_place(n, ohi)[0])]
                        for (to, src), hi in pairs:
                            mm = nc.vector.tensor_tensor(to, src, hi.bitcast(F32), ALU.subtract)
                        mm.then_inc(s_olo, 1)
                for m in range(KD):
                    ba, bb = BK_BR[m % 2]
                    dve.wait_ge(unit_used, L * NU + U_BR + m + RING + 1)
                    dve.wait_ge(gate_ready, L * 16 + 2 * m + 2)
                    if m >= 2:
                        dve.wait_ge(mlo_done, L * KD + m - 1)
                    nc.vector.tensor_tensor(ma[:, m % 2, :], ps[:, ba, 0:TOK], gate[:, 2 * m, :], ALU.mult)
                    nc.vector.tensor_tensor(mb[:, m % 2, :], ps[:, bb, 0:TOK], gate[:, 2 * m + 1, :], ALU.mult)\
                        .then_inc(taken, 1)
                    rest_unit(L, U_BR + 4, 0, 0, m, BR_TILES if m < 4 else UT)
                    if m in (2, 4):
                        finish_gate(13 + m // 2)
                for m in range(KD):
                    dve.wait_ge(unit_used, L * NU + U_WO + m + RING + 1)
                    add_to_x(L, BK_WO + m % 2, m, R_WO + m, 1.0)
                    scale_x(L * 3 + 2, m, m % 2)
                    rest_unit(L, U_WO + 4, 0, 0, m, UT)
                    rest_x(L * 3 + 2, m, m % 2)

            dve.sem_inc(wlo_done, RAW)
            dve.sem_inc(unit_used, RING)
            dve.sem_inc(taken, RING)
            dve.sem_inc(actlo_done, 2)
            nc.vector.memset(ones[:, :], 1.0).then_inc(set_up, 1)
            nc.vector.memset(eps[:, :], EPS).then_inc(set_up, 1)
            dve.wait_ge(gains_in, 16)
            dve.wait_ge(x_in[0], 16)
            scale_x(0, 0, 0)
            for m in range(KD):
                if m + 1 < KD:
                    dve.wait_ge(x_in[(m + 1) * XPARTS // KD], 16)
                    if m >= 1:
                        dve.wait_ge(xs_ready, m)
                    scale_x(0, m + 1, (m + 1) % 2)
                rest_x(0, m, m % 2)
                if m in START_UNITS:
                    rest_unit(0, 0, 0, 0, START_UNITS.index(m), UT)
            with dve.Fori(0, DEPTH) as L:
                ffn_vec(L, 0)
                mixer_vec(L)
                ffn_vec(L, 1)
            dve.wait_ge(xs_ready, (3 * DEPTH + 1) * KD)
            dve.wait_ge(ssq_done, (3 * DEPTH + 1) * (KD + 1))
            invert(3 * DEPTH)
            for m in range(KD):
                nc.vector.scalar_tensor_tensor(x[:, m, :], x[:, m, :], gain(3 * DEPTH, m), rinv[:, :],
                                               ALU.mult, ALU.mult).then_inc(y_done, 1)

        @block.gpsimd
        def _(pool):
            def chunk(t, m):
                return t[:, m, :] if isinstance(m, int) else t[:, at(m), :].rearrange("p o n -> p (o n)")

            def clear_squares(norm, first=False):
                if not first:
                    pool.wait_ge(rinv_ready, norm)
                    plain(pool)
                nc.gpsimd.memset(ssq[:, :], 0.0).then_inc(ssq_done, 1)

            def add_squares(norm, m):
                pool.wait_ge(ssq_done, norm * (KD + 1) + m + 1)
                nc.gpsimd.tensor_tensor(sq[:, :], chunk(x, m), chunk(x, m), ALU.mult).then_inc(sq_done, 1)
                pool.wait_ge(sq_done, norm * KD + m + 1)
                nc.gpsimd.tensor_tensor(ssq[:, :], ssq[:, :], sq[:, :], ALU.add).then_inc(ssq_done, 1)

            def ffn_pool(L, f):
                with pool.Fori(0, KF // 2) as i:
                    for q in range(2):
                        pool.wait_ge(silu_done, L * 2 * KF + i * 2 + f * KF + q + 1)
                        pool.wait_ge(taken, L * NR + i * 4 + R_GU[f] + 2 * q + 2 + RING)
                        nc.gpsimd.tensor_tensor(up_s[:, q, :], gate_s[:, q, :], up_s[:, q, :], ALU.mult)\
                            .then_inc(prod_done, 1)
                        pool.wait_ge(acthi_done, L * 2 * KF + i * 2 + f * KF + q + 1)
                        j = i * 2 + q
                        nc.gpsimd.tensor_tensor(chunk(act_lo, j), up_s[:, q, :], chunk(act_hi, j).bitcast(F32),
                                                ALU.subtract).then_inc(actlo_done, 1)
                norm = L * 3 + 1 + 2 * f
                clear_squares(norm)
                with pool.Fori(0, KD // 2) as i:
                    for o in range(2):
                        pool.wait_ge(taken, L * NR + i * 2 + R_DN[f] + o + RING + 1)
                        add_squares(norm, i * 2 + o)

            def mixer_pool(L):
                pool.wait_ge(unit_used, L * NU + RING + U_IN)
                plain(pool)
                nc.gpsimd.memset(qm[:, :, :, :], 0.0).then_inc(qm_zero, 1)
                pool.wait_ge(tabs_ready, L * 2 + 2)
                for kind, n in STEPS:
                    if kind == "K" and n == 2 * CT:
                        pool.wait_ge(kvc_used, L * N_KV + 1 + 2 * CT)
                        plain(pool)
                        nc.gpsimd.memset(qm_mem[:, :], 0.0).then_inc(pm_zero, 1)
                    if kind != "U":
                        continue
                    what, g, c = COLS[n]
                    pool.wait_ge(zs_done, L * N_IN + n + 1)
                    if n >= 2:
                        before = COLS[n - 2][0]
                        if n - 2 in QK_UNITS:
                            pool.wait_ge(rope_done, L * 17 + QK_UNITS.index(n - 2) + 1)
                        elif before == "v":
                            pool.wait_ge(kvt_done, L * 14 + KV_UNITS.index(n - 2) + 1)
                        else:
                            pool.wait_ge(gtanh_done, L * 16 + G_UNITS.index(n - 2) + 1)
                    by = cosr if what in "qk" else rinv
                    nc.gpsimd.tensor_tensor(t1[:, n % 2, :], zs[:, n % 2, :], by[:, :], ALU.mult).then_inc(t1_done, 1)
                norm = L * 3 + 2
                for m in range(KD):
                    pool.wait_ge(taken, L * NR + R_BR + m + RING + 1)
                    nc.gpsimd.tensor_tensor(ma[:, m % 2, :], ma[:, m % 2, :], mb[:, m % 2, :], ALU.add)\
                        .then_inc(mab_done, 1)
                    pool.wait_ge(mhi_done, L * KD + m + 1)
                    nc.gpsimd.tensor_tensor(mlo[:, m, :], ma[:, m % 2, :], mhi[:, m, :].bitcast(F32), ALU.subtract)\
                        .then_inc(mlo_done, 1)
                clear_squares(norm)
                for m in range(KD):
                    pool.wait_ge(taken, L * NR + R_WO + m + RING + 1)
                    add_squares(norm, m)

            clear_squares(0, True)
            for m in range(KD):
                pool.wait_ge(x_in[m * XPARTS // KD], 16)
                add_squares(0, m)
            with pool.Fori(0, DEPTH) as L:
                ffn_pool(L, 0)
                mixer_pool(L)
                ffn_pool(L, 1)


def tiles_of(w, order=None):
    l, k, n = w.shape
    w = w.reshape(l, k // P, P, n // P, P).transpose(0, 3, 2, 1, 4).reshape(l, n // P, P, k)
    return np.ascontiguousarray(w if order is None else w[:, order]).reshape(-1, P, k)


def gqa_columns(w, axis):
    shape = list(w.shape)
    split = shape[:axis] + [2, 4, HD] + shape[axis + 1:]
    return w.reshape(split).swapaxes(axis, axis + 1).reshape(shape)


def lay_out(inputs):
    i = {k: np.asarray(v) for k, v in inputs.items()}
    tok = np.concatenate([i["x_prompt"].reshape(SEQ, D), i["x_sample"].reshape(NB * NT, D)])
    a = {"x": np.ascontiguousarray(tok.reshape(TOK, KD, P).transpose(2, 1, 0)), "const": constants()}
    norms = np.stack([i[k][l] for l in range(DEPTH) for k in ("norm_ffn1", "norm_mix", "norm_ffn2")] + [i["norm_final"]])
    a["gains"] = np.ascontiguousarray(norms.reshape(-1, KD, P).transpose(2, 0, 1))
    s = i["sinks"]
    rows = np.tile(np.repeat(s.reshape(DEPTH, 2, 4), NT, axis=2), 4)
    a["sinks"] = np.ascontiguousarray(np.concatenate(
        [np.broadcast_to(s[None], (P, DEPTH, 8)), rows.transpose(2, 0, 1)], axis=2))
    for f in (1, 2):
        for k in ("gate", "up", "down"):
            a[f"ffn{f}_{k}"] = tiles_of(i[f"ffn{f}_{k}"])
            if f == 1 and k != "down":
                a[f"ffn{f}_{k}"] = np.concatenate([a[f"ffn{f}_{k}"], a[f"ffn{f}_{k}"][:2]])
    w = i["w_in"]
    ag = NG * 3 * 256
    bq = gqa_columns(w[:, :, ag:ag + 512], 2)
    parts = {("k", 3): w[:, :, ag + 512:ag + 640], ("v", 3): w[:, :, ag + 640:ag + 768], ("q", 3): bq,
             ("ga", 0): w[:, :, ag + 768:ag + 768 + D], ("gb", 0): w[:, :, ag + 768 + D:]}
    for g in range(NG):
        for n, k in enumerate("qkv"):
            c0 = (3 * g + n) * 256
            parts[(k, g)] = w[:, :, c0:c0 + 256]
    a["w_in"] = tiles_of(np.concatenate([parts[(k, g)][:, :, c * P:(c + 1) * P] for k, g, c in COLS], axis=2))
    a["w_branch"] = tiles_of(np.concatenate([i["w_branch_a"], gqa_columns(i["w_branch_b"], 1)], axis=1))
    a["w_out"] = tiles_of(i["w_out"])
    tiles = [i["cache_a1"]] + [i["cache_a2"][:, :, r::4] for r in range(4)] + [i["cache_a3"][:, :, r::16] for r in range(8)]
    kv = np.stack(tiles, axis=2).reshape(DEPTH, NB, CT, P, 2, 2, P)
    kv = kv.reshape(DEPTH, 2, 4, CT, P, 2, 2, P)
    a["kcache"] = np.ascontiguousarray(kv[..., 0, :, :].transpose(0, 1, 3, 6, 5, 2, 4)).reshape(-1, P, NB * P)
    a["vcache"] = np.ascontiguousarray(kv[..., 1, :, :].transpose(0, 1, 3, 4, 2, 5, 6)).reshape(-1, P, NB * P)
    b = i["cache_b"].reshape(DEPTH, NB, P, 2, P)
    a["kcache_b"] = np.ascontiguousarray(b[:, :, :, 0].transpose(0, 3, 1, 2)).reshape(DEPTH, P, NB * P)
    a["vcache_b"] = np.ascontiguousarray(b[:, :, :, 1].transpose(0, 2, 1, 3))
    for k in ("a1", "a2", "a3", "b"):
        a[f"cache_{k}"] = i[f"cache_{k}"]
    return a


_OUTS = {"y": (P, KD, TOK)}
for _n, _w, _h in (("a1", 128, 4), ("a2", 512, 4), ("a3", 2048, 4), ("b", 128, 2)):
    _OUTS[f"new_{_n}_prompt"] = (DEPTH, 1, min(_w, SEQ), 2, _h, HD)
    _OUTS[f"new_{_n}_sample"] = (DEPTH, NB, _w, 2, _h, HD)


def kernel(**inputs):
    import concourse.bacc as _bacc
    from concourse.bass_utils import run_bass_kernel_spmd as _run

    arrays = lay_out(inputs)
    nc = _bacc.Bacc("TRN2", target_bir_lowering=False, num_devices=1, dynamic_dma_scratch_size=1024)
    aps = {n: nc.dram_tensor(f"in_{n}", v.shape, mybir.dt.from_np(v.dtype), kind="ExternalInput").ap() for n, v in arrays.items()}
    for n, shape in _OUTS.items():
        aps[n] = nc.dram_tensor(f"out_{n}", shape, F32, kind="ExternalOutput").ap()
    build(nc, aps)
    got = _run(nc, [{f"in_{n}": v for n, v in arrays.items()}], core_ids=[0]).results[0]
    y = got["out_y"].transpose(2, 1, 0).reshape(TOK, D)
    return (np.ascontiguousarray(y[:SEQ]).reshape(1, SEQ, D), np.ascontiguousarray(y[SEQ:]).reshape(NB, NT, D),
            *(got[f"out_new_{n}_{k}"] for k in ("prompt", "sample") for n in ("a1", "a2", "a3", "b")))
```
